# Optimizing a Trainium2 kernel written in Bass

```python
import math
import jax
import jax.numpy as jnp
from jax import lax
import numpy as np
import jax, jax.numpy as jnp

D_MODEL = 1024
BATCH = 1
SEQ = 512
DEPTH = 2

HEAD_DIM = 64
N_HEADS = D_MODEL // HEAD_DIM
N_MIXERS = 4
GROUP_HEADS = N_HEADS // N_MIXERS
GROUP_WIDTH = GROUP_HEADS * HEAD_DIM
D_FF = 4 * D_MODEL
NORM_EPS = 1e-6
Q_BLOCK = 128
NEG_INF = -1e30
FORCE = 1e30
TINY = 1e-30
N_BUCKETS = 32
MAX_DISTANCE = 128
N_BIAS_HEADS = 3 * GROUP_HEADS
MOBA_BLOCK = 256
MOBA_TOPK = 3
MOBA_Q_CHUNK = 64
NSA_KV_DIM = HEAD_DIM
CMP_LEN = 32
CMP_STRIDE = 16
CMP_HIDDEN = 256
SLC_LEN = 64
SLC_TOPN = 4
WINDOW = 512
DIFF_HALF = HEAD_DIM // 2
SPLIT_SIZES = ((GROUP_WIDTH,) * 3
               + (GROUP_WIDTH,) * 3
               + (GROUP_WIDTH,)
               + (NSA_KV_DIM,) * 6
               + (3 * GROUP_HEADS,)
               + (GROUP_WIDTH,) * 3)
D_IN = sum(SPLIT_SIZES)


def _rmsnorm(x, g):
    xf = x.astype(jnp.float32)
    y = xf * lax.rsqrt(jnp.mean(xf * xf, axis=-1, keepdims=True) + NORM_EPS)
    return (y * g.astype(jnp.float32)).astype(x.dtype)

def _masked_softmax(logits, mask):
    s = jnp.where(mask, logits, NEG_INF)
    m = jnp.max(s, axis=-1, keepdims=True)
    e = jnp.where(mask, jnp.exp(s - m), 0.0)
    return e / jnp.maximum(jnp.sum(e, axis=-1, keepdims=True), TINY)

def _t5_bucket(dist):
    n = jnp.maximum(dist, 0)
    max_exact = N_BUCKETS // 2
    nf = jnp.maximum(n, 1).astype(jnp.float32)
    large = max_exact + (jnp.log(nf / max_exact) / math.log(MAX_DISTANCE / max_exact)
                         * (N_BUCKETS - max_exact)).astype(jnp.int32)
    large = jnp.minimum(large, N_BUCKETS - 1)
    return jnp.where(n < max_exact, n, large)

def _rel_bias(dist, table):
    return jnp.moveaxis(table[_t5_bucket(dist)], -1, 0).astype(jnp.float32)

def _rel_bias_per_head(dist, table):
    h = table.shape[1]
    h_idx = jnp.arange(h).reshape((1, h) + (1,) * (dist.ndim - 2))
    return table.T[h_idx, _t5_bucket(dist)].astype(jnp.float32)

def _heads(t, n_heads):
    b, s, _ = t.shape
    return t.reshape(b, s, n_heads, -1).transpose(0, 2, 1, 3)

def _merge_heads(t):
    b, h, s, d = t.shape
    return t.transpose(0, 2, 1, 3).reshape(b, s, h * d)

def _q_blocks(t, block):
    b, h, s = t.shape[:3]
    t = t.reshape((b, h, s // block, block) + t.shape[3:])
    return jnp.moveaxis(t, 2, 0)

def _unblock(t):
    t = jnp.moveaxis(t, 0, 2)
    b, h, n, blk = t.shape[:4]
    return t.reshape((b, h, n * blk) + t.shape[4:])

def stick_breaking_attention(q, k, v):
    b, h, s, d = q.shape
    scale = d ** -0.5
    kpos = jnp.arange(s)

    def one_block(args):
        qb, i = args
        qpos = i * Q_BLOCK + jnp.arange(Q_BLOCK)
        z = jnp.einsum('bhqd,bhkd->bhqk', qb, k).astype(jnp.float32) * scale
        mask = kpos[None, :] < qpos[:, None]
        log_keep = jnp.where(mask, -jax.nn.softplus(z), 0.0)
        suffix = lax.cumsum(log_keep, axis=3, reverse=True) - log_keep
        a = jnp.where(mask, jnp.exp(jax.nn.log_sigmoid(z) + suffix), 0.0)
        return jnp.einsum('bhqk,bhkd->bhqd', a.astype(v.dtype), v)

    out = lax.map(one_block, (_q_blocks(q, Q_BLOCK), jnp.arange(s // Q_BLOCK)))
    return _unblock(out)

def moba_attention(q, k, v, table):
    b, h, s, d = q.shape
    scale = d ** -0.5
    n_blk = -(-s // MOBA_BLOCK)
    pad = n_blk * MOBA_BLOCK - s
    k_blk = jnp.pad(k, ((0, 0), (0, 0), (0, pad), (0, 0))).reshape(b, h, n_blk, MOBA_BLOCK, d)
    v_blk = jnp.pad(v, ((0, 0), (0, 0), (0, pad), (0, 0))).reshape(b, h, n_blk, MOBA_BLOCK, d)
    k_mean = jnp.mean(k_blk.astype(jnp.float32), axis=3)
    n_sel = min(MOBA_TOPK, n_blk - 1)
    blk_ids = jnp.arange(n_blk)
    in_blk = jnp.arange(MOBA_BLOCK)
    b_idx = jnp.arange(b)[:, None, None, None]
    h_idx = jnp.arange(h)[None, :, None, None]

    def one_chunk(args):
        qc, i = args
        qpos = i * MOBA_Q_CHUNK + jnp.arange(MOBA_Q_CHUNK)
        own = (i * MOBA_Q_CHUNK) // MOBA_BLOCK
        k_own = lax.dynamic_index_in_dim(k_blk, own, axis=2, keepdims=False)
        v_own = lax.dynamic_index_in_dim(v_blk, own, axis=2, keepdims=False)
        dist_own = qpos[:, None] - (own * MOBA_BLOCK + in_blk)[None, :]
        s_own = (jnp.einsum('bhqd,bhkd->bhqk', qc, k_own).astype(jnp.float32) * scale
                 + _rel_bias(dist_own, table)[None])
        m_own = jnp.broadcast_to(dist_own >= 0, s_own.shape)
        if n_sel == 0:
            p = _masked_softmax(s_own, m_own)
            return jnp.einsum('bhqk,bhkd->bhqd', p.astype(v.dtype), v_own)
        gate = jnp.einsum('bhqd,bhnd->bhqn', qc.astype(jnp.float32), k_mean)
        gate = jnp.where(blk_ids < own, gate, NEG_INF)
        _, sel = lax.top_k(gate, n_sel)
        k_sel = k_blk[b_idx, h_idx, sel]
        v_sel = v_blk[b_idx, h_idx, sel]
        sel_pos = sel[..., None] * MOBA_BLOCK + in_blk
        dist_sel = qpos[:, None, None] - sel_pos
        s_sel = (jnp.einsum('bhqd,bhqnkd->bhqnk', qc, k_sel).astype(jnp.float32) * scale
                 + _rel_bias_per_head(dist_sel, table))
        m_sel = jnp.broadcast_to((sel < own)[..., None], s_sel.shape)
        n_flat = n_sel * MOBA_BLOCK
        s_all = jnp.concatenate([s_sel.reshape(b, h, MOBA_Q_CHUNK, n_flat), s_own], axis=-1)
        m_all = jnp.concatenate([m_sel.reshape(b, h, MOBA_Q_CHUNK, n_flat), m_own], axis=-1)
        p = _masked_softmax(s_all, m_all)
        p_sel = p[..., :n_flat].reshape(s_sel.shape)
        p_own = p[..., n_flat:]
        return (jnp.einsum('bhqnk,bhqnkd->bhqd', p_sel.astype(v.dtype), v_sel)
                + jnp.einsum('bhqk,bhkd->bhqd', p_own.astype(v.dtype), v_own))

    out = lax.map(one_chunk, (_q_blocks(q, MOBA_Q_CHUNK), jnp.arange(s // MOBA_Q_CHUNK)))
    return _unblock(out)

def nsa_attention(q, k_c, v_c, k_s, v_s, k_w, v_w, gates, pos_k, pos_v, wk1, wk2, wv1, wv2, table):
    b, h, s, d = q.shape
    scale = d ** -0.5
    tpos = jnp.arange(s)
    n_cmp = (s - CMP_LEN) // CMP_STRIDE + 1
    cmp_idx = np.arange(n_cmp)[:, None] * CMP_STRIDE + np.arange(CMP_LEN)[None, :]
    cmp_end = jnp.asarray(cmp_idx[:, -1])

    def compress(t, pos, w1, w2):
        blocks = t[:, cmp_idx] + pos
        return jax.nn.gelu(blocks.reshape(b, n_cmp, CMP_LEN * d) @ w1) @ w2

    kc = compress(k_c, pos_k, wk1, wk2)
    vc = compress(v_c, pos_v, wv1, wv2)
    dist_c = tpos[:, None] - cmp_end[None, :]
    s_c = (jnp.einsum('bhtd,bcd->bhtc', q, kc).astype(jnp.float32) * scale
           + _rel_bias(dist_c, table)[None])
    p_c = _masked_softmax(s_c, dist_c >= 0)
    o_cmp = jnp.einsum('bhtc,bcd->bhtd', p_c.astype(vc.dtype), vc)
    n_slc = s // SLC_LEN
    n_top = min(SLC_TOPN, n_slc)
    s_start = np.arange(n_slc) * SLC_LEN
    cover = np.clip(np.minimum(cmp_idx[:, -1][:, None], (s_start + SLC_LEN - 1)[None, :])
                    - np.maximum(cmp_idx[:, 0][:, None], s_start[None, :]) + 1, 0, None) / CMP_LEN
    importance = jnp.einsum('btc,cj->btj', jnp.sum(p_c, axis=1), jnp.asarray(cover, jnp.float32))
    own = tpos // SLC_LEN
    blk = jnp.arange(n_slc)
    imp = jnp.where(blk[None, :] == own[:, None], FORCE,
                    jnp.where(blk[None, :] < own[:, None], importance, NEG_INF))
    _, sel = lax.top_k(imp, n_top)
    n_qb = s // Q_BLOCK
    sel_b = sel.reshape(b, n_qb, Q_BLOCK, n_top).transpose(1, 0, 2, 3)
    ks_blk = k_s.reshape(b, n_slc, SLC_LEN, d)
    vs_blk = v_s.reshape(b, n_slc, SLC_LEN, d)
    kw_pad = jnp.pad(k_w, ((0, 0), (WINDOW, 0), (0, 0)))
    vw_pad = jnp.pad(v_w, ((0, 0), (WINDOW, 0), (0, 0)))
    b_idx = jnp.arange(b)[:, None, None]
    in_slc = jnp.arange(SLC_LEN)
    in_win = jnp.arange(WINDOW + Q_BLOCK)

    def one_block(args):
        qb, selc, i = args
        qpos = i * Q_BLOCK + jnp.arange(Q_BLOCK)
        k_sel = ks_blk[b_idx, selc]
        v_sel = vs_blk[b_idx, selc]
        dist_s = qpos[:, None, None] - (selc[..., None] * SLC_LEN + in_slc)
        s_s = (jnp.einsum('bhqd,bqnkd->bhqnk', qb, k_sel).astype(jnp.float32) * scale
               + jnp.moveaxis(table[_t5_bucket(dist_s)], -1, 1).astype(jnp.float32))
        m_s = jnp.broadcast_to((dist_s >= 0)[:, None], s_s.shape)
        flat = (b, h, Q_BLOCK, n_top * SLC_LEN)
        p_s = _masked_softmax(s_s.reshape(flat), m_s.reshape(flat)).reshape(s_s.shape)
        o_s = jnp.einsum('bhqnk,bqnkd->bhqd', p_s.astype(v_sel.dtype), v_sel)
        kw = lax.dynamic_slice_in_dim(kw_pad, i * Q_BLOCK, WINDOW + Q_BLOCK, axis=1)
        vw = lax.dynamic_slice_in_dim(vw_pad, i * Q_BLOCK, WINDOW + Q_BLOCK, axis=1)
        kpos = i * Q_BLOCK - WINDOW + in_win
        dist_w = qpos[:, None] - kpos[None, :]
        m_w = (dist_w >= 0) & (dist_w < WINDOW) & (kpos[None, :] >= 0)
        s_w = (jnp.einsum('bhqd,bkd->bhqk', qb, kw).astype(jnp.float32) * scale
               + _rel_bias(dist_w, table)[None])
        p_w = _masked_softmax(s_w, m_w)
        o_w = jnp.einsum('bhqk,bkd->bhqd', p_w.astype(vw.dtype), vw)
        return o_s, o_w

    o_slc, o_win = lax.map(one_block, (_q_blocks(q, Q_BLOCK), sel_b, jnp.arange(n_qb)))
    o_slc, o_win = _unblock(o_slc), _unblock(o_win)
    g = jax.nn.sigmoid(gates.astype(jnp.float32)).reshape(b, s, 3, h).transpose(2, 0, 3, 1)[..., None]
    g = g.astype(q.dtype)
    return g[0] * o_cmp + g[1] * o_slc + g[2] * o_win

def diff_attention(q, k, v, lam, table):
    s = q.shape[2]
    scale = q.shape[-1] ** -0.5
    kpos = jnp.arange(s)

    def one_block(args):
        qb, i = args
        qpos = i * Q_BLOCK + jnp.arange(Q_BLOCK)
        dist = qpos[:, None] - kpos[None, :]
        sc = (jnp.einsum('bhqcd,bhkcd->bhcqk', qb, k).astype(jnp.float32) * scale
              + _rel_bias(dist, table)[None, :, None])
        p = _masked_softmax(sc, dist >= 0)
        w = p[:, :, 0] - lam * p[:, :, 1]
        return jnp.einsum('bhqk,bhkd->bhqd', w.astype(v.dtype), v)

    out = lax.map(one_block, (_q_blocks(q, Q_BLOCK), jnp.arange(s // Q_BLOCK)))
    return _unblock(out)

def first_inputs(seed: int = 0) -> dict:
    key = jax.random.key(seed)
    ks = jax.random.split(key, 17)
    f32 = jnp.float32

    def nrm(k, shape, scale):
        return jax.random.normal(k, shape, f32) * scale

    return {
        "x": nrm(ks[0], (BATCH, SEQ, D_MODEL), 1.0),
        "w_in": nrm(ks[1], (DEPTH, D_MODEL, D_IN), D_MODEL ** -0.5),
        "w_out": nrm(ks[2], (DEPTH, D_MODEL, D_MODEL), D_MODEL ** -0.5),
        "w_up": nrm(ks[3], (DEPTH, D_MODEL, D_FF), D_MODEL ** -0.5),
        "w_down": nrm(ks[4], (DEPTH, D_FF, D_MODEL), D_FF ** -0.5),
        "norm_attn": 1.0 + nrm(ks[5], (DEPTH, D_MODEL), 0.05),
        "norm_mlp": 1.0 + nrm(ks[6], (DEPTH, D_MODEL), 0.05),
        "cmp_pos_k": nrm(ks[7], (DEPTH, CMP_LEN, HEAD_DIM), 0.1),
        "cmp_pos_v": nrm(ks[8], (DEPTH, CMP_LEN, HEAD_DIM), 0.1),
        "cmp_k_w1": nrm(ks[9], (DEPTH, CMP_LEN * HEAD_DIM, CMP_HIDDEN), (CMP_LEN * HEAD_DIM) ** -0.5),
        "cmp_k_w2": nrm(ks[10], (DEPTH, CMP_HIDDEN, HEAD_DIM), CMP_HIDDEN ** -0.5),
        "cmp_v_w1": nrm(ks[11], (DEPTH, CMP_LEN * HEAD_DIM, CMP_HIDDEN), (CMP_LEN * HEAD_DIM) ** -0.5),
        "cmp_v_w2": nrm(ks[12], (DEPTH, CMP_HIDDEN, HEAD_DIM), CMP_HIDDEN ** -0.5),
        "diff_lambda": nrm(ks[13], (DEPTH, 4, DIFF_HALF), 0.1),
        "diff_subln": 1.0 + nrm(ks[14], (DEPTH, HEAD_DIM), 0.05),
        "rel_bias": nrm(ks[15], (N_BUCKETS, N_BIAS_HEADS), 0.2),
        "final_norm": 1.0 + nrm(ks[16], (D_MODEL,), 0.05),
    }

def first_block(x, w_in, w_out, w_up, w_down, norm_attn, norm_mlp, cmp_pos_k, cmp_pos_v,
              cmp_k_w1, cmp_k_w2, cmp_v_w1, cmp_v_w2, diff_lambda, diff_subln, rel_bias, final_norm):
    bias_moba = rel_bias[:, :GROUP_HEADS]
    bias_nsa = rel_bias[:, GROUP_HEADS:2 * GROUP_HEADS]
    bias_diff = rel_bias[:, 2 * GROUP_HEADS:]
    split_at = np.cumsum(SPLIT_SIZES)[:-1].tolist()
    b, s, _ = x.shape
    for layer in range(DEPTH):
        h = _rmsnorm(x, norm_attn[layer])
        proj = h @ w_in[layer]
        (sb_q, sb_k, sb_v, mb_q, mb_k, mb_v, ns_q, ns_kc, ns_vc, ns_ks, ns_vs, ns_kw, ns_vw,
         ns_g, df_q, df_k, df_v) = jnp.split(proj, split_at, axis=-1)
        o_sb = stick_breaking_attention(_heads(sb_q, GROUP_HEADS), _heads(sb_k, GROUP_HEADS),
                                        _heads(sb_v, GROUP_HEADS))
        o_mb = moba_attention(_heads(mb_q, GROUP_HEADS), _heads(mb_k, GROUP_HEADS),
                              _heads(mb_v, GROUP_HEADS), bias_moba)
        o_ns = nsa_attention(_heads(ns_q, GROUP_HEADS), ns_kc, ns_vc, ns_ks, ns_vs, ns_kw, ns_vw, ns_g,
                             cmp_pos_k[layer], cmp_pos_v[layer], cmp_k_w1[layer], cmp_k_w2[layer],
                             cmp_v_w1[layer], cmp_v_w2[layer], bias_nsa)
        lambda_init = 0.8 - 0.6 * math.exp(-0.3 * layer)
        lv = diff_lambda[layer].astype(jnp.float32)
        lam = jnp.exp(jnp.sum(lv[0] * lv[1])) - jnp.exp(jnp.sum(lv[2] * lv[3])) + lambda_init
        dq = df_q.reshape(b, s, GROUP_HEADS, 2, DIFF_HALF).transpose(0, 2, 1, 3, 4)
        dk = df_k.reshape(b, s, GROUP_HEADS, 2, DIFF_HALF).transpose(0, 2, 1, 3, 4)
        o_df = diff_attention(dq, dk, _heads(df_v, GROUP_HEADS), lam, bias_diff)
        o_df = _rmsnorm(o_df, diff_subln[layer]) * (1.0 - lambda_init)
        mixed = jnp.concatenate([_merge_heads(o_sb), _merge_heads(o_mb),
                                 _merge_heads(o_ns), _merge_heads(o_df)], axis=-1)
        x = x + mixed @ w_out[layer]
        h2 = _rmsnorm(x, norm_mlp[layer])
        x = x + jnp.square(jax.nn.relu(h2 @ w_up[layer])) @ w_down[layer]
    return _rmsnorm(x, final_norm)


D_FF_2 = 2816
D_POOL = 256
POOL_WINDOWS = (2, 4, 8, 16)
POOL_GROUP = D_POOL // len(POOL_WINDOWS)
D_CONV = 256
CONV_WIDTH = 3
NA_HEADS = 8
NA_HEAD_DIM = 64
D_NA = NA_HEADS * NA_HEAD_DIM
D_MIX = D_POOL + D_CONV + D_NA
GRID_W = 64
NA_ROWS = 8
NA_COLS = 16
D_IN_2 = D_POOL + 3 * D_CONV + 3 * D_NA
ALPHA = (2.0 * DEPTH) ** 0.25
BETA = (8.0 * DEPTH) ** -0.25
LN_EPS = 1e-5
NEG_INF_2 = -1e30


def layer_norm(x, g, b):
    xf = x.astype(jnp.float32)
    mu = jnp.mean(xf, axis=-1, keepdims=True)
    var = jnp.mean(jnp.square(xf - mu), axis=-1, keepdims=True)
    y = (xf - mu) * lax.rsqrt(var + LN_EPS)
    return (y * g.astype(jnp.float32) + b.astype(jnp.float32)).astype(x.dtype)

def swiglu(x, w_gate, w_up, w_down):
    return (jax.nn.silu(x @ w_gate) * (x @ w_up)) @ w_down

def pool_mixer(u, pool_w, pool_scale):
    bsz, s, _ = u.shape
    ng = len(POOL_WINDOWS)
    uf = u.astype(jnp.float32).reshape(bsz, s, ng, POOL_GROUP)
    cs = jnp.concatenate([jnp.zeros((bsz, 1, ng, POOL_GROUP), jnp.float32),
                          jnp.cumsum(uf, axis=1)], axis=1)
    t = jnp.arange(s)
    outs = []
    for g, w in enumerate(POOL_WINDOWS):
        lo = jnp.clip(t - w // 2, 0, s)
        hi = jnp.clip(t - w // 2 + w, 0, s)
        cnt = (hi - lo).astype(jnp.float32)[None, :, None]
        mean = (cs[:, hi, g] - cs[:, lo, g]) / cnt
        outs.append(mean - uf[:, :, g])
    p = jnp.stack(outs, axis=2).astype(u.dtype)
    y = jnp.einsum('bsgc,gcd->bsgd', p, pool_w) * pool_scale.reshape(ng, POOL_GROUP)
    return y.reshape(bsz, s, D_POOL)

def gated_conv_mixer(gate_b, gate_c, h, conv_w):
    z = gate_c * h
    zp = jnp.pad(z, ((0, 0), (1, 1), (0, 0)))
    y = conv_w[0] * zp[:, :-2] + conv_w[1] * zp[:, 1:-1] + conv_w[2] * zp[:, 2:]
    return gate_b * y

def neighbourhood_attention(q, k, v, rpb):
    bsz, s, _ = q.shape
    rows = s // GRID_W
    kr = min(NA_ROWS, rows)
    shp = (bsz, rows, GRID_W, NA_HEADS, NA_HEAD_DIM)
    q, k, v = q.reshape(shp), k.reshape(shp), v.reshape(shp)
    r = jnp.arange(rows)
    row_start = jnp.clip(r - kr // 2, 0, rows - kr)
    row_idx = row_start[:, None] + jnp.arange(kr)[None, :]
    kb = k[:, row_idx]
    vb = v[:, row_idx]
    c = jnp.arange(GRID_W)
    col_start = jnp.clip(c - NA_COLS // 2, 0, GRID_W - NA_COLS)
    col_valid = (c[None, :] >= col_start[:, None]) & (c[None, :] < col_start[:, None] + NA_COLS)
    dr = row_idx - r[:, None] + (NA_ROWS - 1)
    dc = jnp.clip(c[None, :] - c[:, None], -(NA_COLS - 1), NA_COLS - 1) + (NA_COLS - 1)
    bias = rpb[:, dr[:, None, :, None], dc[None, :, None, :]]
    scores = jnp.einsum('brqhd,brikhd->bhrqik', q, kb).astype(jnp.float32) * (NA_HEAD_DIM ** -0.5)
    scores = scores + bias.astype(jnp.float32)
    scores = jnp.where(col_valid[:, None, :], scores, NEG_INF_2)
    p = jax.nn.softmax(scores, axis=(-2, -1)).astype(v.dtype)
    o = jnp.einsum('bhrqik,brikhd->brqhd', p, vb)
    return o.reshape(bsz, s, D_NA)

def second_inputs(seed: int = 0) -> dict:
    key = jax.random.key(seed)
    ks = jax.random.split(key, 16)
    L, D, F = DEPTH, D_MODEL, D_FF_2
    nrm = lambda k, shp: jax.random.normal(k, shp, jnp.float32)
    x = nrm(ks[0], (BATCH, SEQ, D))
    ffn1_w_gate = nrm(ks[1], (L, D, F)) * D ** -0.5
    ffn1_w_up = nrm(ks[2], (L, D, F)) * D ** -0.5
    ffn1_w_down = nrm(ks[3], (L, F, D)) * (BETA * F ** -0.5)
    ffn2_w_gate = nrm(ks[4], (L, D, F)) * D ** -0.5
    ffn2_w_up = nrm(ks[5], (L, D, F)) * D ** -0.5
    ffn2_w_down = nrm(ks[6], (L, F, D)) * (BETA * F ** -0.5)
    col_scale = jnp.concatenate([
        jnp.ones((D_POOL + 2 * D_CONV,), jnp.float32),
        jnp.full((D_CONV,), BETA, jnp.float32),
        jnp.ones((2 * D_NA,), jnp.float32),
        jnp.full((D_NA,), BETA, jnp.float32)])
    w_in = nrm(ks[7], (L, D, D_IN_2)) * D ** -0.5 * col_scale
    pool_w = nrm(ks[8], (L, len(POOL_WINDOWS), POOL_GROUP, POOL_GROUP)) * POOL_GROUP ** -0.5
    pool_scale = 1.0 + 0.1 * nrm(ks[9], (L, D_POOL))
    conv_w = nrm(ks[10], (L, CONV_WIDTH, D_CONV)) * CONV_WIDTH ** -0.5
    rpb = 0.02 * nrm(ks[11], (L, NA_HEADS, 2 * NA_ROWS - 1, 2 * NA_COLS - 1))
    w_out = nrm(ks[12], (L, D_MIX, D)) * (BETA * D_MIX ** -0.5)
    ln_g = 1.0 + 0.05 * nrm(ks[13], (L, 3, D))
    ln_b = 0.02 * nrm(ks[14], (L, 3, D))
    return {"x": x,
            "ffn1_w_gate": ffn1_w_gate, "ffn1_w_up": ffn1_w_up, "ffn1_w_down": ffn1_w_down,
            "ffn2_w_gate": ffn2_w_gate, "ffn2_w_up": ffn2_w_up, "ffn2_w_down": ffn2_w_down,
            "w_in": w_in, "pool_w": pool_w, "pool_scale": pool_scale, "conv_w": conv_w,
            "rpb": rpb, "w_out": w_out, "ln_g": ln_g, "ln_b": ln_b}

def second_block(x, ffn1_w_gate, ffn1_w_up, ffn1_w_down, ffn2_w_gate, ffn2_w_up, ffn2_w_down,
              w_in, pool_w, pool_scale, conv_w, rpb, w_out, ln_g, ln_b):
    splits = np.cumsum([D_POOL, D_CONV, D_CONV, D_CONV, D_NA, D_NA])
    for l in range(DEPTH):
        x = layer_norm(ALPHA * x + 0.5 * swiglu(x, ffn1_w_gate[l], ffn1_w_up[l], ffn1_w_down[l]),
                       ln_g[l, 0], ln_b[l, 0])
        proj = x @ w_in[l]
        u, gb, gc, h, q, k, v = jnp.split(proj, splits, axis=-1)
        y_a = pool_mixer(u, pool_w[l], pool_scale[l])
        y_b = gated_conv_mixer(gb, gc, h, conv_w[l])
        y_c = neighbourhood_attention(q, k, v, rpb[l])
        y = jnp.concatenate([y_a, y_b, y_c], axis=-1) @ w_out[l]
        x = layer_norm(ALPHA * x + y, ln_g[l, 1], ln_b[l, 1])
        x = layer_norm(ALPHA * x + 0.5 * swiglu(x, ffn2_w_gate[l], ffn2_w_up[l], ffn2_w_down[l]),
                       ln_g[l, 2], ln_b[l, 2])
    return x


def setup_inputs(seed=0):
    out = dict(first_inputs(seed))
    for name, value in second_inputs(seed + 1).items():
        if name != "x":
            out[name + "_2"] = value
    return out


def reference(
    x, w_in, w_out, w_up, w_down, norm_attn, norm_mlp, cmp_pos_k, cmp_pos_v, cmp_k_w1, cmp_k_w2,
    cmp_v_w1, cmp_v_w2, diff_lambda, diff_subln, rel_bias, final_norm, ffn1_w_gate_2,
    ffn1_w_up_2, ffn1_w_down_2, ffn2_w_gate_2, ffn2_w_up_2, ffn2_w_down_2, w_in_2, pool_w_2,
    pool_scale_2, conv_w_2, rpb_2, w_out_2, ln_g_2, ln_b_2,
):
    x = first_block(
        x, w_in, w_out, w_up, w_down, norm_attn, norm_mlp, cmp_pos_k, cmp_pos_v, cmp_k_w1,
        cmp_k_w2, cmp_v_w1, cmp_v_w2, diff_lambda, diff_subln, rel_bias, final_norm,
    )
    return second_block(
        x, ffn1_w_gate_2, ffn1_w_up_2, ffn1_w_down_2, ffn2_w_gate_2, ffn2_w_up_2, ffn2_w_down_2,
        w_in_2, pool_w_2, pool_scale_2, conv_w_2, rpb_2, w_out_2, ln_g_2, ln_b_2,
    )


_drawn_inputs = setup_inputs


def setup_inputs(seed=0):
    import zlib

    import numpy as np

    out = dict(_drawn_inputs(seed))
    spreads = {}
    factors = {'cmp_pos_k': 23.094,
     'cmp_pos_v': 3.044,
     'diff_lambda': 15.2,
     'pool_scale_2': 3.249,
     'rpb_2': 64.0}
    for name, (base, spread) in spreads.items():
        noise = np.random.default_rng([zlib.crc32(name.encode()), seed]).standard_normal(out[name].shape)
        drawn = base * np.exp(spread * noise) if base else spread * noise
        out[name] = jnp.asarray(drawn.astype(out[name].dtype))
    for name, factor in factors.items():
        out[name] = (out[name] * factor).astype(out[name].dtype)
    return out
```

```python
import math
from contextlib import ExitStack

import numpy as np

import concourse.bass as bass
from concourse import mybir

ALU = mybir.AluOpType
ACT = mybir.ActivationFunctionType
AX = mybir.AxisListType
F32 = mybir.dt.float32

P = 128
DEPTH = 2
SEQ = 512
D_MODEL = 1024
NT = SEQ // P
NC = D_MODEL // P
HEAD = 64
HEADS = 4
GROUP = HEADS * HEAD
PAIRS = HEADS // 2
D_FF = 4 * D_MODEL
D_FF2 = 2816
NORM_EPS = 1e-6
LN_EPS = 1e-5
TINY = 1e-30
NEG = -1e30
N_BUCKETS, MAX_DISTANCE = 32, 128
CMP_LEN, CMP_STRIDE, CMP_HIDDEN = 32, 16, 256
N_CMP = (SEQ - CMP_LEN) // CMP_STRIDE + 1
CMP_PAD = 32
SLC_LEN, SLC_TOPN = 64, 4
N_SLC = SEQ // SLC_LEN
DIFF_HALF = HEAD // 2
ALPHA = (2.0 * DEPTH) ** 0.25
POOL_WINDOWS = (2, 4, 8, 16)
GRID_W = 64
GRID_H = SEQ // GRID_W
NA_HEADS, NA_PAIRS = 8, 4
NA_COLS = 16
RPB_W = 2 * NA_COLS - 1
RPB_H = 2 * GRID_H - 1
RPB_PAD = 64
RPB_SIZE = NA_HEADS * RPB_H * RPB_W + 2 * RPB_PAD
NA_J = 14
HALF1 = D_FF // P // 2
HALVES2 = (12, 10)
assert sum(HALVES2) * P == D_FF2

SLOTS = 4
PIECE = NC * P

R_ATT, R_CMP, R_OUT = 2, 2, NC // SLOTS
R_UP, R_DOWN = HALF1 // SLOTS, NC * 2 // SLOTS
ROUND_SB, ROUND_MB, ROUND_DF, ROUND_CMP = 0, R_ATT, 2 * R_ATT, 3 * R_ATT
ROUND_OUT = ROUND_CMP + R_CMP
ROUND_MLP = ROUND_OUT + R_OUT
ROUNDS1 = ROUND_MLP + 2 * (R_UP + R_DOWN)
R_GU = [2 * n // SLOTS for n in HALVES2]
ROUNDS_FFN = sum(R_GU) + 2 * R_DOWN
ROUND_PROJ = ROUNDS_FFN
ROUND_NA = ROUND_PROJ + 1
ROUND_OUT2 = ROUND_NA + NA_PAIRS
ROUND_FFN2 = ROUND_OUT2 + R_OUT
ROUNDS2 = ROUND_FFN2 + ROUNDS_FFN
ROUND_B2 = DEPTH * ROUNDS1

GP_SETUP = NC // 2
GP_OUT = 3 * R_ATT * 2
GP_MLP = GP_OUT + NC // 2
GP_HALF1 = (HALF1 + NC) // 2
GPS1 = GP_MLP + 2 * GP_HALF1
GP_HALF2 = [n + NC // 2 for n in HALVES2]
GP_FFN = sum(GP_HALF2)
GP_PROJ = GP_FFN
GP_NA = GP_PROJ + 2
GP_OUT2 = GP_NA + 2 * NA_PAIRS
GP_FFN2 = GP_OUT2 + NC // 2
GPS2 = GP_FFN2 + GP_FFN
GP_B2 = GP_SETUP + DEPTH * GPS1

(ST_NORM, ST_SB, ST_MB, ST_DF, ST_NSA, ST_NSP, ST_OUT, ST_NORM2, ST_MLP) = (0, 1, 3, 5, 7, 8, 10, 11, 12)
STAGES1 = 16
ST_FINAL = 1 + DEPTH * STAGES1
ST_B2 = ST_FINAL + 1
(ST_FFN1, ST_LN0, ST_PROJ, ST_NA, ST_POOL, ST_OUT2, ST_LN1, ST_FFN2, ST_LN2) = (0, 4, 5, 6, 10, 11, 12, 13, 17)
STAGES2 = 18
ST_END = ST_B2 + DEPTH * STAGES2

U = 2 * NT
MAPS_MB, MAPS_DF, MAPS_NS = 0, 2 * U, 6 * U
MAPS1 = 10 * U
RECIP_MB, RECIP_DF, RECIP_NS = 0, 2 * U, 4 * U
RECIPS1 = 8 * U
NORM_MB, NORM_NS = 0, 2 * U
NORMS1 = 6 * U
TR_SB, TR_MB, TR_DF, TR_NS = 0, 2 * U, 4 * U, 6 * U
TRS1 = 10 * U



def columns(**widths):
    at, out = 0, {}
    for name, w in widths.items():
        out[name] = (at, at + w)
        at += w
    return out, at


CONST, CONST_W = columns(ident=P, ones=P, head_ones=P, strict=SEQ, cover=N_SLC, past=NT * N_SLC,
                         force=NT * N_SLC, earlier=N_SLC * N_SLC, inv_count=2 * SEQ, col_mask=GRID_W,
                         bucket=SEQ + P, neg_rows=12)
PAR1, PAR1_W = columns(norm_attn=NC, norm_mlp=NC, final_norm=NC, pos=CMP_LEN, subln=1, lam_init=2,
                       lam=4 * DIFF_HALF, w2k=2 * HEAD, w2v=2 * HEAD)
PAR2, PAR2_W = columns(ln_g=3 * NC, ln_b=3 * NC, pool_scale=2, conv=6, pool_w=2 * HEAD)


def emit(nc, x_in, weights, const_in, par1_in, par2_in, table_in, rpb_in, out):
    with ExitStack() as ctx:
        def sb(name, shape):
            return ctx.enter_context(nc.sbuf_tensor(name, shape, F32))

        def sem(name):
            return ctx.enter_context(nc.semaphore(name))

        bias_scratch = nc.dram_tensor("bias_scratch", (12, P, SEQ + P), F32, kind="Internal").ap()


        xT = sb("xT", [P, NC, SEQ])
        hT = sb("hT", [P, NC, SEQ])
        mixT = sb("mixT", [P, NC, SEQ])
        wring = sb("wring", [P, SLOTS, PIECE])
        const = sb("const", [P, CONST_W])
        par1 = sb("par1", [P, PAR1_W])
        par2 = sb("par2", [P, PAR2_W])
        tables = sb("tables", [P, max(12 * SEQ, NA_HEADS * NA_J * GRID_W)])
        big = sb("big", [P, 32 * SEQ])
        rows = sb("rows", [P, 2, SEQ])
        small = sb("small", [P, 1024])

        def c(name):
            return const[:, CONST[name][0]:CONST[name][1]]

        def p1(name):
            return par1[:, PAR1[name][0]:PAR1[name][1]]

        def p2(name):
            return par2[:, PAR2[name][0]:PAR2[name][1]]

        ident, ones = c("ident"), c("ones")
        t5 = tables[:, 0:12 * SEQ].rearrange("p (h k) -> p h k", h=12)
        rpb_raw = tables[:, 0:NA_HEADS * NA_J * GRID_W].rearrange("p (h k) -> p h k", h=NA_HEADS)

        hidden = big[:, :].rearrange("p (f s) -> p f s", s=SEQ)
        place = [0]

        def cut(n):
            place[0] += n
            assert place[0] <= 32 * SEQ
            return big[:, place[0] - n:place[0]]

        qT, kT, vT = cut(SEQ), cut(SEQ), cut(SEQ)
        v_nat = cut(SEQ).rearrange("p (t d) -> p t d", t=NT)
        side = cut(8 * SEQ).rearrange("p (i s) -> p i s", i=8)
        score = cut(2 * SEQ).rearrange("p (b s) -> p b s", b=2)
        prob = cut(4 * SEQ).rearrange("p (b s) -> p b s", b=4)
        probT = cut(2 * SEQ).rearrange("p (b s) -> p b s", b=2)
        pair_bias = cut(2 * NA_J * GRID_W).rearrange("p (h k) -> p h k", h=2)
        sel_bias = cut(2 * SEQ).rearrange("p (b s) -> p b s", b=2)
        vs_nat = cut(SEQ).rearrange("p (t d) -> p t d", t=NT)
        vw_nat = cut(SEQ).rearrange("p (t d) -> p t d", t=NT)
        blocks = cut(CMP_LEN * CMP_PAD).rearrange("p (l n) -> p l n", l=CMP_LEN)
        pcT = cut(SEQ)
        assert place[0] <= 32 * SEQ
        squares = hidden[:, 16:16 + NC, :]
        evac = hidden[:, 30:32, :]

        place2 = [0]

        def bit(n):
            place2[0] += n
            assert place2[0] <= 1024
            return small[:, place2[0] - n:place2[0]]

        negmax, denom, recip = bit(4), bit(4), bit(4)
        lam2, lam_one, lam_scale, lam_eps, lam_tmp, subln = bit(2), bit(1), bit(1), bit(1), bit(2), bit(1)
        gates = bit(NT * 12).rearrange("p (t g) -> p t g", t=NT)
        kcT = bit(CMP_PAD)
        imp = bit(NT * N_SLC).rearrange("p (t j) -> p t j", t=NT)
        rank = bit(NT * N_SLC).rearrange("p (t j) -> p t j", t=NT)
        sel_neg = bit(NT * N_SLC).rearrange("p (t j) -> p t j", t=NT)
        cmax, csum = bit(NT * HEADS), bit(NT * HEADS)
        eps_norm, eps_ln, one_col = bit(1), bit(1), bit(1)
        lam_prod = bit(2 * DIFF_HALF)
        gx = bit(4 * CMP_PAD).rearrange("p (g n) -> p g n", g=4)
        gt = bit(4 * CMP_PAD).rearrange("p (g n) -> p g n", g=4)
        h1v = sb("h1v", [P, 2, HEADS, CMP_PAD])
        vc_diag = sb("vc_diag", [P, GROUP])
        vc_pair = sb("vc_pair", [P, P])
        cmp_bias = sb("cmp_bias", [P, NT, HEADS, CMP_PAD])
        cmp_mask = sb("cmp_mask", [P, NT, HEADS, CMP_PAD])
        pc = sb("pc", [P, NT, HEADS, CMP_PAD])
        pcg = sb("pcg", [P, NT, HEADS, CMP_PAD])
        beats = sb("beats", [P, 2, NT * N_SLC * N_SLC])
        tab33 = sb("tab33", [N_BUCKETS + 1, 12])

        def bank(name):
            return ctx.enter_context(nc.psum_tensor(name, [P, SEQ], F32))

        acc = [bank("acc0"), bank("acc1")]
        scp = [bank("score0"), bank("score1")]
        trp = [bank("trans0"), bank("trans1")]
        outp, spare = bank("outp"), bank("spare")

        w_loaded = [sem(f"w_loaded{s}") for s in range(SLOTS)]
        pieces_done = sem("pieces_done")
        evacuated = [sem("evacuated0"), sem("evacuated1")]
        const_loaded, x_loaded, table_loaded = sem("const_loaded"), sem("x_loaded"), sem("table_loaded")
        par_loaded, rpb_loaded = sem("par_loaded"), sem("rpb_loaded")
        bias_stored, t5_loaded, stored = sem("bias_stored"), sem("t5_loaded"), sem("stored")
        pe_end, act_end, dve_end, pool_end = sem("pe_end"), sem("act_end"), sem("dve_end"), sem("pool_end")
        x_turned, vec_ready, vec_copied, tab_set, zeroed = (sem("x_turned"), sem("vec_ready"), sem("vec_copied"),
                                                            sem("tab_set"), sem("zeroed"))
        squared, summed, rstd_ready = sem("squared"), sem("summed"), sem("rstd_ready")
        ln_summed, centred, ln_squared, ln_var, ln_rstd, ln_scaled = (
            sem("ln_summed"), sem("centred"), sem("ln_squared"), sem("ln_var"), sem("ln_rstd"), sem("ln_scaled"))
        lam_dots, lam_exps = sem("lam_dots"), sem("lam_exps")
        kv_ready = sem("kv_ready")
        v_turned, v_copied = sem("v_turned"), sem("v_copied")
        pair_ready = sem("pair_ready")
        scores_ready, biased, exped, recip_ready, normed = (sem("scores_ready"), sem("biased"), sem("exped"),
                                                            sem("recip_ready"), sem("normed"))
        sel_ready = sem("sel_ready")
        transposed, pt_ready, pv_done = sem("transposed"), sem("pt_ready"), sem("pv_done")
        sb_scores, sb_z, sb_log, sb_arg, sb_prob = (sem("sb_scores"), sem("sb_z"), sem("sb_log"), sem("sb_arg"),
                                                    sem("sb_prob"))
        df_second, df_weight, df_sq, df_sum, df_rstd = (sem("df_second"), sem("df_weight"), sem("df_sq"),
                                                        sem("df_sum"), sem("df_rstd"))
        ns_turned, ns_copied, blocks_ready, hid_copied, hid_sq, hid_poly, hid_exp, gelu_ready = (
            sem("ns_turned"), sem("ns_copied"), sem("blocks_ready"), sem("hid_copied"), sem("hid_sq"),
            sem("hid_poly"), sem("hid_exp"), sem("gelu_ready"))
        cmp_kv, cmp_copied, cmp_scores, cmp_shift, cmp_exp, pc_ready, pc_turned, pc_copied, imp_ready = (
            sem("cmp_kv"), sem("cmp_copied"), sem("cmp_scores"), sem("cmp_shift"), sem("cmp_exp"),
            sem("pc_ready"), sem("pc_turned"), sem("pc_copied"), sem("imp_ready"))
        gate_exp = sem("gate_exp")
        silu_ready = sem("silu_ready")
        pooled, pool_mm, pool_done = sem("pooled"), sem("pool_mm"), sem("pool_done")
        out_turned, out_copied = sem("out_turned"), sem("out_copied")

        def big_pad(n, wide):
            return prob[:, :, :].rearrange("p b s -> p (b s)")[:, n * wide:(n + 1) * wide]

        block = ctx.enter_context(nc.Block())

        def settle(eng, *waits):
            waits = [(s, eng.compute_val(value)) for s, value in waits]
            eng.wait_ge(const_loaded, 16)
            for s, value in waits:
                eng.wait_ge(s, value)

        def begin(eng, stage):
            settle(eng, *[(end, stage) for end in (pe_end, act_end, dve_end, pool_end)])

        def finish(eng, end):
            eng.drain().then_inc(end, 1)

        @block.sync
        def _(sp):
            sp.dma_start(const[:, :], const_in).then_inc(const_loaded, 16)
            sp.dma_start(hidden[:, 0:2 * NT, :].rearrange("p (t h) s -> p t (h s)", t=NT),
                         x_in.rearrange("(t p) d -> p t d", p=P)).then_inc(x_loaded, 16)

            def piece(offset, width, slot, used):
                if used is not None:
                    sp.wait_ge(pieces_done, used)
                sp.dma_start(wring[:, slot, 0:width], bass.AP(weights.tensor, offset, [[width, P], [1, width]])
                             ).then_inc(w_loaded[slot], 16)

            size = P * PIECE
            for s in range(SLOTS):
                piece(s * size, PIECE, s, None)
            with sp.Fori(1, DEPTH * ROUNDS1) as r:
                for s in range(SLOTS):
                    piece(r * (SLOTS * size) + s * size, PIECE, s, r * SLOTS + s - SLOTS + 1)
            ffn = []
            for n, r_gu in zip(HALVES2, R_GU):
                ffn += [(r_gu, PIECE), (R_DOWN, n * P // 2)]
            runs = ffn + [(1 + NA_PAIRS + R_OUT, PIECE)] + ffn
            layer_size = sum(k * SLOTS * P * w for k, w in runs)
            with sp.Fori(0, DEPTH) as layer:
                at, rounds = DEPTH * ROUNDS1 * SLOTS * size, ROUND_B2
                for k, w in runs:
                    with sp.Fori(0, k) as r:
                        for s in range(SLOTS):
                            piece(layer * layer_size + r * (SLOTS * P * w) + (at + s * P * w), w, s,
                                  layer * (ROUNDS2 * SLOTS) + r * SLOTS + ((rounds - 1) * SLOTS + s + 1))
                    at += k * SLOTS * P * w
                    rounds += k

        @block.tensor
        def _(pe):
            def product(slot, rnd, accum, moving, n=NC, first=True, last=True):
                pe.wait_ge(w_loaded[slot], rnd * 16 + 16)
                for k in range(n):
                    mm = pe.matmul(accum[:, :], wring[:, slot, k * P:(k + 1) * P], moving(k),
                                   start=first and k == 0, stop=last and k == n - 1)
                mm.then_inc(pieces_done, 1)

            def four(rnd, gp, moving):
                for j in range(SLOTS):
                    pe.wait_ge(evacuated[j % 2], gp + j // 2)
                    product(j, rnd, acc[j % 2], moving)

            def down_round(rnd, gp, n):
                for j in range(2):
                    pe.wait_ge(evacuated[j], gp)
                    for half in range(2):
                        product(2 * j + half, rnd, acc[j], lambda k, half=half: hidden[:, half * n + k, :], n,
                                first=half == 0, last=half == 1)

            def norm(n):
                for k in range(NC):
                    pe.wait_ge(squared, n * NC + k + 1)
                    mm = pe.matmul(scp[0][:, :], ones, squares[:, k, :], start=k == 0, stop=k == NC - 1)
                mm.then_inc(summed, 1)
                finish(pe, pe_end)

            def layer_norm(n):
                for k in range(NC):
                    mm = pe.matmul(scp[0][:, :], ones, xT[:, k, :], start=k == 0, stop=k == NC - 1)
                mm.then_inc(ln_summed, 1)
                for k in range(NC):
                    pe.wait_ge(ln_squared, n * NC + k + 1)
                    mm = pe.matmul(scp[1][:, :], ones, squares[:, k, :], start=k == 0, stop=k == NC - 1)
                mm.then_inc(ln_var, 1)
                finish(pe, pe_end)

            def turn_values(it):
                pe.wait_ge(kv_ready, it + 1)
                for t in range(NT):
                    mm = pe.transpose(trp[0][:, t * P:(t + 1) * P], vT[:, t * P:(t + 1) * P], ident)
                mm.then_inc(v_turned, 1)

            def turn_probs(m, width, tb):
                if m >= 2:
                    pe.wait_ge(pt_ready, tb + m - 1)
                for j in range(width // P):
                    mm = pe.transpose(trp[m % 2][:, j * P:(j + 1) * P], m_prob[0][:, j * P:(j + 1) * P], ident)
                mm.then_inc(transposed, 1)

            m_prob = [None]

            def apply_values(m, tb, hh, t, width, values, first=True, last=True, extra=None):
                pe.wait_ge(pt_ready, tb + m + 1)
                o = outp[HEAD * hh:HEAD * (hh + 1), t * P:(t + 1) * P]
                if extra is not None:
                    pe.matmul(o, extra[0], extra[1], start=True, stop=False)
                n = width // P
                for j in range(n):
                    mm = pe.matmul(o, values(j), probT[:, m % 2, j * P:(j + 1) * P],
                                   start=first and extra is None and j == 0, stop=last and j == n - 1)
                mm.then_inc(pv_done, 1)

            def softmax_maps(mb, nb, tb, maps):
                n = len(maps)
                for i in range(n + 2):
                    if i < n:
                        q, k, width = maps[i][:3]
                        if i >= 2:
                            pe.wait_ge(biased, mb + i - 1)
                        pe.matmul(scp[i % 2][:, 0:width], q, k, start=True, stop=True).then_inc(scores_ready, 1)
                    if 1 <= i <= n:
                        pe.wait_ge(normed, nb + i)
                        m_prob[0] = prob[:, (i - 1) % 4, :]
                        turn_probs(i - 1, maps[i - 1][2], tb)
                    if i >= 2:
                        _, _, width, args = maps[i - 2]
                        apply_values(i - 2, tb, width=width, **args)

            def half_of(a, hh):
                return a[HEAD * hh:HEAD * (hh + 1)]

            def q_tile(hh, t):
                return half_of(qT, hh)[:, t * P:(t + 1) * P]

            def v_head(hh):
                return lambda j: v_nat[:, j, HEAD * hh:HEAD * (hh + 1)]

            def stick_breaking(layer, pair):
                it = layer * 6 + pair
                four(layer * ROUNDS1 + pair + ROUND_SB, layer * GPS1 + pair * 2 + GP_SETUP, lambda k: hT[:, k, :])
                turn_values(it)
                ub, tb = layer * (2 * U) + pair * U, layer * TRS1 + pair * U + TR_SB
                units = [(hh, t) for hh in range(2) for t in range(NT)]
                pe.wait_ge(v_copied, it + 1)
                for i in range(U + 2):
                    if i < U:
                        hh, t = units[i]
                        if i >= 2:
                            pe.wait_ge(sb_z, ub + i - 1)
                        pe.matmul(scp[i % 2][:, 0:(t + 1) * P], q_tile(hh, t), half_of(kT, hh)[:, 0:(t + 1) * P],
                                  start=True, stop=True).then_inc(sb_scores, 1)
                    if 1 <= i <= U:
                        pe.wait_ge(sb_prob, ub + i)
                        m_prob[0] = prob[:, (i - 1) % 4, :]
                        turn_probs(i - 1, (units[i - 1][1] + 1) * P, tb)
                    if i >= 2:
                        hh, t = units[i - 2]
                        apply_values(i - 2, tb, hh, t, (t + 1) * P, v_head(hh))
                finish(pe, pe_end)

            def moba(layer, pair):
                it = layer * 6 + pair + 2
                four(layer * ROUNDS1 + pair + ROUND_MB, layer * GPS1 + pair * 2 + (GP_SETUP + 2 * R_ATT),
                     lambda k: hT[:, k, :])
                turn_values(it)
                pe.wait_ge(v_copied, it + 1)
                softmax_maps(layer * MAPS1 + pair * U + MAPS_MB, layer * NORMS1 + pair * U + NORM_MB,
                             layer * TRS1 + pair * U + TR_MB,
                             [(q_tile(hh, t), half_of(kT, hh)[:, 0:(t + 1) * P], (t + 1) * P,
                               dict(hh=hh, t=t, values=v_head(hh))) for hh in range(2) for t in range(NT)])
                finish(pe, pe_end)

            def differential(layer, pair):
                it = layer * 6 + pair + 4
                four(layer * ROUNDS1 + pair + ROUND_DF, layer * GPS1 + pair * 2 + (GP_SETUP + 4 * R_ATT),
                     lambda k: hT[:, k, :])
                turn_values(it)
                pe.wait_ge(v_copied, it + 1)
                mb = layer * MAPS1 + pair * (2 * U) + MAPS_DF
                tb = layer * TRS1 + pair * U + TR_DF
                ub = layer * (2 * U) + pair * U
                units = [(hh, t) for hh in range(2) for t in range(NT)]
                for i in range(U + 2):
                    if i < U:
                        hh, t = units[i]
                        for half in range(2):
                            m = 2 * i + half
                            at = HEAD * hh + DIFF_HALF * half
                            if m >= 2:
                                pe.wait_ge(biased, mb + m - 1)
                            pe.matmul(scp[half][:, 0:(t + 1) * P], qT[at:at + DIFF_HALF, t * P:(t + 1) * P],
                                      kT[at:at + DIFF_HALF, 0:(t + 1) * P], start=True, stop=True
                                      ).then_inc(scores_ready, 1)
                    if 1 <= i <= U:
                        pe.wait_ge(df_weight, ub + i)
                        m_prob[0] = prob[:, (2 * (i - 1)) % 4, :]
                        turn_probs(i - 1, (units[i - 1][1] + 1) * P, tb)
                    if i >= 2:
                        hh, t = units[i - 2]
                        apply_values(i - 2, tb, hh, t, (t + 1) * P, v_head(hh))
                pe.wait_ge(df_sq, layer * PAIRS + pair + 1)
                pe.matmul(spare[:, :], c("head_ones"), score[:, 0, :], start=True, stop=True).then_inc(df_sum, 1)
                finish(pe, pe_end)

            def nsa_select(layer):
                rnd = layer * ROUNDS1 + ROUND_CMP
                for i, to in ((1, acc[0]), (2, acc[1]), (3, spare)):
                    for t in range(NT):
                        mm = pe.transpose(to[:, t * P:(t + 1) * P], side[:, i, t * P:(t + 1) * P], ident)
                    mm.then_inc(ns_turned, 1)
                groups = [(0, 0, scp[0]), (0, 1, scp[1]), (1, 0, trp[0]), (1, 1, trp[1])]
                pe.wait_ge(blocks_ready, layer + 1)
                per = PIECE // CMP_HIDDEN
                for n in range(R_CMP * SLOTS):
                    s = n % SLOTS
                    pe.wait_ge(w_loaded[s], (rnd + n // SLOTS) * 16 + 16)
                    for k in range(per):
                        l = n * per + k
                        for kv, h, to in groups:
                            at = k * CMP_HIDDEN + h * P
                            mm = pe.matmul(to[:, 0:N_CMP], half_of(wring[:, s, :], kv)[:, at:at + P],
                                           half_of(blocks, kv)[:, l, 0:N_CMP], start=l == 0, stop=l == CMP_LEN - 1)
                    mm.then_inc(pieces_done, 1)
                pe.wait_ge(gelu_ready, layer * 2 + 2)
                for half in range(2):
                    for h in range(2):
                        pe.matmul(half_of(scp[0], half)[:, 0:N_CMP], p1("w2k")[:, h * HEAD:(h + 1) * HEAD],
                                  gx[:, h, 0:N_CMP], start=h == 0, stop=h == 1)
                for h in range(2):
                    mm = pe.matmul(scp[1][:, 0:HEAD], h1v[:, h, :, :].rearrange("p a b -> p (a b)"),
                                   p1("w2v")[:, h * HEAD:(h + 1) * HEAD], start=h == 0, stop=h == 1)
                mm.then_inc(cmp_kv, 1)
                pe.wait_ge(cmp_copied, layer + 1)
                for t in range(NT):
                    for h in range(HEADS):
                        at = (t * PAIRS + h // 2) * CMP_PAD
                        mm = pe.matmul(trp[h % 2][:, at:at + N_CMP],
                                       half_of(side[:, 4 + h // 2, :], h % 2)[:, t * P:(t + 1) * P],
                                       half_of(kcT, h % 2)[:, 0:N_CMP], start=True, stop=True)
                mm.then_inc(cmp_scores, 1)
                for n, src, to in ((0, pc, trp[1]), (1, pcg, trp[0])):
                    pe.wait_ge(pc_ready, layer * 2 + n + 1)
                    for t in range(NT):
                        mm = pe.transpose(to[:, t * P:(t + 1) * P], src[:, t, :, :].rearrange("p a b -> p (a b)"),
                                          ident)
                    mm.then_inc(pc_turned, 1)
                    if n == 0:
                        pe.wait_ge(pc_copied, layer * 2 + 1)
                        for t in range(NT):
                            mm = pe.matmul(scp[0][:, t * N_SLC:(t + 1) * N_SLC], pcT[:, t * P:(t + 1) * P],
                                           c("cover"), start=True, stop=True)
                        mm.then_inc(imp_ready, 1)
                finish(pe, pe_end)

            def nsa_pair(layer, pair):
                pe.wait_ge(pair_ready, layer * 8 + pair * 2 + 6)
                maps = []
                for hh in range(2):
                    for t in range(NT):
                        cols = slice(0, (t + 1) * P)
                        maps.append((q_tile(hh, t), half_of(side[:, 1, :], hh)[:, cols], (t + 1) * P,
                                     dict(hh=hh, t=t, values=lambda j: vs_nat[:, j, HEAD:2 * HEAD], last=False,
                                          extra=(vc_pair[:, HEAD * hh:HEAD * (hh + 1)],
                                                 pcT[:, t * P:(t + 1) * P]))))
                        maps.append((q_tile(hh, t), half_of(side[:, 2, :], hh)[:, cols], (t + 1) * P,
                                     dict(hh=hh, t=t, values=lambda j: vw_nat[:, j, HEAD:2 * HEAD], first=False)))
                softmax_maps(layer * MAPS1 + pair * (2 * U) + MAPS_NS, layer * NORMS1 + pair * (2 * U) + NORM_NS,
                             layer * TRS1 + pair * (2 * U) + TR_NS, maps)
                finish(pe, pe_end)

            def neighbourhood(layer, pair):
                it = layer * NA_PAIRS + pair + DEPTH * 6
                four(layer * ROUNDS2 + pair + (ROUND_B2 + ROUND_NA), layer * GPS2 + pair * 2 + (GP_B2 + GP_NA),
                     lambda k: xT[:, k, :])
                turn_values(it)
                pe.wait_ge(v_copied, it + 1)
                softmax_maps(layer * (4 * U) + pair * U + DEPTH * MAPS1, layer * (4 * U) + pair * U + DEPTH * NORMS1,
                             layer * (4 * U) + pair * U + DEPTH * TRS1,
                             [(q_tile(hh, t), half_of(kT, hh), SEQ, dict(hh=hh, t=t, values=v_head(hh)))
                              for hh in range(2) for t in range(NT)])
                finish(pe, pe_end)

            def ffn(layer, stage, rounds, gps):
                for half, n in enumerate(HALVES2):
                    begin(pe, stage + 2 * half)
                    with pe.Fori(0, R_GU[half]) as r:
                        four(r + rounds, r * 2 + gps, lambda k: xT[:, k, :])
                    finish(pe, pe_end)
                    rounds, gps = rounds + R_GU[half], gps + n
                    begin(pe, stage + 2 * half + 1)
                    with pe.Fori(0, R_DOWN) as r:
                        down_round(r + rounds, r + gps, n // 2)
                    finish(pe, pe_end)
                    rounds, gps = rounds + R_DOWN, gps + NC // 2

            pe.wait_ge(const_loaded, 16)
            pe.wait_ge(x_loaded, 16)
            for k in range(NC):
                if k >= 2:
                    pe.wait_ge(evacuated[k % 2], k // 2)
                for t in range(NT):
                    at = t * D_MODEL + k * P
                    mm = pe.transpose(acc[k % 2][:, t * P:(t + 1) * P], big[:, at:at + P], ident)
                mm.then_inc(x_turned, 1)
            pe.wait_ge(table_loaded, 16)
            bucket = c("bucket")[0:N_BUCKETS + 1]
            pe.matmul(scp[0][0:12, 0:SEQ], tab33[:, :], bucket[:, 0:SEQ], start=True, stop=True)
            pe.matmul(scp[1][0:12, 0:P], tab33[:, :], bucket[:, SEQ:SEQ + P], start=True, stop=True
                      ).then_inc(vec_ready, 1)
            finish(pe, pe_end)

            with pe.Fori(0, DEPTH) as layer:
                stage = layer * STAGES1 + 1
                begin(pe, stage + ST_NORM)
                norm(layer * 2)
                with pe.Fori(0, PAIRS) as pair:
                    begin(pe, stage + pair + ST_SB)
                    stick_breaking(layer, pair)
                with pe.Fori(0, PAIRS) as pair:
                    begin(pe, stage + pair + ST_MB)
                    moba(layer, pair)
                with pe.Fori(0, PAIRS) as pair:
                    begin(pe, stage + pair + ST_DF)
                    differential(layer, pair)
                begin(pe, stage + ST_NSA)
                nsa_select(layer)
                with pe.Fori(0, PAIRS) as pair:
                    begin(pe, stage + pair + ST_NSP)
                    nsa_pair(layer, pair)
                begin(pe, stage + ST_OUT)
                with pe.Fori(0, R_OUT) as r:
                    four(layer * ROUNDS1 + r + ROUND_OUT, layer * GPS1 + r * 2 + (GP_SETUP + GP_OUT),
                         lambda k: mixT[:, k, :])
                finish(pe, pe_end)
                begin(pe, stage + ST_NORM2)
                norm(layer * 2 + 1)
                for half in range(2):
                    rounds = layer * ROUNDS1 + (ROUND_MLP + half * (R_UP + R_DOWN))
                    gps = layer * GPS1 + (GP_SETUP + GP_MLP + half * GP_HALF1)
                    begin(pe, stage + (ST_MLP + 2 * half))
                    with pe.Fori(0, R_UP) as r:
                        four(r + rounds, r * 2 + gps, lambda k: hT[:, k, :])
                    finish(pe, pe_end)
                    begin(pe, stage + (ST_MLP + 2 * half + 1))
                    with pe.Fori(0, R_DOWN) as r:
                        down_round(r + rounds + R_UP, r + gps + HALF1 // 2, HALF1 // 2)
                    finish(pe, pe_end)
            begin(pe, ST_FINAL)
            norm(2 * DEPTH)
            with pe.Fori(0, DEPTH) as layer:
                stage = layer * STAGES2 + ST_B2
                rounds, gps = layer * ROUNDS2 + ROUND_B2, layer * GPS2 + GP_B2
                ffn(layer, stage + ST_FFN1, rounds, gps)
                begin(pe, stage + ST_LN0)
                layer_norm(layer * 3)
                begin(pe, stage + ST_PROJ)
                four(rounds + ROUND_PROJ, gps + GP_PROJ, lambda k: xT[:, k, :])
                finish(pe, pe_end)
                with pe.Fori(0, NA_PAIRS) as pair:
                    begin(pe, stage + pair + ST_NA)
                    neighbourhood(layer, pair)
                begin(pe, stage + ST_POOL)
                for i in range(2):
                    settle(pe, (pooled, layer * 2 + i + 1))
                    for g in range(2):
                        mm = pe.matmul(half_of(scp[i], g)[:, :], half_of(p2("pool_w"), g)[:, i * HEAD:(i + 1) * HEAD],
                                       half_of(score[:, i, :], g), start=True, stop=True)
                    mm.then_inc(pool_mm, 1)
                finish(pe, pe_end)
                begin(pe, stage + ST_OUT2)
                with pe.Fori(0, R_OUT) as r:
                    four(rounds + r + ROUND_OUT2, gps + r * 2 + GP_OUT2, lambda k: mixT[:, k, :])
                finish(pe, pe_end)
                begin(pe, stage + ST_LN1)
                layer_norm(layer * 3 + 1)
                ffn(layer, stage + ST_FFN2, rounds + ROUND_FFN2, gps + GP_FFN2)
                begin(pe, stage + ST_LN2)
                layer_norm(layer * 3 + 2)
            begin(pe, ST_END)
            for n in range(2 * NT):
                t, half = n // 2, n % 2
                if n >= 2:
                    pe.wait_ge(out_copied, n - 1)
                for k in range(NC // 2):
                    mm = pe.transpose(acc[n % 2][:, k * P:(k + 1) * P],
                                      xT[:, half * NC // 2 + k, t * P:(t + 1) * P], ident)
                mm.then_inc(out_turned, 1)

        @block.scalar
        def _(act):
            def copy(to, src, scale=1.0):
                return act.activation(to, src, ACT.Copy, scale=scale)

            def power(rs, src, scale, eps, n_ready):
                act.activation(rs, src, ACT.Ln, scale=scale, bias=eps)
                act.drain()
                act.activation(rs, rs, ACT.Exp, scale=-0.5).then_inc(n_ready, 1)

            def norm(n):
                for k in range(NC):
                    act.activation(squares[:, k, :], xT[:, k, :], ACT.Square).then_inc(squared, 1)
                act.wait_ge(summed, n + 1)
                power(rows[:, 0, :], scp[0][:, :], 1.0 / D_MODEL, eps_norm, rstd_ready)

            def layer_norm(n):
                for k in range(NC):
                    act.wait_ge(centred, n * NC + k + 1)
                    act.activation(squares[:, k, :], xT[:, k, :], ACT.Square).then_inc(ln_squared, 1)
                act.wait_ge(ln_var, n + 1)
                power(rows[:, 0, :], scp[1][:, :], 1.0 / D_MODEL, eps_ln, ln_rstd)

            def shift(n, which):
                for k in range(NC):
                    act.wait_ge(ln_scaled, n * NC + k + 1)
                    act.activation(xT[:, k, :], xT[:, k, :], ACT.Identity,
                                   bias=p2("ln_b")[:, which * NC + k:which * NC + k + 1])
                finish(act, act_end)

            def project(done, scale, to_side, side_scale, it):
                for j, (to, s) in enumerate(((qT, scale), (kT, 1.0), (vT, 1.0), (None, side_scale))):
                    settle(act, (pieces_done, done + j + 1))
                    if to is None:
                        copy(side[:, to_side, :].rearrange("p a s -> p (a s)"), acc[j % 2][:, :], s
                             ).then_inc(evacuated[j % 2], 1)
                    else:
                        copy(to, acc[j % 2][:, :], s).then_inc(evacuated[j % 2], 1)
                    if j == 2:
                        act.drain().then_inc(kv_ready, 1)
                act.wait_ge(v_turned, it + 1)
                copy(v_nat[:, :, :].rearrange("p t d -> p (t d)"), trp[0][:, :]).then_inc(v_copied, 1)

            def probs_out(m, width, tb):
                if m >= 2:
                    act.wait_ge(pv_done, tb + m - 1)
                act.wait_ge(transposed, tb + m + 1)
                copy(probT[:, m % 2, 0:width], trp[m % 2][:, 0:width]).then_inc(pt_ready, 1)

            def softmax_exp(m, width, mb):
                act.wait_ge(biased, mb + m + 1)
                act.activation(prob[:, m % 4, 0:width], score[:, m % 2, 0:width], ACT.Exp,
                               bias=negmax[:, m % 4:m % 4 + 1], scale=-1.0,
                               accum_out=denom[:, m % 4:m % 4 + 1]).then_inc(exped, 1)

            def softmax_maps(mb, tb, widths):
                n = len(widths)
                for i in range(n + 1):
                    if i < n:
                        if i >= 4:
                            act.wait_ge(transposed, tb + i - 3)
                        softmax_exp(i, widths[i], mb)
                    if i >= 1:
                        probs_out(i - 1, widths[i - 1], tb)

            causal = [(t + 1) * P for hh in range(2) for t in range(NT)]

            def stick_breaking(layer, pair):
                project(layer * (ROUNDS1 * SLOTS) + pair * SLOTS + ROUND_SB * SLOTS, HEAD ** -0.5,
                        bass.ds(pair, 1), 1.0, layer * 6 + pair)
                ub, tb = layer * (2 * U) + pair * U, layer * TRS1 + pair * U + TR_SB
                for i in range(U + 2):
                    if i < U:
                        w = causal[i]
                        if i >= 2:
                            act.wait_ge(sb_arg, ub + i - 1)
                        act.wait_ge(sb_z, ub + i + 1)
                        tail = sel_bias[:, i % 2, 0:w]
                        act.activation(tail, score[:, i % 2, 0:w], ACT.Abs)
                        act.drain()
                        act.activation(tail, tail, ACT.Exp, scale=-1.0)
                        act.drain()
                        act.activation(tail, tail, ACT.Ln, bias=one_col).then_inc(sb_log, 1)
                    if 1 <= i <= U:
                        m, w = i - 1, causal[i - 1]
                        if m >= 4:
                            act.wait_ge(transposed, tb + m - 3)
                        act.wait_ge(sb_arg, ub + m + 1)
                        act.activation(prob[:, m % 4, 0:w], prob_arg(m, w), ACT.Exp).then_inc(sb_prob, 1)
                    if i >= 2:
                        probs_out(i - 2, causal[i - 2], tb)
                finish(act, act_end)

            def prob_arg(m, w):
                return vs_vw[m % 2][:, 0:w]

            vs_vw = [vs_nat[:, :, :].rearrange("p t d -> p (t d)"), vw_nat[:, :, :].rearrange("p t d -> p (t d)")]

            def moba(layer, pair):
                project(layer * (ROUNDS1 * SLOTS) + pair * SLOTS + ROUND_MB * SLOTS, HEAD ** -0.5,
                        bass.ds(pair + 2, 1), 1.0, layer * 6 + pair + 2)
                softmax_maps(layer * MAPS1 + pair * U + MAPS_MB, layer * TRS1 + pair * U + TR_MB, causal)
                finish(act, act_end)

            def differential(layer, pair):
                project(layer * (ROUNDS1 * SLOTS) + pair * SLOTS + ROUND_DF * SLOTS, DIFF_HALF ** -0.5,
                        bass.ds(pair + 4, 1), HEAD ** -0.5, layer * 6 + pair + 4)
                mb = layer * MAPS1 + pair * (2 * U) + MAPS_DF
                tb = layer * TRS1 + pair * U + TR_DF
                for i in range(U + 1):
                    if i < U:
                        for half in range(2):
                            if i >= 2:
                                act.wait_ge(transposed, tb + i - 1)
                            softmax_exp(2 * i + half, causal[i], mb)
                    if i >= 1:
                        probs_out(i - 1, causal[i - 1], tb)
                n = layer * PAIRS + pair
                act.wait_ge(pv_done, tb + U)
                act.activation(score[:, 0, :], outp[:, :], ACT.Square).then_inc(df_sq, 1)
                act.wait_ge(df_sum, n + 1)
                power(rows[:, 1, :], spare[:, :], 1.0 / HEAD, lam_eps, df_rstd)
                finish(act, act_end)

            def nsa_select(layer):
                act.wait_ge(ns_turned, layer * 3 + 1)
                copy(vs_vw[0], acc[0][:, :])
                copy(side[HEAD:P, 1, :], side[0:HEAD, 1, :])
                act.wait_ge(ns_turned, layer * 3 + 2)
                copy(vs_vw[1], acc[1][:, :])
                copy(side[HEAD:P, 2, :], side[0:HEAD, 2, :])
                act.wait_ge(ns_turned, layer * 3 + 3)
                act.activation(gates, spare[:, :].rearrange("p (t g) -> p t g", t=NT)[:, :, 0:12], ACT.Exp,
                               scale=-1.0).then_inc(gate_exp, 1)
                act.wait_ge(pieces_done, layer * (ROUNDS1 * SLOTS) + (ROUND_CMP + R_CMP) * SLOTS)
                for g, src in enumerate((scp[0], scp[1], trp[0], trp[1])):
                    copy(gx[:, g, 0:N_CMP], src[:, 0:N_CMP])
                act.drain().then_inc(hid_copied, 1)
                act.activation(gt[:, :, 0:N_CMP], gx[:, :, 0:N_CMP], ACT.Square).then_inc(hid_sq, 1)
                act.wait_ge(hid_poly, layer + 1)
                act.activation(gt[:, :, 0:N_CMP], gt[:, :, 0:N_CMP], ACT.Exp,
                               scale=-2.0 * math.sqrt(2.0 / math.pi)).then_inc(hid_exp, 1)
                act.wait_ge(cmp_kv, layer + 1)
                copy(kcT[:, 0:N_CMP], scp[0][:, 0:N_CMP])
                for h in range(HEADS):
                    at = slice(h * CMP_PAD, (h + 1) * CMP_PAD)
                    copy(vc_diag[at, h * HEAD:(h + 1) * HEAD], scp[1][at, 0:HEAD])
                act.drain().then_inc(cmp_copied, 1)
                act.wait_ge(cmp_shift, layer + 1)
                act.activation(pc[:, :, :, 0:N_CMP].rearrange("p t h n -> p (t h) n"),
                               pcg[:, :, :, 0:N_CMP].rearrange("p t h n -> p (t h) n"), ACT.Exp
                               ).then_inc(cmp_exp, 1)
                for n, src in enumerate((trp[1], trp[0])):
                    act.wait_ge(pc_turned, layer * 2 + n + 1)
                    if n == 1:
                        act.wait_ge(imp_ready, layer + 1)
                    copy(pcT, src[:, :]).then_inc(pc_copied, 1)
                finish(act, act_end)

            def nsa_pair(layer, pair):
                softmax_maps(layer * MAPS1 + pair * (2 * U) + MAPS_NS, layer * TRS1 + pair * (2 * U) + TR_NS,
                             [w for w in causal for _ in range(2)])
                finish(act, act_end)

            def neighbourhood(layer, pair):
                project(layer * (ROUNDS2 * SLOTS) + pair * SLOTS + (ROUND_B2 + ROUND_NA) * SLOTS, HEAD ** -0.5,
                        bass.ds(pair, 1), 1.0, layer * NA_PAIRS + pair + DEPTH * 6)
                softmax_maps(layer * (4 * U) + pair * U + DEPTH * MAPS1, layer * (4 * U) + pair * U + DEPTH * TRS1,
                             [SEQ] * U)
                finish(act, act_end)

            def ffn(stage, rounds, count):
                for half, n in enumerate(HALVES2):
                    begin(act, stage + 2 * half)
                    with act.Fori(0, R_GU[half]) as r:
                        for j in range(2):
                            settle(act, (pieces_done, r * SLOTS + rounds * SLOTS + 2 * j + 1),
                                   *[(evacuated[1], r * 2 + count)][j:])
                            act.activation(evac[:, j, :], acc[0][:, :], ACT.Silu).then_inc(evacuated[0], 1)
                            act.drain().then_inc(silu_ready, 1)
                    finish(act, act_end)
                    finish(act, act_end)
                    rounds, count = rounds + R_GU[half] + R_DOWN, count + GP_HALF2[half]

            act.dma_start(tab33[0:N_BUCKETS, :], table_in).then_inc(table_loaded, 16)
            act.wait_ge(const_loaded, 16)
            act.wait_ge(zeroed, 1)
            copy(tab33[N_BUCKETS:N_BUCKETS + 1, :], c("neg_rows")[N_BUCKETS:N_BUCKETS + 1, :]).then_inc(tab_set, 1)
            for k in range(0, NC, 2):
                act.wait_ge(x_turned, k + 1)
                copy(xT[:, k, :], acc[0][:, :]).then_inc(evacuated[0], 1)
            act.wait_ge(vec_ready, 1)
            copy(score[0:12, :, :].rearrange("p b s -> p (b s)")[:, 0:SEQ], scp[0][0:12, 0:SEQ])
            copy(score[0:12, :, :].rearrange("p b s -> p (b s)")[:, SEQ:SEQ + P], scp[1][0:12, 0:P])
            act.drain().then_inc(vec_copied, 1)
            act.wait_ge(vec_copied, 1)
            vec = score[0:12, :, :].rearrange("p b s -> p (b s)")[:, 0:SEQ + P]
            act.dma_start(bias_scratch, vec.unsqueeze(1).to_broadcast([12, P, SEQ + P])).then_inc(bias_stored, 16)
            act.wait_ge(bias_stored, 16)
            act.dma_start(t5, bass.AP(bias_scratch.tensor, P - 1, [[SEQ + P - 1, P], [P * (SEQ + P), 12], [1, SEQ]])
                          ).then_inc(t5_loaded, 16)
            finish(act, act_end)

            with act.Fori(0, DEPTH) as layer:
                stage = layer * STAGES1 + 1
                begin(act, stage + ST_NORM)
                act.dma_start(par1[:, :], par1_in[bass.ds(layer, 1)].rearrange("o p n -> p (o n)")
                              ).then_inc(par_loaded, 16)
                norm(layer * 2)
                act.wait_ge(lam_dots, layer + 1)
                act.activation(lam2, lam_tmp, ACT.Exp).then_inc(lam_exps, 1)
                finish(act, act_end)
                with act.Fori(0, PAIRS) as pair:
                    begin(act, stage + pair + ST_SB)
                    stick_breaking(layer, pair)
                with act.Fori(0, PAIRS) as pair:
                    begin(act, stage + pair + ST_MB)
                    moba(layer, pair)
                with act.Fori(0, PAIRS) as pair:
                    begin(act, stage + pair + ST_DF)
                    differential(layer, pair)
                begin(act, stage + ST_NSA)
                nsa_select(layer)
                with act.Fori(0, PAIRS) as pair:
                    begin(act, stage + pair + ST_NSP)
                    nsa_pair(layer, pair)
                finish(act, act_end)
                begin(act, stage + ST_NORM2)
                norm(layer * 2 + 1)
                finish(act, act_end)
                for half in range(2):
                    begin(act, stage + (ST_MLP + 2 * half))
                    done = layer * (ROUNDS1 * SLOTS) + (ROUND_MLP + half * (R_UP + R_DOWN)) * SLOTS
                    with act.Fori(0, R_UP) as r:
                        for j in range(SLOTS):
                            settle(act, (pieces_done, done + r * SLOTS + j + 1))
                            act.activation(evac[:, j % 2, :], acc[j % 2][:, :], ACT.Relu).then_inc(evacuated[j % 2], 1)
                            act.drain()
                            act.activation(hidden[:, bass.ds(r * SLOTS + j, 1), :].rearrange("p a s -> p (a s)"),
                                           evac[:, j % 2, :], ACT.Square)
                            act.drain()
                    finish(act, act_end)
                    finish(act, act_end)
            begin(act, ST_FINAL)
            norm(2 * DEPTH)
            finish(act, act_end)
            with act.Fori(0, DEPTH) as layer:
                stage = layer * STAGES2 + ST_B2
                begin(act, stage + ST_FFN1)
                act.dma_start(par2[:, :], par2_in[bass.ds(layer, 1)].rearrange("o p n -> p (o n)")
                              ).then_inc(par_loaded, 16)
                with act.Fori(0, NA_HEADS) as h:
                    for a in range(2):
                        act.dma_start(
                            rpb_raw[a * GRID_W:(a + 1) * GRID_W, bass.ds(h, 1), :].rearrange(
                                "p o (j k) -> p (o j) k", j=NA_J),
                            bass.AP(rpb_in.tensor,
                                    layer * (GRID_W * RPB_SIZE) + h * (RPB_H * RPB_W)
                                    + (RPB_PAD + (1 - a) * RPB_W + NA_COLS - 1),
                                    [[RPB_SIZE - 1, GRID_W], [RPB_W, NA_J], [1, GRID_W]])).then_inc(rpb_loaded, 16)
                ffn(stage + ST_FFN1, layer * ROUNDS2 + ROUND_B2, layer * GPS2 + GP_B2)
                begin(act, stage + ST_LN0)
                layer_norm(layer * 3)
                shift(layer * 3, 0)
                begin(act, stage + ST_PROJ)
                for j in range(SLOTS):
                    act.wait_ge(pieces_done, layer * (ROUNDS2 * SLOTS) + (ROUND_B2 + ROUND_PROJ) * SLOTS + j + 1)
                    copy(side[:, 4 + j, :], acc[j % 2][:, :]).then_inc(evacuated[j % 2], 1)
                finish(act, act_end)
                with act.Fori(0, NA_PAIRS) as pair:
                    begin(act, stage + pair + ST_NA)
                    neighbourhood(layer, pair)
                begin(act, stage + ST_POOL)
                for i in range(2):
                    settle(act, (pool_mm, layer * 2 + i + 1))
                    act.activation(mixT[:, i, :], scp[i][:, :], ACT.Copy, scale=p2("pool_scale")[:, i:i + 1])
                finish(act, act_end)
                finish(act, act_end)
                begin(act, stage + ST_LN1)
                layer_norm(layer * 3 + 1)
                shift(layer * 3 + 1, 1)
                ffn(stage + ST_FFN2, layer * ROUNDS2 + (ROUND_B2 + ROUND_FFN2), layer * GPS2 + (GP_B2 + GP_FFN2))
                begin(act, stage + ST_LN2)
                layer_norm(layer * 3 + 2)
                shift(layer * 3 + 2, 2)
            begin(act, ST_END)
            for n in range(2 * NT):
                act.wait_ge(out_turned, n + 1)
                copy(big[:, n * SEQ:(n + 1) * SEQ], acc[n % 2][:, :]).then_inc(out_copied, 1)
                if n % 2:
                    t = n // 2
                    act.wait_ge(out_copied, n + 1)
                    act.dma_start(out[t * P:(t + 1) * P, :], big[:, t * D_MODEL:(t + 1) * D_MODEL]
                                  ).then_inc(stored, 16)
            act.wait_ge(stored, 16 * NT)

        @block.vector
        def _(dve):
            def norm(n, gain, to):
                dve.wait_ge(rstd_ready, n + 1)
                for k in range(NC):
                    dve.scalar_tensor_tensor(to[:, k, :], xT[:, k, :], gain[:, k:k + 1], rows[:, 0, :],
                                             ALU.mult, ALU.mult)
                finish(dve, dve_end)

            def layer_norm(n, which):
                dve.wait_ge(ln_summed, n + 1)
                for k in range(NC):
                    dve.scalar_tensor_tensor(xT[:, k, :], scp[0][:, :], -1.0 / D_MODEL, xT[:, k, :],
                                             ALU.mult, ALU.add).then_inc(centred, 1)
                dve.drain()
                dve.wait_ge(ln_rstd, n + 1)
                for k in range(NC):
                    dve.scalar_tensor_tensor(xT[:, k, :], xT[:, k, :],
                                             p2("ln_g")[:, which * NC + k:which * NC + k + 1], rows[:, 0, :],
                                             ALU.mult, ALU.mult).then_inc(ln_scaled, 1)
                finish(dve, dve_end)

            def out_chunk(chunk):
                return mixT[:, chunk, :].rearrange("p a s -> p (a s)")

            def bias_map(m, width, mb, bias, selected=None):
                waits = [(scores_ready, mb + m + 1)]
                if m >= 2:
                    waits.append((exped, mb + m - 1))
                if selected is not None:
                    waits.append((sel_ready, selected))
                settle(dve, *waits)
                dve.tensor_tensor_reduce(score[:, m % 2, 0:width], scp[m % 2][:, 0:width], bias, -1.0, 3e38,
                                         ALU.add, ALU.min, negmax[:, m % 4:m % 4 + 1]).then_inc(biased, 1)

            def reciprocal_of(m, mb, gate=None):
                col = slice(m % 4, m % 4 + 1)
                dve.wait_ge(exped, mb + m + 1)
                dve.tensor_scalar(denom[:, col], denom[:, col], TINY, None, ALU.max)
                dve.drain()
                if gate is None:
                    return dve.reciprocal(recip[:, col], denom[:, col])
                dve.reciprocal(recip[:, col], denom[:, col])
                dve.drain()
                return dve.tensor_tensor(recip[:, col], recip[:, col], gate, ALU.mult)

            def softmax_maps(mb, maps):
                for i in range(len(maps) + 1):
                    if i < len(maps):
                        width, bias, _, ready = maps[i]
                        bias_map(i, width, mb, bias, ready)
                    if i >= 1:
                        reciprocal_of(i - 1, mb, maps[i - 1][2]).then_inc(recip_ready, 1)

            def heads_out(tb, count, chunk):
                dve.wait_ge(pv_done, tb + count)
                dve.tensor_scalar(out_chunk(chunk), outp[:, :], 1.0, None, ALU.mult)
                finish(dve, dve_end)

            def t5_cols(a, hh, t):
                return a[:, hh, SEQ - (t + 1) * P:SEQ]

            units = [(hh, t) for hh in range(2) for t in range(NT)]

            def stick_breaking(layer, pair):
                ub, tb = layer * (2 * U) + pair * U, layer * TRS1 + pair * U + TR_SB
                arg = [vs_nat[:, :, :].rearrange("p t d -> p (t d)"), vw_nat[:, :, :].rearrange("p t d -> p (t d)")]
                dve.memset(blocks[:, 0:SEQ // CMP_PAD, :], 1.0)
                one_row = blocks[:, 0:SEQ // CMP_PAD, :].rearrange("p a b -> p (a b)")
                for i in range(U + 1):
                    if i < U:
                        t = units[i][1]
                        w = (t + 1) * P
                        dve.wait_ge(sb_scores, ub + i + 1)
                        dve.tensor_tensor(score[:, i % 2, 0:w], scp[i % 2][:, 0:w], c("strict")[:, SEQ - w:SEQ],
                                          ALU.add).then_inc(sb_z, 1)
                    if i >= 1:
                        m = i - 1
                        w = (units[m][1] + 1) * P
                        z, tail, a = score[:, m % 2, 0:w], sel_bias[:, m % 2, 0:w], arg[m % 2][:, 0:w]
                        dve.wait_ge(sb_log, ub + m + 1)
                        dve.scalar_tensor_tensor(tail, z, 0.0, tail, ALU.max, ALU.add)
                        dve.drain()
                        if m >= 2:
                            dve.wait_ge(sb_prob, ub + m - 1)
                        dve.tensor_tensor_scan(a[:, ::-1], one_row[:, 0:w], tail[:, ::-1], 0.0,
                                               ALU.mult, ALU.subtract)
                        dve.drain()
                        dve.tensor_tensor(a, a, z, ALU.add).then_inc(sb_arg, 1)
                        dve.drain()
                heads_out(tb, U, bass.ds(pair, 1))

            def moba(layer, pair):
                dve.wait_ge(pair_ready, layer * 8 + pair + 1)
                softmax_maps(layer * MAPS1 + pair * U + MAPS_MB,
                             [((t + 1) * P, t5_cols(pair_bias, hh, t), None, None) for hh, t in units])
                heads_out(layer * TRS1 + pair * U + TR_MB, U, bass.ds(pair + 2, 1))

            def differential(layer, pair):
                mb = layer * MAPS1 + pair * (2 * U) + MAPS_DF
                ub = layer * (2 * U) + pair * U
                dve.wait_ge(pair_ready, layer * 8 + pair + 3)
                for i in range(U + 1):
                    if i < U:
                        hh, t = units[i]
                        for half in range(2):
                            bias_map(2 * i + half, (t + 1) * P, mb, t5_cols(pair_bias, hh, t))
                    if i >= 1:
                        u = i - 1
                        w = (units[u][1] + 1) * P
                        m = 2 * u
                        reciprocal_of(m, mb, lam_scale)
                        reciprocal_of(m + 1, mb, lam_one).then_inc(recip_ready, 1)
                        dve.drain()
                        dve.wait_ge(df_second, ub + u + 1)
                        dve.scalar_tensor_tensor(prob[:, m % 4, 0:w], prob[:, m % 4, 0:w],
                                                 recip[:, m % 4:m % 4 + 1], prob[:, m % 4 + 1, 0:w],
                                                 ALU.mult, ALU.subtract).then_inc(df_weight, 1)
                dve.wait_ge(df_rstd, layer * PAIRS + pair + 1)
                dve.scalar_tensor_tensor(out_chunk(bass.ds(pair + 6, 1)), outp[:, :], subln, rows[:, 1, :],
                                         ALU.mult, ALU.mult)
                finish(dve, dve_end)

            def nsa_select(layer):
                src = side[:, 0, :]
                dve.tensor_tensor(blocks[:, :, 0:N_CMP],
                                  bass.AP(src.tensor, src.offset, [list(src.ap[0]), [1, CMP_LEN], [CMP_STRIDE, N_CMP]]),
                                  p1("pos").unsqueeze(2).to_broadcast([P, CMP_LEN, N_CMP]), ALU.add
                                  ).then_inc(blocks_ready, 1)
                dve.wait_ge(gate_exp, layer + 1)
                dve.tensor_scalar(gates, gates, 1.0, None, ALU.add)
                dve.drain()
                dve.reciprocal(gates, gates)
                x, g = gx[:, :, 0:N_CMP], gt[:, :, 0:N_CMP]
                dve.wait_ge(hid_sq, layer + 1)
                dve.tensor_scalar(g, g, 0.044715, 1.0, ALU.mult, ALU.add)
                dve.drain()
                dve.tensor_tensor(g, g, x, ALU.mult).then_inc(hid_poly, 1)
                dve.wait_ge(hid_exp, layer + 1)
                dve.tensor_scalar(g, g, 1.0, None, ALU.add)
                dve.drain()
                dve.reciprocal(g, g)
                dve.drain()
                for h in range(2):
                    dve.tensor_tensor(h1v[:, h, :, 0:N_CMP],
                                      gx[:, 2 + h, 0:N_CMP].unsqueeze(1).to_broadcast([P, HEADS, N_CMP]),
                                      gt[:, 2 + h, 0:N_CMP].unsqueeze(1).to_broadcast([P, HEADS, N_CMP]), ALU.mult)
                dve.drain().then_inc(gelu_ready, 1)
                dve.tensor_tensor(gx[:, 0:2, 0:N_CMP], gx[:, 0:2, 0:N_CMP], gt[:, 0:2, 0:N_CMP], ALU.mult
                                  ).then_inc(gelu_ready, 1)

                def flat(a):
                    return a[:, :, :, 0:N_CMP].rearrange("p t h n -> p (t h) n")

                def spread(a):
                    return a.unsqueeze(2).to_broadcast([P, NT * HEADS, N_CMP])

                dve.wait_ge(cmp_scores, layer + 1)
                for odd in range(2):
                    def every_other(a):
                        return a.rearrange("p t (a b) n -> p b (t a) n", b=2)[:, odd, :, 0:N_CMP]

                    dve.tensor_tensor(every_other(pcg[:, :, :, :]),
                                      trp[odd][:, 0:SEQ // 2].rearrange("p (a n) -> p a n", n=CMP_PAD)[:, :, 0:N_CMP],
                                      every_other(cmp_bias[:, :, :, :]), ALU.add)
                dve.drain()
                dve.tensor_reduce(cmax, flat(pcg), AX.X, ALU.max)
                dve.drain()
                dve.tensor_tensor(flat(pcg), flat(pcg), spread(cmax), ALU.subtract).then_inc(cmp_shift, 1)
                dve.wait_ge(cmp_exp, layer + 1)
                dve.tensor_tensor(flat(pc), flat(pc), flat(cmp_mask), ALU.mult)
                dve.drain()
                dve.tensor_reduce(csum, flat(pc), AX.X, ALU.add)
                dve.drain()
                dve.tensor_scalar(csum, csum, TINY, None, ALU.max)
                dve.drain()
                dve.reciprocal(csum, csum)
                dve.drain()
                dve.tensor_tensor(flat(pc), flat(pc), spread(csum), ALU.mult).then_inc(pc_ready, 1)
                dve.drain()
                dve.tensor_tensor(pcg[:, :, :, 0:N_CMP].rearrange("p t h n -> p (t h) n"), flat(pc),
                                  gates_of(0), ALU.mult).then_inc(pc_ready, 1)
                dve.wait_ge(imp_ready, layer + 1)
                dve.tensor_tensor(imp, scp[0][:, 0:NT * N_SLC].rearrange("p (t j) -> p t j", t=NT),
                                  c("past").rearrange("p (t j) -> p t j", t=NT), ALU.mult)
                dve.drain()
                dve.tensor_tensor(imp, imp, c("force").rearrange("p (t j) -> p t j", t=NT), ALU.add)
                dve.drain()
                shape = [P, NT, N_SLC, N_SLC]
                mine, other = imp.unsqueeze(3).to_broadcast(shape), imp.unsqueeze(2).to_broadcast(shape)
                more = beats[:, 0, :].rearrange("p (t j i) -> p t j i", t=NT, j=N_SLC)
                same = beats[:, 1, :].rearrange("p (t j i) -> p t j i", t=NT, j=N_SLC)
                dve.tensor_tensor(more, other, mine, ALU.is_gt)
                dve.tensor_tensor(same, other, mine, ALU.is_equal)
                dve.drain()
                dve.tensor_tensor(beats[:, 1, :].rearrange("p (t j) -> p t j", t=NT),
                                  beats[:, 1, :].rearrange("p (t j) -> p t j", t=NT),
                                  c("earlier").unsqueeze(1).to_broadcast([P, NT, N_SLC * N_SLC]), ALU.mult)
                dve.drain()
                dve.tensor_tensor(beats[:, 0, :], beats[:, 0, :], beats[:, 1, :], ALU.add)
                dve.drain()
                dve.tensor_reduce(rank, more, AX.X, ALU.add)
                dve.drain()
                dve.tensor_scalar(sel_neg, rank, float(SLC_TOPN), NEG, ALU.is_ge, ALU.mult)
                finish(dve, dve_end)

            def gates_of(branch):
                g = gates[:, :, branch * HEADS:(branch + 1) * HEADS]
                return g.unsqueeze(3).to_broadcast([P, NT, HEADS, N_CMP])

            def nsa_pair(layer, pair):
                dve.tensor_copy(qT, side[:, bass.ds(pair + 4, 1), :].rearrange("p a s -> p (a s)"))
                dve.tensor_copy(vc_pair[:, :], vc_diag[:, bass.ds(pair * P, P)])
                dve.drain().then_inc(pair_ready, 1)
                dve.wait_ge(pair_ready, layer * 8 + pair * 2 + 6)
                sel = layer * (2 * U) + pair * U
                maps = []
                for n, (hh, t) in enumerate(units):
                    w = (t + 1) * P
                    for branch in (1, 2):
                        g = gates[:, t, bass.ds(pair * 2 + (branch * HEADS + hh), 1)]
                        if branch == 1:
                            maps.append((w, sel_bias[:, n % 2, 0:w], g, sel + n + 1))
                        else:
                            maps.append((w, t5_cols(pair_bias, hh, t), g, None))
                softmax_maps(layer * MAPS1 + pair * (2 * U) + MAPS_NS, maps)
                heads_out(layer * TRS1 + pair * (2 * U) + TR_NS, 2 * U, bass.ds(pair + 4, 1))

            def neighbourhood(layer, pair):
                dve.wait_ge(pair_ready, layer * NA_PAIRS + pair + (DEPTH * 8 + 1))
                maps = []
                for hh, t in units:
                    at = (NT - 1 - t) * 2 * GRID_W
                    maps.append((SEQ, pair_bias[:, hh, at:at + SEQ], None, None))
                softmax_maps(layer * (4 * U) + pair * U + DEPTH * MAPS1, maps)
                heads_out(layer * (4 * U) + pair * U + DEPTH * TRS1, U, bass.ds(pair + 4, 1))

            def add_out(rounds, count, per, scale, base=xT, to=xT):
                with dve.Fori(0, count // per) as r:
                    for j in range(per):
                        dve.wait_ge(pieces_done, r * SLOTS + rounds * SLOTS + (j + 1) * SLOTS // per)
                        x, y = (a[:, bass.ds(r * per + j, 1), :].rearrange("p a s -> p (a s)") for a in (base, to))
                        if scale is None:
                            ins = dve.tensor_tensor(y, acc[j % 2][:, :], x, ALU.add)
                        else:
                            ins = dve.scalar_tensor_tensor(y, x, scale, acc[j % 2][:, :], ALU.mult, ALU.add)
                        ins.then_inc(evacuated[j % 2], 1)
                finish(dve, dve_end)

            def ffn(stage, rounds, silu):
                for half, n in enumerate(HALVES2):
                    begin(dve, stage + 2 * half)
                    with dve.Fori(0, R_GU[half]) as r:
                        for j in range(2):
                            dve.wait_ge(silu_ready, silu + r * 2 + j + 1)
                            dve.wait_ge(pieces_done, r * SLOTS + rounds * SLOTS + 2 * j + 2)
                            dve.scalar_tensor_tensor(
                                hidden[:, bass.ds(r * 2 + j, 1), :].rearrange("p a s -> p (a s)"), acc[1][:, :], 0.5,
                                evac[:, j, :], ALU.mult, ALU.mult).then_inc(evacuated[1], 1)
                    finish(dve, dve_end)
                    rounds, silu = rounds + R_GU[half], silu + n
                    begin(dve, stage + 2 * half + 1)
                    if half == 0:
                        add_out(rounds, NC, 2, ALPHA, to=hT)
                    else:
                        add_out(rounds, NC, 2, None, base=hT)
                    rounds = rounds + R_DOWN

            dve.memset(eps_norm, NORM_EPS)
            dve.memset(eps_ln, LN_EPS)
            dve.memset(one_col, 1.0)
            dve.memset(vc_diag[:, :], 0.0)
            dve.memset(h1v[:, :, :, :], 0.0)
            dve.memset(pc[:, :, :, :], 0.0)
            dve.memset(pcg[:, :, :, :], 0.0)
            dve.memset(cmp_bias[:, :, :, :], NEG)
            dve.memset(pair_bias, 0.0).then_inc(zeroed, 1)
            for k in range(1, NC, 2):
                dve.wait_ge(x_turned, k + 1)
                dve.tensor_copy(xT[:, k, :], acc[1][:, :]).then_inc(evacuated[1], 1)
            dve.wait_ge(t5_loaded, 16)
            for t in range(NT):
                n = (t + 1) * P // CMP_STRIDE - 1
                first = (NT - 1 - t) * P + CMP_LEN - 1
                dve.tensor_copy(cmp_bias[:, t, :, 0:n],
                                t5[:, HEADS:2 * HEADS, first:first + (n - 1) * CMP_STRIDE + 1:CMP_STRIDE])
            dve.drain()
            dve.tensor_scalar(cmp_mask[:, :, :, :].rearrange("p t h n -> p (t h n)"),
                              cmp_bias[:, :, :, :].rearrange("p t h n -> p (t h n)"), NEG / 10, None, ALU.is_gt)
            finish(dve, dve_end)

            with dve.Fori(0, DEPTH) as layer:
                stage = layer * STAGES1 + 1
                begin(dve, stage + ST_NORM)
                dve.wait_ge(par_loaded, layer * 16 + 16)
                lv = p1("lam").rearrange("p (a b d) -> p a b d", a=2, b=2)
                dve.tensor_tensor(lam_prod.rearrange("p (a d) -> p a d", a=2), lv[:, :, 0, :], lv[:, :, 1, :], ALU.mult)
                dve.drain()
                dve.tensor_reduce(lam_tmp, lam_prod.rearrange("p (a d) -> p a d", a=2), AX.X, ALU.add
                                  ).then_inc(lam_dots, 1)
                dve.wait_ge(lam_exps, layer + 1)
                dve.scalar_tensor_tensor(lam_one, lam2[:, 0:1], p1("lam_init")[:, 0:1], lam2[:, 1:2], ALU.add,
                                         ALU.subtract)
                dve.drain()
                dve.scalar_tensor_tensor(lam_scale, lam_one, -1.0, lam_one, ALU.mult, ALU.max)
                dve.drain()
                dve.tensor_scalar(lam_scale, lam_scale, 1.0, None, ALU.max)
                dve.drain()
                dve.reciprocal(lam_scale, lam_scale)
                dve.drain()
                dve.tensor_tensor(lam_one, lam_one, lam_scale, ALU.mult)
                dve.tensor_scalar(lam_eps, lam_scale, lam_scale, NORM_EPS, ALU.mult, ALU.mult)
                dve.tensor_tensor(subln, p1("subln"), p1("lam_init")[:, 1:2], ALU.mult)
                norm(layer * 2, p1("norm_attn"), hT)
                with dve.Fori(0, PAIRS) as pair:
                    begin(dve, stage + pair + ST_SB)
                    stick_breaking(layer, pair)
                with dve.Fori(0, PAIRS) as pair:
                    begin(dve, stage + pair + ST_MB)
                    moba(layer, pair)
                with dve.Fori(0, PAIRS) as pair:
                    begin(dve, stage + pair + ST_DF)
                    differential(layer, pair)
                begin(dve, stage + ST_NSA)
                nsa_select(layer)
                with dve.Fori(0, PAIRS) as pair:
                    begin(dve, stage + pair + ST_NSP)
                    nsa_pair(layer, pair)
                begin(dve, stage + ST_OUT)
                add_out(layer * ROUNDS1 + ROUND_OUT, NC, SLOTS, None)
                begin(dve, stage + ST_NORM2)
                norm(layer * 2 + 1, p1("norm_mlp"), hT)
                for half in range(2):
                    finish(dve, dve_end)
                    begin(dve, stage + (ST_MLP + 2 * half + 1))
                    add_out(layer * ROUNDS1 + (ROUND_MLP + half * (R_UP + R_DOWN) + R_UP), NC, 2, None)
            begin(dve, ST_FINAL)
            norm(2 * DEPTH, p1("final_norm"), xT)
            with dve.Fori(0, DEPTH) as layer:
                stage = layer * STAGES2 + ST_B2
                ffn(stage + ST_FFN1, layer * ROUNDS2 + ROUND_B2, layer * (2 * sum(HALVES2)))
                begin(dve, stage + ST_LN0)
                dve.wait_ge(par_loaded, layer * 16 + 16 * (DEPTH + 1))
                layer_norm(layer * 3, 0)
                finish(dve, dve_end)
                with dve.Fori(0, NA_PAIRS) as pair:
                    begin(dve, stage + pair + ST_NA)
                    neighbourhood(layer, pair)
                begin(dve, stage + ST_POOL)
                border = max(POOL_WINDOWS)
                wide = SEQ + 2 * border
                pads = [big_pad(n, wide) for n in range(3)]
                dve.memset(pads[0], 0.0)
                dve.memset(pads[1], 0.0)
                dve.memset(pads[2], 0.0)
                dve.drain()
                for i in range(2):
                    dve.tensor_copy(pads[0][:, border:border + SEQ], side[:, i, :])
                    dve.drain()
                    at, reach, done = 0, 1, 0
                    for w in POOL_WINDOWS[0:2 * i + 2]:
                        lo, hi = (1, 0) if w == 2 else (w // 4, w // 4)
                        to = 1 if at != 1 else 2
                        span = slice(border // 2, wide - border // 2)
                        dve.tensor_tensor(pads[to][:, span], pads[at][:, span.start - lo:span.stop - lo],
                                          pads[at][:, span.start + hi:span.stop + hi], ALU.add)
                        dve.drain()
                        at = to
                        if w in POOL_WINDOWS[2 * i:2 * i + 2]:
                            g = slice(HEAD * done, HEAD * (done + 1))
                            mean = score[g, i, :]
                            dve.tensor_tensor(mean, pads[at][g, border:border + SEQ],
                                              c("inv_count")[g, i * SEQ:(i + 1) * SEQ], ALU.mult)
                            dve.drain()
                            dve.tensor_tensor(mean, mean, side[g, i, :], ALU.subtract)
                            done += 1
                    dve.drain().then_inc(pooled, 1)
                for i in range(2):
                    w = p2("conv")[:, 3 * i:3 * i + 3]
                    z = pads[1 + i]
                    dve.memset(z[:, 0:SEQ + 2], 0.0)
                    dve.drain()
                    dve.tensor_tensor(z[:, 1:SEQ + 1], side[:, 4 + i, :], side[:, 6 + i, :], ALU.mult)
                    dve.drain()
                    y = mixT[:, 2 + i, :]
                    dve.tensor_scalar(y, z[:, 0:SEQ], w[:, 0:1], None, ALU.mult)
                    dve.drain()
                    for k in (1, 2):
                        dve.scalar_tensor_tensor(y, z[:, k:k + SEQ], w[:, k:k + 1], y, ALU.mult, ALU.add)
                        dve.drain()
                    dve.tensor_tensor(y, y, side[:, 2 + i, :], ALU.mult)
                finish(dve, dve_end)
                begin(dve, stage + ST_OUT2)
                add_out(layer * ROUNDS2 + (ROUND_B2 + ROUND_OUT2), NC, SLOTS, ALPHA)
                begin(dve, stage + ST_LN1)
                layer_norm(layer * 3 + 1, 1)
                ffn(stage + ST_FFN2, layer * ROUNDS2 + (ROUND_B2 + ROUND_FFN2),
                    layer * (2 * sum(HALVES2)) + sum(HALVES2))
                begin(dve, stage + ST_LN2)
                layer_norm(layer * 3 + 2, 2)

        @block.gpsimd
        def _(pool):
            def scale_prob(m, width):
                return pool.tensor_tensor(prob[:, m % 4, 0:width], prob[:, m % 4, 0:width],
                                          recip[:, m % 4:m % 4 + 1].to_broadcast([P, width]), ALU.mult)

            def softmax_maps(rb, widths):
                for m, w in enumerate(widths):
                    pool.wait_ge(recip_ready, rb + m + 1)
                    scale_prob(m, w).then_inc(normed, 1)

            def idle(stage):
                finish(pool, pool_end)

            causal = [(t + 1) * P for hh in range(2) for t in range(NT)]

            def stage_bias(head):
                pool.tensor_copy(pair_bias[:, :, 0:SEQ], t5[:, bass.ds(head, 2), :])
                pool.drain().then_inc(pair_ready, 1)

            finish(pool, pool_end)
            pool.wait_ge(t5_loaded, 16)
            with pool.Fori(0, DEPTH) as layer:
                stage = layer * STAGES1 + 1
                idle(stage + ST_NORM)
                with pool.Fori(0, PAIRS) as pair:
                    idle(stage + pair + ST_SB)
                with pool.Fori(0, PAIRS) as pair:
                    begin(pool, stage + pair + ST_MB)
                    stage_bias(pair * 2)
                    softmax_maps(layer * RECIPS1 + pair * U + RECIP_MB, causal)
                    finish(pool, pool_end)
                with pool.Fori(0, PAIRS) as pair:
                    begin(pool, stage + pair + ST_DF)
                    stage_bias(pair * 2 + 2 * HEADS)
                    for u, w in enumerate(causal):
                        pool.wait_ge(recip_ready, layer * RECIPS1 + pair * U + (RECIP_DF + u + 1))
                        scale_prob(2 * u + 1, w).then_inc(df_second, 1)
                    finish(pool, pool_end)
                idle(stage + ST_NSA)
                with pool.Fori(0, PAIRS) as pair:
                    begin(pool, stage + pair + ST_NSP)
                    stage_bias(pair * 2 + HEADS)
                    rb = layer * RECIPS1 + pair * (2 * U) + RECIP_NS
                    mb = layer * MAPS1 + pair * (2 * U) + MAPS_NS

                    def select(n):
                        hh, t = n // NT, n % NT
                        w = (t + 1) * P
                        if n >= 2:
                            pool.wait_ge(biased, mb + 2 * (n - 2) + 1)
                        pool.tensor_tensor(
                            sel_bias[:, n % 2, 0:w].rearrange("p (j k) -> p j k", k=SLC_LEN),
                            pair_bias[:, hh, SEQ - w:SEQ].rearrange("p (j k) -> p j k", k=SLC_LEN),
                            sel_neg[:, t, 0:w // SLC_LEN].unsqueeze(2).to_broadcast([P, w // SLC_LEN, SLC_LEN]),
                            ALU.add).then_inc(sel_ready, 1)

                    select(0)
                    select(1)
                    for m in range(2 * U):
                        w = causal[m // 2]
                        pool.wait_ge(recip_ready, rb + m + 1)
                        scale_prob(m, w).then_inc(normed, 1)
                        if m % 2 and m // 2 + 2 < U:
                            select(m // 2 + 2)
                    finish(pool, pool_end)
                idle(stage + ST_OUT)
                idle(stage + ST_NORM2)
                for n in range(4):
                    idle(stage + (ST_MLP + n))
            idle(ST_FINAL)
            with pool.Fori(0, DEPTH) as layer:
                stage = layer * STAGES2 + ST_B2
                for n in range(ST_NA):
                    idle(stage + n)
                with pool.Fori(0, NA_PAIRS) as pair:
                    begin(pool, stage + pair + ST_NA)
                    pool.wait_ge(rpb_loaded, layer * (32 * NA_HEADS) + 32 * NA_HEADS)
                    for hh in range(2):
                        pool.tensor_tensor(
                            pair_bias[:, hh, :].rearrange("p (j k) -> p j k", k=GRID_W),
                            rpb_raw[:, bass.ds(pair * 2 + hh, 1), :].rearrange("p o (j k) -> p (o j) k", k=GRID_W),
                            c("col_mask").unsqueeze(1).to_broadcast([P, NA_J, GRID_W]), ALU.add)
                    pool.drain().then_inc(pair_ready, 1)
                    softmax_maps(layer * (4 * U) + pair * U + DEPTH * RECIPS1, [SEQ] * U)
                    finish(pool, pool_end)
                for n in range(ST_POOL, STAGES2):
                    idle(stage + n)


def _bucket(n):
    exact = N_BUCKETS // 2
    nf = np.maximum(n, 1).astype(np.float32)
    large = exact + (np.log(nf / np.float32(exact)) / np.float32(math.log(MAX_DISTANCE / exact))
                     * np.float32(N_BUCKETS - exact)).astype(np.int32)
    return np.where(n < exact, n, np.minimum(large, N_BUCKETS - 1))


def _constants():
    a = np.zeros((P, CONST_W), np.float32)

    def put(name, v):
        lo, hi = CONST[name]
        a[:v.shape[0], lo:hi] = v.reshape(v.shape[0], -1)

    p, m = np.arange(P)[:, None], np.arange(SEQ)[None]
    put("ident", np.eye(P))
    put("ones", np.ones((P, P)))
    put("head_ones", np.kron(np.eye(2), np.ones((HEAD, HEAD))))
    put("strict", np.where(p + SEQ - P - m >= 1, 0.0, NEG))
    start = np.arange(CMP_PAD)[:, None] * CMP_STRIDE
    s0 = np.arange(N_SLC)[None] * SLC_LEN
    cover = np.clip(np.minimum(start + CMP_LEN - 1, s0 + SLC_LEN - 1) - np.maximum(start, s0) + 1, 0, None) / CMP_LEN
    cover[N_CMP:] = 0
    put("cover", np.tile(cover, (HEADS, 1)))
    own = (np.arange(NT)[None, :, None] * P + p[:, :, None]) // SLC_LEN
    j = np.arange(N_SLC)[None, None]
    put("past", (j < own).astype(np.float32))
    put("force", np.where(j == own, -NEG, np.where(j < own, 0.0, NEG)))
    put("earlier", np.broadcast_to(np.arange(N_SLC)[None, None] < np.arange(N_SLC)[None, :, None], (P, N_SLC, N_SLC)))
    t = np.arange(SEQ)
    counts = [np.clip(t - w // 2 + w, 0, SEQ) - np.clip(t - w // 2, 0, SEQ) for w in POOL_WINDOWS]
    inv = 1.0 / np.stack(counts)
    put("inv_count", np.stack([np.repeat(inv[0:2], HEAD, 0), np.repeat(inv[2:4], HEAD, 0)], 1))
    qc, kc = np.arange(P)[:, None] % GRID_W, np.arange(GRID_W)[None]
    left = np.clip(qc - NA_COLS // 2, 0, GRID_W - NA_COLS)
    put("col_mask", np.where((kc >= left) & (kc < left + NA_COLS), 0.0, NEG))
    u = np.arange(SEQ + P)
    dist = SEQ - 1 - u
    hot = np.where(dist[None] >= 0, np.arange(N_BUCKETS)[:, None] == _bucket(np.maximum(dist, 0))[None], False)
    put("bucket", np.concatenate([hot, (dist < 0)[None]], 0).astype(np.float32))
    put("neg_rows", np.full((P, 12), NEG))
    return a


def _pieces(inputs):
    out = []

    def put(w):
        k = w.shape[0] // P
        out.append(w.reshape(k, P, P).transpose(1, 0, 2).reshape(-1))

    g = inputs
    sizes = (GROUP,) * 7 + (HEAD,) * 6 + (3 * HEADS,) + (GROUP,) * 3
    at = np.concatenate([[0], np.cumsum(sizes)]).tolist()
    for l in range(DEPTH):
        w = g["w_in"][l]

        def cols(i, pair):
            return w[:, at[i] + pair * P:at[i] + (pair + 1) * P]

        gate_cols = np.zeros((D_MODEL, P), w.dtype)
        gate_cols[:, 0:3 * HEADS] = w[:, at[13]:at[14]]
        sides = [[cols(7, 0), cols(9, 0)], [cols(11, 0), gate_cols], [cols(6, 0), cols(6, 1)]]
        for first, fourth in zip((0, 3, 14), sides):
            for pair in range(PAIRS):
                for i in range(3):
                    put(cols(first + i, pair))
                put(fourth[pair])
        both = np.concatenate([g[n][l].reshape(CMP_LEN, HEAD, CMP_HIDDEN).transpose(1, 0, 2)
                               for n in ("cmp_k_w1", "cmp_v_w1")], 0)
        per = PIECE // CMP_HIDDEN
        for n in range(CMP_LEN // per):
            out.append(both[:, n * per:(n + 1) * per].reshape(-1))
        for d in range(NC):
            put(g["w_out"][l][:, d * P:(d + 1) * P])
        for half in range(2):
            for f in range(half * HALF1, (half + 1) * HALF1):
                put(g["w_up"][l][:, f * P:(f + 1) * P])
            for d in range(NC):
                for k in range(2):
                    lo = (half * HALF1 + k * HALF1 // 2) * P
                    put(g["w_down"][l][lo:lo + HALF1 // 2 * P, d * P:(d + 1) * P])
    for l in range(DEPTH):
        def ffn(name):
            f0 = 0
            for n in HALVES2:
                for f in range(f0, f0 + n):
                    for part in ("gate", "up"):
                        put(g[f"{name}_w_{part}_2"][l][:, f * P:(f + 1) * P])
                for d in range(NC):
                    for k in range(2):
                        lo = (f0 + k * n // 2) * P
                        put(g[f"{name}_w_down_2"][l][lo:lo + n // 2 * P, d * P:(d + 1) * P])
                f0 += n

        ffn("ffn1")
        w = g["w_in_2"][l]
        for i in (4, 5, 6, 7):
            put(w[:, i * P:(i + 1) * P])
        qkv = NC * P
        for pair in range(NA_PAIRS):
            for i in range(3):
                lo = qkv + i * NA_HEADS * HEAD + pair * P
                put(w[:, lo:lo + P])
            put(w[:, pair * P:(pair + 1) * P])
        for d in range(NC):
            put(g["w_out_2"][l][:, d * P:(d + 1) * P])
        ffn("ffn2")
    return np.concatenate(out)


def _parameters(g):
    a = np.zeros((DEPTH, P, PAR1_W), np.float32)
    b = np.zeros((DEPTH, P, PAR2_W), np.float32)

    def put(to, cols, l, name, v):
        lo, hi = cols[name]
        to[l, :, lo:hi] = v.reshape(P, -1)

    def chunks(v):
        return v.reshape(-1, P).T

    for l in range(DEPTH):
        put(a, PAR1, l, "norm_attn", chunks(g["norm_attn"][l]))
        put(a, PAR1, l, "norm_mlp", chunks(g["norm_mlp"][l]))
        put(a, PAR1, l, "final_norm", chunks(g["final_norm"]))
        put(a, PAR1, l, "pos", np.concatenate([g["cmp_pos_k"][l].T, g["cmp_pos_v"][l].T], 0))
        put(a, PAR1, l, "subln", np.tile(g["diff_subln"][l], 2))
        init = 0.8 - 0.6 * math.exp(-0.3 * l)
        put(a, PAR1, l, "lam_init", np.tile(np.array([init, 1.0 - init], np.float32), (P, 1)))
        put(a, PAR1, l, "lam", np.tile(g["diff_lambda"][l].reshape(1, -1), (P, 1)))
        for n in "kv":
            put(a, PAR1, l, f"w2{n}", g[f"cmp_{n}_w2"][l].reshape(2, P, HEAD).transpose(1, 0, 2))
        put(b, PAR2, l, "ln_g", chunks(g["ln_g_2"][l]))
        put(b, PAR2, l, "ln_b", chunks(g["ln_b_2"][l]))
        put(b, PAR2, l, "pool_scale", chunks(g["pool_scale_2"][l]))
        put(b, PAR2, l, "conv", g["conv_w_2"][l].reshape(3, 2, P).transpose(2, 1, 0))
        put(b, PAR2, l, "pool_w", g["pool_w_2"][l].reshape(2, P, HEAD).transpose(1, 0, 2))
    return a, b


def kernel(**inputs):
    import concourse.bacc as bacc
    from concourse.bass_utils import run_bass_kernel_spmd

    g = {k: np.asarray(v) for k, v in inputs.items()}
    par1, par2 = _parameters(g)
    rpb = np.pad(g["rpb_2"].reshape(DEPTH, 1, -1), ((0, 0), (0, 0), (RPB_PAD, RPB_PAD)))
    rpb = np.ascontiguousarray(np.broadcast_to(rpb, (DEPTH, GRID_W, RPB_SIZE)))
    arrays = {
        "in_x": np.ascontiguousarray(g["x"].reshape(SEQ, D_MODEL)),
        "in_weights": _pieces(g),
        "in_const": _constants(),
        "in_par1": par1,
        "in_par2": par2,
        "in_table": np.ascontiguousarray(g["rel_bias"]),
        "in_rpb": rpb,
    }
    nc = bacc.Bacc("TRN2", target_bir_lowering=False, num_devices=1)
    args = [nc.dram_tensor(n, a.shape, mybir.dt.from_np(a.dtype), kind="ExternalInput").ap() for n, a in arrays.items()]
    out = nc.dram_tensor("out_x", (SEQ, D_MODEL), F32, kind="ExternalOutput").ap()
    emit(nc, *args, out)
    r = run_bass_kernel_spmd(nc, [arrays], core_ids=[0])
    return r.results[0]["out_x"].reshape(1, SEQ, D_MODEL)
```

```python
import math
from contextlib import ExitStack

import numpy as np

import concourse.bass as bass
from concourse import mybir

ALU = mybir.AluOpType
ACT = mybir.ActivationFunctionType
AX = mybir.AxisListType
F32 = mybir.dt.float32
F32R = mybir.dt.float32r

P = 128
DEPTH = 2
SEQ = 512
D_MODEL = 1024
NT = SEQ // P
NC = D_MODEL // P
HEAD = 64
HEADS = 4
GROUP = HEADS * HEAD
PAIRS = HEADS // 2
D_FF = 4 * D_MODEL
D_FF2 = 2816
NORM_EPS = 1e-6
LN_EPS = 1e-5
TINY = 1e-30
NEG = -1e30
N_BUCKETS, MAX_DISTANCE = 32, 128
CMP_LEN, CMP_STRIDE, CMP_HIDDEN = 32, 16, 256
N_CMP = (SEQ - CMP_LEN) // CMP_STRIDE + 1
CMP_PAD = 32
SLC_LEN, SLC_TOPN = 64, 4
N_SLC = SEQ // SLC_LEN
DIFF_HALF = HEAD // 2
ALPHA = (2.0 * DEPTH) ** 0.25
POOL_WINDOWS = (2, 4, 8, 16)
GRID_W = 64
GRID_H = SEQ // GRID_W
NA_HEADS, NA_PAIRS = 8, 4
NA_COLS = 16
RPB_W = 2 * NA_COLS - 1
RPB_H = 2 * GRID_H - 1
RPB_PAD = 64
RPB_SIZE = NA_HEADS * RPB_H * RPB_W + 2 * RPB_PAD
NA_J = 14
PART = 8
PARTS1 = D_FF // P // PART
PARTS2 = (8, 8, 6)
assert sum(PARTS2) * P == D_FF2

SLOTS = 4
BLOCKS_AT = 12 * SEQ
PIECE = NC * P

R_ATT, R_CMP, R_OUT = 2, 2, NC // SLOTS
R_UP, R_DOWN = PART // SLOTS, NC // SLOTS
ROUND_SB, ROUND_MB, ROUND_DF, ROUND_CMP = 0, R_ATT, 2 * R_ATT, 3 * R_ATT
ROUND_OUT = ROUND_CMP + R_CMP
ROUND_MLP = ROUND_OUT + R_OUT
R_PART1 = R_UP + R_DOWN
ROUNDS1 = ROUND_MLP + PARTS1 * R_PART1
R_GU = [2 * n // SLOTS for n in PARTS2]
ROUNDS_FFN = sum(R_GU) + len(PARTS2) * R_DOWN
ROUND_PROJ = ROUNDS_FFN
ROUND_NA = ROUND_PROJ + 1
ROUND_OUT2 = ROUND_NA + NA_PAIRS
ROUND_FFN2 = ROUND_OUT2 + R_OUT
ROUNDS2 = ROUND_FFN2 + ROUNDS_FFN
ROUND_B2 = DEPTH * ROUNDS1

GP_SETUP = NC // 2
GP_OUT = 3 * R_ATT * 2
GP_MLP = GP_OUT + NC // 2
GP_PART1 = (PART + NC) // 2
GPS1 = GP_MLP + PARTS1 * GP_PART1
GP_FFN = sum(PARTS2) + len(PARTS2) * NC // 2
GP_PROJ = GP_FFN
GP_NA = GP_PROJ + 2
GP_OUT2 = GP_NA + 2 * NA_PAIRS
GP_FFN2 = GP_OUT2 + NC // 2
GPS2 = GP_FFN2 + GP_FFN
GP_B2 = GP_SETUP + DEPTH * GPS1

SPLITS1, SPLITS2 = 3, 4
SPLIT_B2 = DEPTH * SPLITS1 + 1

(ST_NORM, ST_SB, ST_MB, ST_DF, ST_NSA, ST_NSP, ST_OUT, ST_NORM2, ST_MLP) = (0, 1, 3, 5, 7, 8, 10, 11, 12)
STAGES1 = 13
ST_FINAL = 1 + DEPTH * STAGES1
ST_B2 = ST_FINAL + 1
(ST_FFN1, ST_LN0, ST_PROJ, ST_NA, ST_POOL, ST_OUT2, ST_LN1, ST_FFN2, ST_LN2) = (0, 1, 2, 3, 7, 8, 9, 10, 11)
STAGES2 = 12
ST_END = ST_B2 + DEPTH * STAGES2
T5_LOADS = 3 * PAIRS

STATS = 8
U = 2 * NT
MAPS_MB, MAPS_DF, MAPS_NS = 0, 2 * U, 6 * U
MAPS1 = 10 * U
RECIP_MB, RECIP_DF, RECIP_NS = 0, 2 * U, 4 * U
RECIPS1 = 8 * U
NORM_MB, NORM_NS = 0, 2 * U
NORMS1 = 6 * U
TR_SB, TR_MB, TR_DF, TR_NS = 0, 2 * U, 4 * U, 6 * U
TRS1 = 10 * U



def columns(**widths):
    at, out = 0, {}
    for name, w in widths.items():
        out[name] = (at, at + w)
        at += w
    return out, at


CONST, CONST_W = columns(ident=P, ones=P, head_ones=P, strict=SEQ, cover=N_SLC, past=NT * N_SLC,
                         force=NT * N_SLC, earlier=N_SLC * N_SLC, inv_count=2 * SEQ, col_mask=GRID_W,
                         neg_rows=12)
PAR1, PAR1_W = columns(norm_attn=NC, norm_mlp=NC, final_norm=NC, pos=CMP_LEN, subln=1, lam_init=2,
                       lam=4 * DIFF_HALF, w2k=2 * HEAD, w2v=2 * HEAD)
PAR2, PAR2_W = columns(ln_g=3 * NC, ln_b=3 * NC, pool_scale=2, conv=6, pool_w=2 * HEAD)


def emit(nc, x_in, weights, const_in, bucket_in, par1_in, par2_in, table_in, rpb_in, out):
    with ExitStack() as ctx:
        def sb(name, shape, dtype=F32):
            return ctx.enter_context(nc.sbuf_tensor(name, shape, dtype))

        def sem(name):
            return ctx.enter_context(nc.semaphore(name))

        bias_scratch = nc.dram_tensor("bias_scratch", (12, P, SEQ + P), F32, kind="Internal").ap()


        xT = sb("xT", [P, NC, SEQ])
        mixT = sb("mixT", [P, NC, SEQ])
        opH = sb("opH", [P, NC, SEQ], F32R)
        opL = sb("opL", [P, NC, SEQ], F32R)
        wraw = sb("wraw", [P, SLOTS, PIECE])
        wH = sb("wH", [P, SLOTS, PIECE], F32R)
        wL = sb("wL", [P, SLOTS, PIECE], F32R)
        const = sb("const", [P, CONST_W])
        par1 = sb("par1", [P, PAR1_W])
        par2 = sb("par2", [P, PAR2_W])
        with ExitStack() as hidden_ctx:
            hidH = hidden_ctx.enter_context(nc.sbuf_tensor("hidH", [P, PART, SEQ], F32R))
            hidL = hidden_ctx.enter_context(nc.sbuf_tensor("hidL", [P, PART, SEQ], F32R))
        with ExitStack() as blocks_ctx:
            blocks_ctx.enter_context(nc.sbuf_tensor("below_blocks", [P, BLOCKS_AT], F32))
            blkH = blocks_ctx.enter_context(nc.sbuf_tensor("blkH", [P, CMP_LEN + 1, HEAD], F32R))
            blkL = blocks_ctx.enter_context(nc.sbuf_tensor("blkL", [P, CMP_LEN + 1, HEAD], F32R))
        big = sb("big", [P, 32 * SEQ])
        rows = sb("rows", [P, 2, SEQ])
        small = sb("small", [P, 1024])

        def c(name):
            return const[:, CONST[name][0]:CONST[name][1]]

        def p1(name):
            return par1[:, PAR1[name][0]:PAR1[name][1]]

        def p2(name):
            return par2[:, PAR2[name][0]:PAR2[name][1]]

        ident, ones = c("ident"), c("ones")
        space = big[:, :].rearrange("p (f s) -> p f s", s=SEQ)
        place = [0]

        def cut(n):
            place[0] += n
            assert place[0] <= 32 * SEQ
            return big[:, place[0] - n:place[0]]

        qT, kT, vT = cut(SEQ), cut(SEQ), cut(SEQ)
        v_nat = cut(SEQ).rearrange("p (t d) -> p t d", t=NT)
        side = cut(8 * SEQ).rearrange("p (i s) -> p i s", i=8)
        score_at = place[0]
        assert score_at == BLOCKS_AT
        score = cut(2 * SEQ).rearrange("p (b s) -> p b s", b=2)
        prob = cut(4 * SEQ).rearrange("p (b s) -> p b s", b=4)
        probT = cut(2 * SEQ).rearrange("p (b s) -> p b s", b=2)
        bias_at = place[0]
        pair_bias = cut(2 * NA_J * GRID_W).rearrange("p (h k) -> p h k", h=2)
        sel_bias = cut(2 * SEQ).rearrange("p (b s) -> p b s", b=2)
        vs_nat = cut(SEQ).rearrange("p (t d) -> p t d", t=NT)
        vw_nat = cut(SEQ).rearrange("p (t d) -> p t d", t=NT)
        blocks = cut(CMP_LEN * CMP_PAD).rearrange("p (l n) -> p l n", l=CMP_LEN)
        pcT = cut(SEQ)
        assert place[0] <= 32 * SEQ
        def flat2(a):
            return a[:, :, :].rearrange("p t d -> p (t d)")

        sb_width = P * NT * (NT + 1) // 2
        sb_z_buf = [big[:, score_at + h * sb_width:score_at + (h + 1) * sb_width] for h in range(2)]
        sb_t = [big[:, bias_at + h * sb_width:bias_at + (h + 1) * sb_width] for h in range(2)]

        def sb_unit(bufs, hh, t):
            at = P * t * (t + 1) // 2
            return bufs[hh][:, at:at + (t + 1) * P]

        df_probs = [(prob[:, 0, :], prob[:, 1, :]), (prob[:, 2, :], prob[:, 3, :]),
                    (sel_bias[:, 0, :], sel_bias[:, 1, :]), (flat2(vs_nat), flat2(vw_nat))]
        t5_nsa = side[:, 4:8, :]
        bucket = score[:, :, :].rearrange("p b s -> p (b s)")[0:N_BUCKETS + 1, 0:SEQ + P]
        vec = prob[:, :, :].rearrange("p b s -> p (b s)")[0:12, 0:SEQ + P]
        squares = space[:, 16:16 + NC, :]
        evac = space[:, 24:26, :]
        raw = space[:, 26:28, :]

        place2 = [0]

        def bit(n):
            place2[0] += n
            assert place2[0] <= 1024
            return small[:, place2[0] - n:place2[0]]

        negmax, denom, recip = bit(STATS), bit(STATS), bit(STATS)
        lam2, lam_one, lam_scale, lam_eps, lam_tmp, subln = bit(2), bit(1), bit(1), bit(1), bit(2), bit(1)
        gates = bit(NT * 12).rearrange("p (t g) -> p t g", t=NT)
        kcT = bit(CMP_PAD)
        imp = bit(NT * N_SLC).rearrange("p (t j) -> p t j", t=NT)
        rank = bit(NT * N_SLC).rearrange("p (t j) -> p t j", t=NT)
        sel_neg = bit(NT * N_SLC).rearrange("p (t j) -> p t j", t=NT)
        cmax, csum = bit(NT * HEADS), bit(NT * HEADS)
        eps_norm, eps_ln, one_col = bit(1), bit(1), bit(1)
        lam_prod = bit(2 * DIFF_HALF)
        gx = bit(4 * CMP_PAD).rearrange("p (g n) -> p g n", g=4)
        gt = bit(4 * CMP_PAD).rearrange("p (g n) -> p g n", g=4)
        h1v = sb("h1v", [P, 2, HEADS, CMP_PAD])
        vc_diag = sb("vc_diag", [P, GROUP])
        vc_pair = sb("vc_pair", [P, P])
        cmp_bias = sb("cmp_bias", [P, NT, HEADS, CMP_PAD])
        cmp_mask = sb("cmp_mask", [P, NT, HEADS, CMP_PAD])
        pc = sb("pc", [P, NT, HEADS, CMP_PAD])
        pcg = sb("pcg", [P, NT, HEADS, CMP_PAD])
        beats = score[:, 0, :].rearrange("p (b n) -> p b n", b=2)
        tab33 = sb("tab33", [N_BUCKETS + 1, 12])

        def bank(name):
            return ctx.enter_context(nc.psum_tensor(name, [P, SEQ], F32))

        acc = [bank("acc0"), bank("acc1")]
        scp = [bank("score0"), bank("score1")]
        trp = [bank("trans0"), bank("trans1")]
        outp, spare = bank("outp"), bank("spare")

        w_loaded = [sem(f"w_loaded{s}") for s in range(SLOTS)]
        pieces_done = sem("pieces_done")
        evacuated = [sem("evacuated0"), sem("evacuated1")]
        const_loaded, x_loaded, table_loaded = sem("const_loaded"), sem("x_loaded"), sem("table_loaded")
        par_loaded, rpb_loaded = sem("par_loaded"), sem("rpb_loaded")
        split_done = sem("split_done")
        op_raw, op_hi, op_lo, op_lo_pool = sem("op_raw"), sem("op_hi"), sem("op_lo"), sem("op_lo_pool")
        hid_ready, relu_ready = sem("hid_ready"), sem("relu_ready")
        bias_stored, t5_loaded, stored = sem("bias_stored"), sem("t5_loaded"), sem("stored")
        pe_end, act_end, dve_end, pool_end = sem("pe_end"), sem("act_end"), sem("dve_end"), sem("pool_end")
        x_turned, vec_ready, vec_copied, tab_set, zeroed = (sem("x_turned"), sem("vec_ready"), sem("vec_copied"),
                                                            sem("tab_set"), sem("zeroed"))
        squared, summed, rstd_ready = sem("squared"), sem("summed"), sem("rstd_ready")
        ln_summed, centred, ln_squared, ln_var, ln_rstd, ln_scaled = (
            sem("ln_summed"), sem("centred"), sem("ln_squared"), sem("ln_var"), sem("ln_rstd"), sem("ln_scaled"))
        lam_dots, lam_exps = sem("lam_dots"), sem("lam_exps")
        kv_ready = sem("kv_ready")
        v_turned, v_copied = sem("v_turned"), sem("v_copied")
        pair_ready = sem("pair_ready")
        bias_ready = sem("bias_ready")
        scores_ready, biased, exped, recip_ready, normed = (sem("scores_ready"), sem("biased"), sem("exped"),
                                                            sem("recip_ready"), sem("normed"))
        sel_ready = sem("sel_ready")
        transposed, pt_ready, pv_done = sem("transposed"), sem("pt_ready"), sem("pv_done")
        sb_scores, sb_z, sb_log, sb_arg, sb_prob = (sem("sb_scores"), sem("sb_z"), sem("sb_log"), sem("sb_arg"),
                                                    sem("sb_prob"))
        df_second, df_weight, df_sq, df_sum, df_rstd = (sem("df_second"), sem("df_weight"), sem("df_sq"),
                                                        sem("df_sum"), sem("df_rstd"))
        hid_out, hid_turned, low_cleared = sem("hid_out"), sem("hid_turned"), sem("low_cleared")
        ns_turned, ns_copied, blocks_ready, hid_copied, hid_sq, hid_poly, hid_exp, gelu_ready = (
            sem("ns_turned"), sem("ns_copied"), sem("blocks_ready"), sem("hid_copied"), sem("hid_sq"),
            sem("hid_poly"), sem("hid_exp"), sem("gelu_ready"))
        cmp_kv, cmp_copied, cmp_scores, cmp_shift, cmp_exp, pc_ready, pc_turned, pc_copied, imp_ready = (
            sem("cmp_kv"), sem("cmp_copied"), sem("cmp_scores"), sem("cmp_shift"), sem("cmp_exp"),
            sem("pc_ready"), sem("pc_turned"), sem("pc_copied"), sem("imp_ready"))
        gate_exp = sem("gate_exp")
        silu_ready = sem("silu_ready")
        pooled, pool_mm, pool_done = sem("pooled"), sem("pool_mm"), sem("pool_done")
        out_turned, out_copied = sem("out_turned"), sem("out_copied")

        def big_pad(n, wide):
            return prob[:, :, :].rearrange("p b s -> p (b s)")[:, n * wide:(n + 1) * wide]

        block = ctx.enter_context(nc.Block())

        def settle(eng, *waits):
            waits = [(s, eng.compute_val(value)) for s, value in waits]
            eng.wait_ge(const_loaded, 16)
            for s, value in waits:
                eng.wait_ge(s, value)

        def begin(eng, stage):
            settle(eng, *[(end, stage) for end in (pe_end, act_end, dve_end, pool_end)])

        def finish(eng, end):
            eng.drain().then_inc(end, 1)

        @block.sync
        def _(sp):
            sp.dma_start(const[:, :], const_in).then_inc(const_loaded, 16)
            sp.dma_start(space[:, 0:2 * NT, :].rearrange("p (t h) s -> p t (h s)", t=NT),
                         x_in.rearrange("(t p) d -> p t d", p=P)).then_inc(x_loaded, 16)

            def piece(offset, width, slot, split):
                if split is not None:
                    sp.wait_ge(split_done, split)
                sp.dma_start(wraw[:, slot, 0:width], bass.AP(weights.tensor, offset, [[width, P], [1, width]])
                             ).then_inc(w_loaded[slot], 16)

            size = P * PIECE
            for s in range(SLOTS):
                piece(s * size, PIECE, s, None)
            with sp.Fori(1, DEPTH * ROUNDS1) as r:
                for s in range(SLOTS):
                    piece(r * (SLOTS * size) + s * size, PIECE, s, r * SLOTS + s - SLOTS + 1)
            ffn = []
            for n, r_gu in zip(PARTS2, R_GU):
                ffn += [(r_gu, PIECE), (R_DOWN, n * P)]
            runs = ffn + [(1 + NA_PAIRS + R_OUT, PIECE)] + ffn
            layer_size = sum(k * SLOTS * P * w for k, w in runs)
            with sp.Fori(0, DEPTH) as layer:
                at, rounds = DEPTH * ROUNDS1 * SLOTS * size, ROUND_B2
                for k, w in runs:
                    with sp.Fori(0, k) as r:
                        for s in range(SLOTS):
                            piece(layer * layer_size + r * (SLOTS * P * w) + (at + s * P * w), w, s,
                                  layer * (ROUNDS2 * SLOTS) + r * SLOTS + ((rounds - 1) * SLOTS + s + 1))
                    at += k * SLOTS * P * w
                    rounds += k
            for s in range(SLOTS):
                last = DEPTH * (ROUNDS1 * SLOTS * size + layer_size)
                piece(last + s * size, PIECE, s, (ROUND_B2 + DEPTH * ROUNDS2 - 1) * SLOTS + s + 1)

        @block.tensor
        def _(pe):
            def product(slot, rnd, accum, n=NC, hi=opH, lo=opL, ready=None):
                pe.wait_ge(split_done, rnd * SLOTS + slot + 1)
                for k in range(n):
                    if ready is not None:
                        pe.wait_ge(*ready(k))
                    w = slice(k * P, (k + 1) * P)
                    pe.matmul(accum[:, :], wH[:, slot, w], hi[:, k, :], start=k == 0, stop=False)
                    pe.matmul(accum[:, :], wH[:, slot, w], lo[:, k, :], start=False, stop=False)
                    mm = pe.matmul(accum[:, :], wL[:, slot, w], hi[:, k, :], start=False, stop=k == n - 1)
                mm.then_inc(pieces_done, 1)

            def four(rnd, gp, n=NC, hi=opH, lo=opL, ready=None):
                for j in range(SLOTS):
                    pe.wait_ge(evacuated[j % 2], gp + j // 2)
                    product(j, rnd, acc[j % 2], n, hi, lo, ready if j == 0 else None)

            def down(rounds, gps, hids, n):
                for r in range(R_DOWN):
                    four(r + rounds, r * 2 + gps, n, hidH, hidL,
                         (lambda k: (hid_ready, hids + k + 1)) if r == 0 else None)

            def op_split(n):
                settle(pe, (op_lo, n * (NC // 2) + NC // 2), (op_lo_pool, n * (NC // 2) + NC // 2))

            def norm(n):
                for k in range(NC):
                    pe.wait_ge(squared, n * NC + k + 1)
                    mm = pe.matmul(scp[0][:, :], ones, squares[:, k, :], start=k == 0, stop=k == NC - 1)
                mm.then_inc(summed, 1)
                finish(pe, pe_end)

            def layer_norm(n):
                for k in range(NC):
                    mm = pe.matmul(scp[0][:, :], ones, xT[:, k, :], start=k == 0, stop=k == NC - 1)
                mm.then_inc(ln_summed, 1)
                for k in range(NC):
                    pe.wait_ge(ln_squared, n * NC + k + 1)
                    mm = pe.matmul(scp[1][:, :], ones, squares[:, k, :], start=k == 0, stop=k == NC - 1)
                mm.then_inc(ln_var, 1)
                finish(pe, pe_end)

            def turn_values(it):
                pe.wait_ge(kv_ready, it + 1)
                for t in range(NT):
                    mm = pe.transpose(trp[0][:, t * P:(t + 1) * P], vT[:, t * P:(t + 1) * P], ident)
                mm.then_inc(v_turned, 1)

            def turn_probs(m, width, tb):
                if m >= 2:
                    pe.wait_ge(pt_ready, tb + m - 1)
                for j in range(width // P):
                    mm = pe.transpose(trp[m % 2][:, j * P:(j + 1) * P], m_prob[0][:, j * P:(j + 1) * P], ident)
                mm.then_inc(transposed, 1)

            m_prob = [None]

            def apply_values(m, tb, hh, t, width, values, first=True, last=True, extra=None):
                pe.wait_ge(pt_ready, tb + m + 1)
                o = outp[HEAD * hh:HEAD * (hh + 1), t * P:(t + 1) * P]
                if extra is not None:
                    pe.matmul(o, extra[0], extra[1], start=True, stop=False)
                n = width // P
                for j in range(n):
                    mm = pe.matmul(o, values(j), probT[:, m % 2, j * P:(j + 1) * P],
                                   start=first and extra is None and j == 0, stop=last and j == n - 1)
                mm.then_inc(pv_done, 1)

            def softmax_maps(mb, nb, tb, maps):
                n = len(maps)
                for i in range(n + 3):
                    if i < n:
                        q, k, width = maps[i][:3]
                        if i >= 2:
                            pe.wait_ge(biased, mb + i - 1)
                        pe.matmul(scp[i % 2][:, 0:width], q, k, start=True, stop=True).then_inc(scores_ready, 1)
                    if 2 <= i < n + 2:
                        pe.wait_ge(normed, nb + i - 1)
                        m_prob[0] = prob[:, (i - 2) % 4, :]
                        turn_probs(i - 2, maps[i - 2][2], tb)
                    if i >= 3:
                        _, _, width, args = maps[i - 3]
                        apply_values(i - 3, tb, width=width, **args)

            def half_of(a, hh):
                return a[HEAD * hh:HEAD * (hh + 1)]

            def q_tile(hh, t):
                return half_of(qT, hh)[:, t * P:(t + 1) * P]

            def v_head(hh):
                return lambda j: v_nat[:, j, HEAD * hh:HEAD * (hh + 1)]

            def stick_breaking(layer, pair):
                it = layer * 6 + pair
                four(layer * ROUNDS1 + pair + ROUND_SB, layer * GPS1 + pair * 2 + GP_SETUP)
                turn_values(it)
                ub, tb = layer * (2 * U) + pair * U, layer * TRS1 + pair * U + TR_SB
                units = [(hh, t) for hh in range(2) for t in range(NT)]
                pe.wait_ge(v_copied, it + 1)
                for i, (hh, t) in enumerate(units):
                    if i >= 2:
                        pe.wait_ge(sb_z, ub + i - 1)
                    pe.matmul(scp[i % 2][:, 0:(t + 1) * P], q_tile(hh, t), half_of(kT, hh)[:, 0:(t + 1) * P],
                              start=True, stop=True).then_inc(sb_scores, 1)
                for i in range(U + 1):
                    if i < U:
                        hh, t = units[i]
                        if t == 0:
                            pe.wait_ge(sb_prob, layer * 4 + pair * 2 + hh + 1)
                        m_prob[0] = sb_unit(sb_t, hh, t)
                        turn_probs(i, (t + 1) * P, tb)
                    if i >= 1:
                        hh, t = units[i - 1]
                        apply_values(i - 1, tb, hh, t, (t + 1) * P, v_head(hh))
                finish(pe, pe_end)

            def moba(layer, pair):
                it = layer * 6 + pair + 2
                four(layer * ROUNDS1 + pair + ROUND_MB, layer * GPS1 + pair * 2 + (GP_SETUP + 2 * R_ATT))
                turn_values(it)
                pe.wait_ge(v_copied, it + 1)
                softmax_maps(layer * MAPS1 + pair * U + MAPS_MB, layer * NORMS1 + pair * U + NORM_MB,
                             layer * TRS1 + pair * U + TR_MB,
                             [(q_tile(hh, t), half_of(kT, hh)[:, 0:(t + 1) * P], (t + 1) * P,
                               dict(hh=hh, t=t, values=v_head(hh))) for hh in range(2) for t in range(NT)])
                finish(pe, pe_end)

            def differential(layer, pair):
                it = layer * 6 + pair + 4
                four(layer * ROUNDS1 + pair + ROUND_DF, layer * GPS1 + pair * 2 + (GP_SETUP + 4 * R_ATT))
                turn_values(it)
                pe.wait_ge(v_copied, it + 1)
                mb = layer * MAPS1 + pair * (2 * U) + MAPS_DF
                tb = layer * TRS1 + pair * U + TR_DF
                ub = layer * (2 * U) + pair * U
                units = [(hh, t) for hh in range(2) for t in range(NT)]
                for i in range(U + 3):
                    if i < U:
                        hh, t = units[i]
                        for half in range(2):
                            m = 2 * i + half
                            at = HEAD * hh + DIFF_HALF * half
                            if m >= 2:
                                pe.wait_ge(biased, mb + m - 1)
                            pe.matmul(scp[half][:, 0:(t + 1) * P], qT[at:at + DIFF_HALF, t * P:(t + 1) * P],
                                      kT[at:at + DIFF_HALF, 0:(t + 1) * P], start=True, stop=True
                                      ).then_inc(scores_ready, 1)
                    if 2 <= i < U + 2:
                        pe.wait_ge(df_weight, ub + i - 1)
                        m_prob[0] = df_probs[(i - 2) % 4][0]
                        turn_probs(i - 2, (units[i - 2][1] + 1) * P, tb)
                    if i >= 3:
                        hh, t = units[i - 3]
                        apply_values(i - 3, tb, hh, t, (t + 1) * P, v_head(hh))
                pe.wait_ge(df_sq, layer * PAIRS + pair + 1)
                pe.matmul(spare[:, :], c("head_ones"), score[:, 0, :], start=True, stop=True).then_inc(df_sum, 1)
                finish(pe, pe_end)

            def nsa_select(layer):
                rnd = layer * ROUNDS1 + ROUND_CMP
                for i, to in ((1, acc[0]), (2, acc[1]), (3, spare)):
                    for t in range(NT):
                        mm = pe.transpose(to[:, t * P:(t + 1) * P], side[:, i, t * P:(t + 1) * P], ident)
                    mm.then_inc(ns_turned, 1)
                pe.wait_ge(blocks_ready, layer + 1)
                per = PIECE // CMP_HIDDEN
                flatH, flatL = (b[:, :, :].rearrange("p l n -> p (l n)") for b in (blkH, blkL))
                for n in range(R_CMP * SLOTS):
                    s = n % SLOTS
                    pe.wait_ge(split_done, (rnd + n // SLOTS) * SLOTS + s + 1)
                    for k in range(per):
                        l = n * per + k
                        w = slice(k * CMP_HIDDEN, (k + 1) * CMP_HIDDEN)
                        b = slice(l * HEAD, l * HEAD + P)
                        to = scp[0][:, 0:CMP_HIDDEN]
                        pe.matmul(to, flatH[:, b], wH[:, s, w], start=l == 0, stop=False)
                        pe.matmul(to, flatH[:, b], wL[:, s, w], start=False, stop=False)
                        mm = pe.matmul(to, flatL[:, b], wH[:, s, w], start=False, stop=l == CMP_LEN - 1)
                    mm.then_inc(pieces_done, 1)
                settle(pe, (hid_out, layer + 1))
                for h in range(2):
                    mm = pe.transpose(scp[1][:, h * HEAD:(h + 1) * HEAD], rows[0:HEAD, 1, h * P:(h + 1) * P],
                                      ident[0:HEAD, 0:HEAD])
                mm.then_inc(hid_turned, 1)
                pe.wait_ge(gelu_ready, layer * 2 + 2)
                for half in range(2):
                    for h in range(2):
                        pe.matmul(half_of(scp[0], half)[:, 0:N_CMP], p1("w2k")[:, h * HEAD:(h + 1) * HEAD],
                                  gx[:, h, 0:N_CMP], start=h == 0, stop=h == 1)
                for h in range(2):
                    mm = pe.matmul(scp[1][:, 0:HEAD], h1v[:, h, :, :].rearrange("p a b -> p (a b)"),
                                   p1("w2v")[:, h * HEAD:(h + 1) * HEAD], start=h == 0, stop=h == 1)
                mm.then_inc(cmp_kv, 1)
                pe.wait_ge(cmp_copied, layer + 1)
                for t in range(NT):
                    for h in range(HEADS):
                        at = (t * PAIRS + h // 2) * CMP_PAD
                        mm = pe.matmul(trp[h % 2][:, at:at + N_CMP],
                                       half_of(side[:, 4 + h // 2, :], h % 2)[:, t * P:(t + 1) * P],
                                       half_of(kcT, h % 2)[:, 0:N_CMP], start=True, stop=True)
                mm.then_inc(cmp_scores, 1)
                for n, src, to in ((0, pc, trp[1]), (1, pcg, trp[0])):
                    pe.wait_ge(pc_ready, layer * 2 + n + 1)
                    for t in range(NT):
                        mm = pe.transpose(to[:, t * P:(t + 1) * P], src[:, t, :, :].rearrange("p a b -> p (a b)"),
                                          ident)
                    mm.then_inc(pc_turned, 1)
                    if n == 0:
                        pe.wait_ge(pc_copied, layer * 2 + 1)
                        for t in range(NT):
                            mm = pe.matmul(scp[0][:, t * N_SLC:(t + 1) * N_SLC], pcT[:, t * P:(t + 1) * P],
                                           c("cover"), start=True, stop=True)
                        mm.then_inc(imp_ready, 1)
                finish(pe, pe_end)

            def nsa_pair(layer, pair):
                pe.wait_ge(pair_ready, layer * PAIRS + pair + 1)
                maps = []
                for hh in range(2):
                    for t in range(NT):
                        cols = slice(0, (t + 1) * P)
                        maps.append((q_tile(hh, t), half_of(side[:, 1, :], hh)[:, cols], (t + 1) * P,
                                     dict(hh=hh, t=t, values=lambda j: vs_nat[:, j, HEAD:2 * HEAD], last=False,
                                          extra=(vc_pair[:, HEAD * hh:HEAD * (hh + 1)],
                                                 pcT[:, t * P:(t + 1) * P]))))
                        maps.append((q_tile(hh, t), half_of(side[:, 2, :], hh)[:, cols], (t + 1) * P,
                                     dict(hh=hh, t=t, values=lambda j: vw_nat[:, j, HEAD:2 * HEAD], first=False)))
                softmax_maps(layer * MAPS1 + pair * (2 * U) + MAPS_NS, layer * NORMS1 + pair * (2 * U) + NORM_NS,
                             layer * TRS1 + pair * (2 * U) + TR_NS, maps)
                finish(pe, pe_end)

            def neighbourhood(layer, pair):
                it = layer * NA_PAIRS + pair + DEPTH * 6
                four(layer * ROUNDS2 + pair + (ROUND_B2 + ROUND_NA), layer * GPS2 + pair * 2 + (GP_B2 + GP_NA))
                turn_values(it)
                pe.wait_ge(v_copied, it + 1)
                softmax_maps(layer * (4 * U) + pair * U + DEPTH * MAPS1, layer * (4 * U) + pair * U + DEPTH * NORMS1,
                             layer * (4 * U) + pair * U + DEPTH * TRS1,
                             [(q_tile(hh, t), half_of(kT, hh), SEQ, dict(hh=hh, t=t, values=v_head(hh)))
                              for hh in range(2) for t in range(NT)])
                finish(pe, pe_end)

            def ffn(stage, rounds, gps, hids):
                begin(pe, stage)
                for r_gu, n in zip(R_GU, PARTS2):
                    with pe.Fori(0, r_gu) as r:
                        four(r + rounds, r * 2 + gps)
                    down(rounds + r_gu, gps + n, hids, n)
                    rounds, gps, hids = rounds + r_gu + R_DOWN, gps + n + NC // 2, hids + n
                finish(pe, pe_end)

            pe.wait_ge(const_loaded, 16)
            pe.wait_ge(x_loaded, 16)
            for k in range(NC):
                if k >= 2:
                    pe.wait_ge(evacuated[k % 2], k // 2)
                for t in range(NT):
                    at = t * D_MODEL + k * P
                    mm = pe.transpose(acc[k % 2][:, t * P:(t + 1) * P], big[:, at:at + P], ident)
                mm.then_inc(x_turned, 1)
            pe.wait_ge(table_loaded, 32)
            pe.matmul(scp[0][0:12, 0:SEQ], tab33[:, :], bucket[:, 0:SEQ], start=True, stop=True)
            pe.matmul(scp[1][0:12, 0:P], tab33[:, :], bucket[:, SEQ:SEQ + P], start=True, stop=True
                      ).then_inc(vec_ready, 1)
            finish(pe, pe_end)

            with pe.Fori(0, DEPTH) as layer:
                stage = layer * STAGES1 + 1
                begin(pe, stage + ST_NORM)
                norm(layer * 2)
                with pe.Fori(0, PAIRS) as pair:
                    begin(pe, stage + pair + ST_SB)
                    stick_breaking(layer, pair)
                with pe.Fori(0, PAIRS) as pair:
                    begin(pe, stage + pair + ST_MB)
                    moba(layer, pair)
                with pe.Fori(0, PAIRS) as pair:
                    begin(pe, stage + pair + ST_DF)
                    differential(layer, pair)
                begin(pe, stage + ST_NSA)
                nsa_select(layer)
                with pe.Fori(0, PAIRS) as pair:
                    begin(pe, stage + pair + ST_NSP)
                    nsa_pair(layer, pair)
                begin(pe, stage + ST_OUT)
                op_split(layer * SPLITS1 + 1)
                with pe.Fori(0, R_OUT) as r:
                    four(layer * ROUNDS1 + r + ROUND_OUT, layer * GPS1 + r * 2 + (GP_SETUP + GP_OUT))
                finish(pe, pe_end)
                begin(pe, stage + ST_NORM2)
                norm(layer * 2 + 1)
                begin(pe, stage + ST_MLP)
                with pe.Fori(0, PARTS1) as part:
                    rounds = layer * ROUNDS1 + part * R_PART1 + ROUND_MLP
                    gps = layer * GPS1 + part * GP_PART1 + (GP_SETUP + GP_MLP)
                    with pe.Fori(0, R_UP) as r:
                        four(r + rounds, r * 2 + gps)
                    down(rounds + R_UP, gps + PART // 2, layer * (PARTS1 * PART) + part * PART, PART)
                finish(pe, pe_end)
            begin(pe, ST_FINAL)
            norm(2 * DEPTH)
            with pe.Fori(0, DEPTH) as layer:
                stage = layer * STAGES2 + ST_B2
                rounds, gps = layer * ROUNDS2 + ROUND_B2, layer * GPS2 + GP_B2
                hids = layer * (2 * sum(PARTS2)) + DEPTH * PARTS1 * PART
                ffn(stage + ST_FFN1, rounds, gps, hids)
                begin(pe, stage + ST_LN0)
                layer_norm(layer * 3)
                begin(pe, stage + ST_PROJ)
                four(rounds + ROUND_PROJ, gps + GP_PROJ)
                finish(pe, pe_end)
                with pe.Fori(0, NA_PAIRS) as pair:
                    begin(pe, stage + pair + ST_NA)
                    neighbourhood(layer, pair)
                begin(pe, stage + ST_POOL)
                for i in range(2):
                    settle(pe, (pooled, layer * 2 + i + 1))
                    for g in range(2):
                        mm = pe.matmul(half_of(scp[i], g)[:, :], half_of(p2("pool_w"), g)[:, i * HEAD:(i + 1) * HEAD],
                                       half_of(score[:, i, :], g), start=True, stop=True)
                    mm.then_inc(pool_mm, 1)
                finish(pe, pe_end)
                begin(pe, stage + ST_OUT2)
                op_split(layer * SPLITS2 + (SPLIT_B2 + 1))
                with pe.Fori(0, R_OUT) as r:
                    four(rounds + r + ROUND_OUT2, gps + r * 2 + GP_OUT2)
                finish(pe, pe_end)
                begin(pe, stage + ST_LN1)
                layer_norm(layer * 3 + 1)
                ffn(stage + ST_FFN2, rounds + ROUND_FFN2, gps + GP_FFN2, hids + sum(PARTS2))
                begin(pe, stage + ST_LN2)
                layer_norm(layer * 3 + 2)
            begin(pe, ST_END)
            for n in range(2 * NT):
                t, half = n // 2, n % 2
                if n >= 2:
                    pe.wait_ge(out_copied, n - 1)
                for k in range(NC // 2):
                    mm = pe.transpose(acc[n % 2][:, k * P:(k + 1) * P],
                                      xT[:, half * NC // 2 + k, t * P:(t + 1) * P], ident)
                mm.then_inc(out_turned, 1)

        @block.scalar
        def _(act):
            def copy(to, src, scale=1.0):
                return act.activation(to, src, ACT.Copy, scale=scale)

            def power(rs, src, scale, eps, n_ready):
                act.activation(rs, src, ACT.Ln, scale=scale, bias=eps)
                act.drain()
                act.activation(rs, rs, ACT.Exp, scale=-0.5).then_inc(n_ready, 1)

            def op_high(src, k, n=None):
                if n is not None:
                    act.wait_ge(op_raw, n * NC + k + 1)
                copy(opH[:, k, :], src[:, k, :]).then_inc(op_hi, 1)

            def norm(n):
                for k in range(NC):
                    act.activation(squares[:, k, :], xT[:, k, :], ACT.Square).then_inc(squared, 1)
                act.wait_ge(summed, n + 1)
                power(rows[:, 0, :], scp[0][:, :], 1.0 / D_MODEL, eps_norm, rstd_ready)

            def norm_high(n, to):
                for k in range(NC):
                    op_high(to, k, n)
                finish(act, act_end)

            def layer_norm(n):
                for k in range(NC):
                    act.wait_ge(centred, n * NC + k + 1)
                    act.activation(squares[:, k, :], xT[:, k, :], ACT.Square).then_inc(ln_squared, 1)
                act.wait_ge(ln_var, n + 1)
                power(rows[:, 0, :], scp[1][:, :], 1.0 / D_MODEL, eps_ln, ln_rstd)

            def shift(n, which):
                for k in range(NC):
                    act.wait_ge(ln_scaled, n * NC + k + 1)
                    act.activation(xT[:, k, :], xT[:, k, :], ACT.Identity,
                                   bias=p2("ln_b")[:, which * NC + k:which * NC + k + 1])
                    act.drain()
                    op_high(xT, k)
                finish(act, act_end)

            def project(done, scale, to_side, side_scale, it):
                for j, (to, s) in enumerate(((qT, scale), (kT, 1.0), (vT, 1.0), (None, side_scale))):
                    settle(act, (pieces_done, done + j + 1))
                    if to is None:
                        copy(side[:, to_side, :].rearrange("p a s -> p (a s)"), acc[j % 2][:, :], s
                             ).then_inc(evacuated[j % 2], 1)
                    else:
                        copy(to, acc[j % 2][:, :], s).then_inc(evacuated[j % 2], 1)
                    if j == 2:
                        act.drain().then_inc(kv_ready, 1)
                act.wait_ge(v_turned, it + 1)
                copy(v_nat[:, :, :].rearrange("p t d -> p (t d)"), trp[0][:, :]).then_inc(v_copied, 1)

            def probs_out(m, width, tb):
                if m >= 2:
                    act.wait_ge(pv_done, tb + m - 1)
                act.wait_ge(transposed, tb + m + 1)
                copy(probT[:, m % 2, 0:width], trp[m % 2][:, 0:width]).then_inc(pt_ready, 1)

            def softmax_exp(m, width, mb, to):
                act.wait_ge(biased, mb + m + 1)
                act.activation(to[:, 0:width], score[:, m % 2, 0:width], ACT.Exp,
                               bias=negmax[:, m % STATS:m % STATS + 1], scale=-1.0,
                               accum_out=denom[:, m % STATS:m % STATS + 1]).then_inc(exped, 1)

            def softmax_maps(mb, tb, widths):
                n = len(widths)
                for i in range(n + 2):
                    if i < n:
                        if i >= 4:
                            act.wait_ge(transposed, tb + i - 3)
                        softmax_exp(i, widths[i], mb, prob[:, i % 4, :])
                    if i >= 2:
                        probs_out(i - 2, widths[i - 2], tb)

            causal = [(t + 1) * P for hh in range(2) for t in range(NT)]

            def stick_breaking(layer, pair):
                project(layer * (ROUNDS1 * SLOTS) + pair * SLOTS + ROUND_SB * SLOTS, HEAD ** -0.5,
                        bass.ds(pair, 1), 1.0, layer * 6 + pair)
                ub, tb = layer * (2 * U) + pair * U, layer * TRS1 + pair * U + TR_SB
                heads = layer * 4 + pair * 2
                for hh in range(2):
                    act.wait_ge(sb_z, ub + (hh + 1) * NT)
                    act.activation(sb_t[hh], sb_z_buf[hh], ACT.Abs)
                    act.drain()
                    act.activation(sb_t[hh], sb_t[hh], ACT.Exp, scale=-1.0)
                act.drain()
                for hh in range(2):
                    act.activation(sb_t[hh], sb_t[hh], ACT.Ln, bias=one_col).then_inc(sb_log, 1)

                def weights_of(hh):
                    act.wait_ge(sb_arg, heads + hh + 1)
                    act.activation(sb_t[hh], sb_t[hh], ACT.Exp).then_inc(sb_prob, 1)

                weights_of(0)
                for i in range(U):
                    probs_out(i, causal[i], tb)
                    if i == 1:
                        weights_of(1)
                finish(act, act_end)

            def moba(layer, pair):
                project(layer * (ROUNDS1 * SLOTS) + pair * SLOTS + ROUND_MB * SLOTS, HEAD ** -0.5,
                        bass.ds(pair + 2, 1), 1.0, layer * 6 + pair + 2)
                softmax_maps(layer * MAPS1 + pair * U + MAPS_MB, layer * TRS1 + pair * U + TR_MB, causal)
                finish(act, act_end)

            def differential(layer, pair):
                project(layer * (ROUNDS1 * SLOTS) + pair * SLOTS + ROUND_DF * SLOTS, DIFF_HALF ** -0.5,
                        bass.ds(pair + 4, 1), HEAD ** -0.5, layer * 6 + pair + 4)
                mb = layer * MAPS1 + pair * (2 * U) + MAPS_DF
                tb = layer * TRS1 + pair * U + TR_DF
                for i in range(U + 2):
                    if i < U:
                        for half in range(2):
                            if i >= 4:
                                act.wait_ge(transposed, tb + i - 3)
                            softmax_exp(2 * i + half, causal[i], mb, df_probs[i % 4][half])
                    if i >= 2:
                        probs_out(i - 2, causal[i - 2], tb)
                n = layer * PAIRS + pair
                act.wait_ge(pv_done, tb + U)
                act.activation(score[:, 0, :], outp[:, :], ACT.Square).then_inc(df_sq, 1)
                act.wait_ge(df_sum, n + 1)
                power(rows[:, 1, :], spare[:, :], 1.0 / HEAD, lam_eps, df_rstd)
                finish(act, act_end)

            def nsa_select(layer):
                act.wait_ge(ns_turned, layer * 3 + 1)
                copy(flat2(vs_nat), acc[0][:, :])
                copy(side[HEAD:P, 1, :], side[0:HEAD, 1, :])
                act.wait_ge(ns_turned, layer * 3 + 2)
                copy(flat2(vw_nat), acc[1][:, :])
                copy(side[HEAD:P, 2, :], side[0:HEAD, 2, :])
                act.wait_ge(ns_turned, layer * 3 + 3)
                act.activation(gates, spare[:, :].rearrange("p (t g) -> p t g", t=NT)[:, :, 0:12], ACT.Exp,
                               scale=-1.0).then_inc(gate_exp, 1)
                act.wait_ge(pieces_done, layer * (ROUNDS1 * SLOTS) + (ROUND_CMP + R_CMP) * SLOTS)
                copy(rows[0:HEAD, 1, 0:CMP_HIDDEN], scp[0][0:HEAD, 0:CMP_HIDDEN]).then_inc(hid_out, 1)
                act.wait_ge(hid_turned, layer + 1)
                for kv in range(2):
                    copy(gx[:, 2 * kv:2 * kv + 2, :],
                         scp[1][:, 0:2 * HEAD].rearrange("p (h k n) -> p h k n", h=2, k=2)[:, :, kv, :])
                act.drain().then_inc(hid_copied, 1)
                act.activation(gt[:, :, 0:N_CMP], gx[:, :, 0:N_CMP], ACT.Square).then_inc(hid_sq, 1)
                act.wait_ge(hid_poly, layer + 1)
                act.activation(gt[:, :, 0:N_CMP], gt[:, :, 0:N_CMP], ACT.Exp,
                               scale=-2.0 * math.sqrt(2.0 / math.pi)).then_inc(hid_exp, 1)
                act.wait_ge(cmp_kv, layer + 1)
                copy(kcT[:, 0:N_CMP], scp[0][:, 0:N_CMP])
                for h in range(HEADS):
                    at = slice(h * CMP_PAD, (h + 1) * CMP_PAD)
                    copy(vc_diag[at, h * HEAD:(h + 1) * HEAD], scp[1][at, 0:HEAD])
                act.drain().then_inc(cmp_copied, 1)
                act.wait_ge(cmp_shift, layer + 1)
                act.activation(pc[:, :, :, 0:N_CMP].rearrange("p t h n -> p (t h) n"),
                               pcg[:, :, :, 0:N_CMP].rearrange("p t h n -> p (t h) n"), ACT.Exp
                               ).then_inc(cmp_exp, 1)
                for n, src in enumerate((trp[1], trp[0])):
                    act.wait_ge(pc_turned, layer * 2 + n + 1)
                    if n == 1:
                        act.wait_ge(imp_ready, layer + 1)
                    copy(pcT, src[:, :]).then_inc(pc_copied, 1)
                finish(act, act_end)

            def nsa_pair(layer, pair):
                softmax_maps(layer * MAPS1 + pair * (2 * U) + MAPS_NS, layer * TRS1 + pair * (2 * U) + TR_NS,
                             [w for w in causal for _ in range(2)])
                finish(act, act_end)

            def neighbourhood(layer, pair):
                project(layer * (ROUNDS2 * SLOTS) + pair * SLOTS + (ROUND_B2 + ROUND_NA) * SLOTS, HEAD ** -0.5,
                        bass.ds(pair, 1), 1.0, layer * NA_PAIRS + pair + DEPTH * 6)
                softmax_maps(layer * (4 * U) + pair * U + DEPTH * MAPS1, layer * (4 * U) + pair * U + DEPTH * TRS1,
                             [SEQ] * U)
                finish(act, act_end)

            def ffn(stage, rounds, count):
                begin(act, stage)
                for r_gu, n in zip(R_GU, PARTS2):
                    with act.Fori(0, r_gu) as r:
                        for j in range(2):
                            settle(act, (pieces_done, r * SLOTS + rounds * SLOTS + 2 * j + 1),
                                   *[(evacuated[1], r * 2 + count)][j:])
                            act.activation(evac[:, j, :], acc[0][:, :], ACT.Silu).then_inc(evacuated[0], 1)
                            act.drain().then_inc(silu_ready, 1)
                    rounds, count = rounds + r_gu + R_DOWN, count + n + NC // 2
                finish(act, act_end)

            act.dma_start(bucket, bucket_in).then_inc(table_loaded, 16)
            act.dma_start(tab33[0:N_BUCKETS, :], table_in).then_inc(table_loaded, 16)
            act.wait_ge(const_loaded, 16)
            act.wait_ge(zeroed, 1)
            copy(tab33[N_BUCKETS:N_BUCKETS + 1, :], c("neg_rows")[N_BUCKETS:N_BUCKETS + 1, :]).then_inc(tab_set, 1)
            for k in range(0, NC, 2):
                act.wait_ge(x_turned, k + 1)
                copy(xT[:, k, :], acc[0][:, :]).then_inc(evacuated[0], 1)
            act.wait_ge(vec_ready, 1)
            copy(vec[:, 0:SEQ], scp[0][0:12, 0:SEQ])
            copy(vec[:, SEQ:SEQ + P], scp[1][0:12, 0:P])
            act.drain().then_inc(vec_copied, 1)
            act.wait_ge(vec_copied, 1)
            act.dma_start(bias_scratch, vec.unsqueeze(1).to_broadcast([12, P, SEQ + P])).then_inc(bias_stored, 16)
            act.wait_ge(bias_stored, 16)

            def load_t5(to, head, heads):
                act.dma_start(to, bass.AP(bias_scratch.tensor, head * (P * (SEQ + P)) + (P - 1),
                                          [[SEQ + P - 1, P], [P * (SEQ + P), heads], [1, SEQ]])
                              ).then_inc(t5_loaded, 16)

            act.dma_start(t5_nsa, bass.AP(bias_scratch.tensor, HEADS * P * (SEQ + P) + P - 1,
                                          [[SEQ + P - 1, P], [P * (SEQ + P), HEADS], [1, SEQ]])
                          ).then_inc(t5_loaded, 16)
            finish(act, act_end)

            with act.Fori(0, DEPTH) as layer:
                stage = layer * STAGES1 + 1
                begin(act, stage + ST_NORM)
                act.dma_start(par1[:, :], par1_in[bass.ds(layer, 1)].rearrange("o p n -> p (o n)")
                              ).then_inc(par_loaded, 16)
                norm(layer * 2)
                act.wait_ge(lam_dots, layer + 1)
                act.activation(lam2, lam_tmp, ACT.Exp).then_inc(lam_exps, 1)
                norm_high(layer * 2, mixT)
                with act.Fori(0, PAIRS) as pair:
                    begin(act, stage + pair + ST_SB)
                    stick_breaking(layer, pair)
                with act.Fori(0, PAIRS) as pair:
                    begin(act, stage + pair + ST_MB)
                    load_t5(pair_bias[:, :, 0:SEQ], pair * 2, 2)
                    moba(layer, pair)
                with act.Fori(0, PAIRS) as pair:
                    begin(act, stage + pair + ST_DF)
                    load_t5(pair_bias[:, :, 0:SEQ], pair * 2 + 2 * HEADS, 2)
                    differential(layer, pair)
                begin(act, stage + ST_NSA)
                nsa_select(layer)
                with act.Fori(0, PAIRS) as pair:
                    begin(act, stage + pair + ST_NSP)
                    load_t5(pair_bias[:, :, 0:SEQ], pair * 2 + HEADS, 2)
                    nsa_pair(layer, pair)
                begin(act, stage + ST_OUT)
                for k in range(NC):
                    op_high(mixT, k)
                finish(act, act_end)
                begin(act, stage + ST_NORM2)
                norm(layer * 2 + 1)
                norm_high(layer * 2 + 1, mixT)
                begin(act, stage + ST_MLP)
                with act.Fori(0, PARTS1) as part:
                    done = layer * (ROUNDS1 * SLOTS) + part * (R_PART1 * SLOTS) + ROUND_MLP * SLOTS
                    tiles = layer * (PARTS1 * PART) + part * PART
                    for j in range(PART):
                        waits = [(pieces_done, done + j + 1)]
                        if j >= 2:
                            waits.append((hid_ready, tiles + j - 1))
                        settle(act, *waits)
                        act.activation(evac[:, j % 2, :], acc[j % 2][:, :], ACT.Relu).then_inc(evacuated[j % 2], 1)
                        act.drain()
                        act.activation(hidH[:, j, :], evac[:, j % 2, :], ACT.Square).then_inc(relu_ready, 1)
                finish(act, act_end)
            begin(act, ST_FINAL)
            norm(2 * DEPTH)
            norm_high(2 * DEPTH, xT)
            with act.Fori(0, DEPTH) as layer:
                stage = layer * STAGES2 + ST_B2
                begin(act, stage + ST_FFN1)
                act.dma_start(par2[:, :], par2_in[bass.ds(layer, 1)].rearrange("o p n -> p (o n)")
                              ).then_inc(par_loaded, 16)
                ffn(stage + ST_FFN1, layer * ROUNDS2 + ROUND_B2, layer * GPS2 + GP_B2)
                begin(act, stage + ST_LN0)
                layer_norm(layer * 3)
                shift(layer * 3, 0)
                begin(act, stage + ST_PROJ)
                for j in range(SLOTS):
                    act.wait_ge(pieces_done, layer * (ROUNDS2 * SLOTS) + (ROUND_B2 + ROUND_PROJ) * SLOTS + j + 1)
                    copy(side[:, 4 + j, :], acc[j % 2][:, :]).then_inc(evacuated[j % 2], 1)
                finish(act, act_end)
                with act.Fori(0, NA_PAIRS) as pair:
                    begin(act, stage + pair + ST_NA)
                    for hh in range(2):
                        for a in range(2):
                            act.dma_start(
                                pair_bias[a * GRID_W:(a + 1) * GRID_W, hh, :].rearrange("p (j k) -> p j k", j=NA_J),
                                bass.AP(rpb_in.tensor,
                                        layer * (GRID_W * RPB_SIZE) + pair * (2 * RPB_H * RPB_W)
                                        + (hh * RPB_H * RPB_W + RPB_PAD + (1 - a) * RPB_W + NA_COLS - 1),
                                        [[RPB_SIZE - 1, GRID_W], [RPB_W, NA_J], [1, GRID_W]])
                            ).then_inc(rpb_loaded, 16)
                    neighbourhood(layer, pair)
                begin(act, stage + ST_POOL)
                for i in range(2):
                    settle(act, (pool_mm, layer * 2 + i + 1))
                    act.activation(mixT[:, i, :], scp[i][:, :], ACT.Copy, scale=p2("pool_scale")[:, i:i + 1])
                finish(act, act_end)
                begin(act, stage + ST_OUT2)
                for k in range(NC):
                    op_high(mixT, k)
                finish(act, act_end)
                begin(act, stage + ST_LN1)
                layer_norm(layer * 3 + 1)
                shift(layer * 3 + 1, 1)
                ffn(stage + ST_FFN2, layer * ROUNDS2 + (ROUND_B2 + ROUND_FFN2), layer * GPS2 + (GP_B2 + GP_FFN2))
                begin(act, stage + ST_LN2)
                layer_norm(layer * 3 + 2)
                shift(layer * 3 + 2, 2)
            begin(act, ST_END)
            for n in range(2 * NT):
                act.wait_ge(out_turned, n + 1)
                copy(big[:, n * SEQ:(n + 1) * SEQ], acc[n % 2][:, :]).then_inc(out_copied, 1)
                if n % 2:
                    t = n // 2
                    act.wait_ge(out_copied, n + 1)
                    act.dma_start(out[t * P:(t + 1) * P, :], big[:, t * D_MODEL:(t + 1) * D_MODEL]
                                  ).then_inc(stored, 16)
            act.wait_ge(stored, 16 * NT)

        @block.vector
        def _(dve):
            def split(rnd, slot):
                dve.wait_ge(w_loaded[slot], rnd * 16 + 32)
                dve.wait_ge(pieces_done, rnd * SLOTS + slot + 1)
                split_piece(slot)

            def split_piece(slot):
                dve.tensor_copy(wH[:, slot, :], wraw[:, slot, :])
                dve.drain()
                dve.tensor_tensor(wL[:, slot, :], wraw[:, slot, :], wH[:, slot, :].bitcast(F32), ALU.subtract
                                  ).then_inc(split_done, 1)

            def split_round(rnd):
                for s in range(SLOTS):
                    split(rnd, s)

            def op_low(src, n):
                for k in range(0, NC, 2):
                    settle(dve, (op_hi, n * NC + k + 1))
                    dve.tensor_tensor(opL[:, k, :], src[:, k, :], opH[:, k, :].bitcast(F32), ALU.subtract
                                      ).then_inc(op_lo, 1)

            def norm(n, gain, to, at):
                dve.wait_ge(rstd_ready, n + 1)
                for k in range(NC):
                    dve.scalar_tensor_tensor(to[:, k, :], xT[:, k, :], gain[:, k:k + 1], rows[:, 0, :],
                                             ALU.mult, ALU.mult).then_inc(op_raw, 1)
                dve.drain()
                op_low(to, at)
                finish(dve, dve_end)

            def layer_norm(n, which, at):
                dve.wait_ge(ln_summed, n + 1)
                for k in range(NC):
                    dve.scalar_tensor_tensor(xT[:, k, :], scp[0][:, :], -1.0 / D_MODEL, xT[:, k, :],
                                             ALU.mult, ALU.add).then_inc(centred, 1)
                dve.drain()
                dve.wait_ge(ln_rstd, n + 1)
                for k in range(NC):
                    dve.scalar_tensor_tensor(xT[:, k, :], xT[:, k, :],
                                             p2("ln_g")[:, which * NC + k:which * NC + k + 1], rows[:, 0, :],
                                             ALU.mult, ALU.mult).then_inc(ln_scaled, 1)
                op_low(xT, at)
                finish(dve, dve_end)

            def out_chunk(chunk):
                return mixT[:, chunk, :].rearrange("p a s -> p (a s)")

            def bias_map(m, width, mb, bias, selected=None):
                waits = [(scores_ready, mb + m + 1)]
                if m >= 2:
                    waits.append((exped, mb + m - 1))
                if selected is not None:
                    waits.append((sel_ready, selected))
                settle(dve, *waits)
                dve.tensor_tensor_reduce(score[:, m % 2, 0:width], scp[m % 2][:, 0:width], bias, -1.0, 3e38,
                                         ALU.add, ALU.min, negmax[:, m % STATS:m % STATS + 1]).then_inc(biased, 1)

            def reciprocal_of(m, mb, gate=None):
                col = slice(m % STATS, m % STATS + 1)
                dve.wait_ge(exped, mb + m + 1)
                dve.tensor_scalar(denom[:, col], denom[:, col], TINY, None, ALU.max)
                dve.drain()
                if gate is None:
                    return dve.reciprocal(recip[:, col], denom[:, col])
                dve.reciprocal(recip[:, col], denom[:, col])
                dve.drain()
                return dve.tensor_tensor(recip[:, col], recip[:, col], gate, ALU.mult)

            def softmax_maps(mb, maps):
                for i in range(len(maps) + 1):
                    if i < len(maps):
                        width, bias, _, ready = maps[i]
                        bias_map(i, width, mb, bias, ready)
                    if i >= 1:
                        reciprocal_of(i - 1, mb, maps[i - 1][2]).then_inc(recip_ready, 1)

            def heads_out(tb, count, chunk):
                dve.wait_ge(pv_done, tb + count)
                dve.tensor_scalar(out_chunk(chunk), outp[:, :], 1.0, None, ALU.mult)
                finish(dve, dve_end)

            def t5_cols(a, hh, t):
                return a[:, hh, SEQ - (t + 1) * P:SEQ]

            units = [(hh, t) for hh in range(2) for t in range(NT)]

            def t5_wait(eng, layer, n):
                settle(eng, (t5_loaded, layer * (T5_LOADS * 16) + n * 16 + 32))

            def stick_breaking(layer, pair):
                split_round(layer * ROUNDS1 + pair + ROUND_SB)
                ub, tb = layer * (2 * U) + pair * U, layer * TRS1 + pair * U + TR_SB
                dve.memset(blocks[:, 0:SEQ // CMP_PAD, :], 1.0)
                one_row = blocks[:, 0:SEQ // CMP_PAD, :].rearrange("p a b -> p (a b)")
                for i, (hh, t) in enumerate(units):
                    w = (t + 1) * P
                    dve.wait_ge(sb_scores, ub + i + 1)
                    dve.tensor_tensor(sb_unit(sb_z_buf, hh, t), scp[i % 2][:, 0:w], c("strict")[:, SEQ - w:SEQ], ALU.add
                                      ).then_inc(sb_z, 1)
                dve.drain()
                for hh in range(2):
                    dve.wait_ge(sb_log, layer * 4 + pair * 2 + hh + 1)
                    dve.scalar_tensor_tensor(sb_t[hh], sb_z_buf[hh], 0.0, sb_t[hh], ALU.max, ALU.add)
                    dve.drain()
                    for t in range(NT):
                        a = sb_unit(sb_t, hh, t)
                        dve.tensor_tensor_scan(a[:, ::-1], one_row[:, 0:(t + 1) * P], a[:, ::-1], 0.0,
                                               ALU.mult, ALU.subtract)
                    dve.drain()
                    dve.tensor_tensor(sb_t[hh], sb_t[hh], sb_z_buf[hh], ALU.add).then_inc(sb_arg, 1)
                heads_out(tb, U, bass.ds(pair, 1))

            def moba(layer, pair):
                split_round(layer * ROUNDS1 + pair + ROUND_MB)
                t5_wait(dve, layer, pair)
                softmax_maps(layer * MAPS1 + pair * U + MAPS_MB,
                             [((t + 1) * P, t5_cols(pair_bias, hh, t), None, None) for hh, t in units])
                heads_out(layer * TRS1 + pair * U + TR_MB, U, bass.ds(pair + 2, 1))

            def differential(layer, pair):
                mb = layer * MAPS1 + pair * (2 * U) + MAPS_DF
                ub = layer * (2 * U) + pair * U
                split_round(layer * ROUNDS1 + pair + ROUND_DF)
                t5_wait(dve, layer, pair + PAIRS)
                for i in range(U + 1):
                    if i < U:
                        hh, t = units[i]
                        for half in range(2):
                            bias_map(2 * i + half, (t + 1) * P, mb, t5_cols(pair_bias, hh, t))
                    if i >= 1:
                        u = i - 1
                        w = (units[u][1] + 1) * P
                        m = 2 * u
                        reciprocal_of(m, mb, lam_scale)
                        reciprocal_of(m + 1, mb, lam_one).then_inc(recip_ready, 1)
                        dve.drain()
                        dve.wait_ge(df_second, ub + u + 1)
                        first, second = df_probs[u % 4]
                        dve.scalar_tensor_tensor(first[:, 0:w], first[:, 0:w], recip[:, m % STATS:m % STATS + 1],
                                                 second[:, 0:w], ALU.mult, ALU.subtract).then_inc(df_weight, 1)
                dve.wait_ge(df_rstd, layer * PAIRS + pair + 1)
                dve.scalar_tensor_tensor(out_chunk(bass.ds(pair + 6, 1)), outp[:, :], subln, rows[:, 1, :],
                                         ALU.mult, ALU.mult)
                finish(dve, dve_end)

            def nsa_select(layer):
                src = side[:, 0, :]
                dve.tensor_tensor(blocks[:, :, 0:N_CMP],
                                  bass.AP(src.tensor, src.offset, [list(src.ap[0]), [1, CMP_LEN], [CMP_STRIDE, N_CMP]]),
                                  p1("pos").unsqueeze(2).to_broadcast([P, CMP_LEN, N_CMP]), ALU.add)
                dve.memset(blkH[:, :, :].bitcast(F32), 0.0)
                dve.drain()
                diagonal = [(slice(HEAD * kv, HEAD * (kv + 1)), slice(CMP_PAD * kv, CMP_PAD * kv + N_CMP))
                            for kv in range(2)]
                for p, n in diagonal:
                    dve.tensor_copy(blkH[p, 0:CMP_LEN, n], blocks[p, :, 0:N_CMP])
                dve.drain()
                dve.wait_ge(low_cleared, layer + 1)
                for p, n in diagonal:
                    dve.tensor_tensor(blkL[p, 0:CMP_LEN, n], blocks[p, :, 0:N_CMP],
                                      blkH[p, 0:CMP_LEN, n].bitcast(F32), ALU.subtract)
                dve.drain().then_inc(blocks_ready, 1)
                for r in range(R_CMP):
                    split_round(layer * ROUNDS1 + (ROUND_CMP + r))
                dve.wait_ge(gate_exp, layer + 1)
                dve.tensor_scalar(gates, gates, 1.0, None, ALU.add)
                dve.drain()
                dve.reciprocal(gates, gates)
                x, g = gx[:, :, 0:N_CMP], gt[:, :, 0:N_CMP]
                dve.wait_ge(hid_sq, layer + 1)
                dve.tensor_scalar(g, g, 0.044715, 1.0, ALU.mult, ALU.add)
                dve.drain()
                dve.tensor_tensor(g, g, x, ALU.mult).then_inc(hid_poly, 1)
                dve.wait_ge(hid_exp, layer + 1)
                dve.tensor_scalar(g, g, 1.0, None, ALU.add)
                dve.drain()
                dve.reciprocal(g, g)
                dve.drain()
                for h in range(2):
                    dve.tensor_tensor(h1v[:, h, :, 0:N_CMP],
                                      gx[:, 2 + h, 0:N_CMP].unsqueeze(1).to_broadcast([P, HEADS, N_CMP]),
                                      gt[:, 2 + h, 0:N_CMP].unsqueeze(1).to_broadcast([P, HEADS, N_CMP]), ALU.mult)
                dve.drain().then_inc(gelu_ready, 1)
                dve.tensor_tensor(gx[:, 0:2, 0:N_CMP], gx[:, 0:2, 0:N_CMP], gt[:, 0:2, 0:N_CMP], ALU.mult
                                  ).then_inc(gelu_ready, 1)

                def flat(a):
                    return a[:, :, :, 0:N_CMP].rearrange("p t h n -> p (t h) n")

                def spread(a):
                    return a.unsqueeze(2).to_broadcast([P, NT * HEADS, N_CMP])

                dve.wait_ge(cmp_scores, layer + 1)
                for odd in range(2):
                    def every_other(a):
                        return a.rearrange("p t (a b) n -> p b (t a) n", b=2)[:, odd, :, 0:N_CMP]

                    dve.tensor_tensor(every_other(pcg[:, :, :, :]),
                                      trp[odd][:, 0:SEQ // 2].rearrange("p (a n) -> p a n", n=CMP_PAD)[:, :, 0:N_CMP],
                                      every_other(cmp_bias[:, :, :, :]), ALU.add)
                dve.drain()
                dve.tensor_reduce(cmax, flat(pcg), AX.X, ALU.max)
                dve.drain()
                dve.tensor_tensor(flat(pcg), flat(pcg), spread(cmax), ALU.subtract).then_inc(cmp_shift, 1)
                dve.wait_ge(cmp_exp, layer + 1)
                dve.tensor_tensor(flat(pc), flat(pc), flat(cmp_mask), ALU.mult)
                dve.drain()
                dve.tensor_reduce(csum, flat(pc), AX.X, ALU.add)
                dve.drain()
                dve.tensor_scalar(csum, csum, TINY, None, ALU.max)
                dve.drain()
                dve.reciprocal(csum, csum)
                dve.drain()
                dve.tensor_tensor(flat(pc), flat(pc), spread(csum), ALU.mult).then_inc(pc_ready, 1)
                dve.drain()
                dve.tensor_tensor(pcg[:, :, :, 0:N_CMP].rearrange("p t h n -> p (t h) n"), flat(pc),
                                  gates_of(0), ALU.mult).then_inc(pc_ready, 1)
                dve.wait_ge(imp_ready, layer + 1)
                dve.tensor_tensor(imp, scp[0][:, 0:NT * N_SLC].rearrange("p (t j) -> p t j", t=NT),
                                  c("past").rearrange("p (t j) -> p t j", t=NT), ALU.mult)
                dve.drain()
                dve.tensor_tensor(imp, imp, c("force").rearrange("p (t j) -> p t j", t=NT), ALU.add)
                dve.drain()
                shape = [P, NT, N_SLC, N_SLC]
                mine, other = imp.unsqueeze(3).to_broadcast(shape), imp.unsqueeze(2).to_broadcast(shape)
                more = beats[:, 0, :].rearrange("p (t j i) -> p t j i", t=NT, j=N_SLC)
                same = beats[:, 1, :].rearrange("p (t j i) -> p t j i", t=NT, j=N_SLC)
                dve.tensor_tensor(more, other, mine, ALU.is_gt)
                dve.tensor_tensor(same, other, mine, ALU.is_equal)
                dve.drain()
                dve.tensor_tensor(beats[:, 1, :].rearrange("p (t j) -> p t j", t=NT),
                                  beats[:, 1, :].rearrange("p (t j) -> p t j", t=NT),
                                  c("earlier").unsqueeze(1).to_broadcast([P, NT, N_SLC * N_SLC]), ALU.mult)
                dve.drain()
                dve.tensor_tensor(beats[:, 0, :], beats[:, 0, :], beats[:, 1, :], ALU.add)
                dve.drain()
                dve.tensor_reduce(rank, more, AX.X, ALU.add)
                dve.drain()
                dve.tensor_scalar(sel_neg, rank, float(SLC_TOPN), NEG, ALU.is_ge, ALU.mult)
                finish(dve, dve_end)

            def gates_of(branch):
                g = gates[:, :, branch * HEADS:(branch + 1) * HEADS]
                return g.unsqueeze(3).to_broadcast([P, NT, HEADS, N_CMP])

            def nsa_pair(layer, pair):
                dve.tensor_copy(qT, side[:, bass.ds(pair + 4, 1), :].rearrange("p a s -> p (a s)"))
                dve.tensor_copy(vc_pair[:, :], vc_diag[:, bass.ds(pair * P, P)])
                dve.drain().then_inc(pair_ready, 1)
                t5_wait(dve, layer, pair + 2 * PAIRS)
                sel = layer * (2 * U) + pair * U
                maps = []
                for n, (hh, t) in enumerate(units):
                    w = (t + 1) * P
                    for branch in (1, 2):
                        g = gates[:, t, bass.ds(pair * 2 + (branch * HEADS + hh), 1)]
                        if branch == 1:
                            maps.append((w, sel_bias[:, n % 2, 0:w], g, sel + n + 1))
                        else:
                            maps.append((w, t5_cols(pair_bias, hh, t), g, None))
                softmax_maps(layer * MAPS1 + pair * (2 * U) + MAPS_NS, maps)
                heads_out(layer * TRS1 + pair * (2 * U) + TR_NS, 2 * U, bass.ds(pair + 4, 1))

            def neighbourhood(layer, pair):
                split_round(layer * ROUNDS2 + pair + (ROUND_B2 + ROUND_NA))
                dve.wait_ge(bias_ready, layer * NA_PAIRS + pair + 1)
                maps = []
                for hh, t in units:
                    at = (NT - 1 - t) * 2 * GRID_W
                    maps.append((SEQ, pair_bias[:, hh, at:at + SEQ], None, None))
                softmax_maps(layer * (4 * U) + pair * U + DEPTH * MAPS1, maps)
                heads_out(layer * (4 * U) + pair * U + DEPTH * TRS1, U, bass.ds(pair + 4, 1))

            def add_tile(rounds, r, j, scale):
                dve.wait_ge(pieces_done, r * SLOTS + rounds * SLOTS + j + 1)
                x = xT[:, bass.ds(r * SLOTS + j, 1), :].rearrange("p a s -> p (a s)")
                if scale is None:
                    ins = dve.tensor_tensor(x, acc[j % 2][:, :], x, ALU.add)
                else:
                    ins = dve.scalar_tensor_tensor(x, x, scale, acc[j % 2][:, :], ALU.mult, ALU.add)
                ins.then_inc(evacuated[j % 2], 1)

            def add_out(rounds, scale=None):
                with dve.Fori(0, R_OUT) as r:
                    for j in range(SLOTS):
                        add_tile(rounds, r, j, scale)
                        split(r + rounds, j)

            def hidden_tile(a, tile):
                return a[:, bass.ds(tile, 1), :].rearrange("p a s -> p (a s)")

            def hidden_low(tile, value):
                dve.tensor_tensor(hidden_tile(hidL, tile), value, hidden_tile(hidH, tile).bitcast(F32), ALU.subtract
                                  ).then_inc(hid_ready, 1)

            def ffn(stage, rounds, silu):
                begin(dve, stage)
                for part, (r_gu, n) in enumerate(zip(R_GU, PARTS2)):
                    with dve.Fori(0, r_gu) as r:
                        for j in range(2):
                            split(r + rounds, 2 * j)
                            dve.wait_ge(silu_ready, silu + r * 2 + j + 1)
                            dve.wait_ge(pieces_done, r * SLOTS + rounds * SLOTS + 2 * j + 2)
                            dve.scalar_tensor_tensor(raw[:, j, :], acc[1][:, :], 0.5, evac[:, j, :], ALU.mult,
                                                     ALU.mult).then_inc(evacuated[1], 1)
                            dve.drain()
                            tile = r * 2 + j
                            dve.tensor_copy(hidden_tile(hidH, tile), raw[:, j, :])
                            dve.drain()
                            hidden_low(tile, raw[:, j, :])
                            split(r + rounds, 2 * j + 1)
                    add_out(rounds + r_gu, ALPHA if part == 0 else None)
                    rounds, silu = rounds + r_gu + R_DOWN, silu + n
                finish(dve, dve_end)

            dve.memset(eps_norm, NORM_EPS)
            dve.memset(eps_ln, LN_EPS)
            dve.memset(one_col, 1.0)
            dve.memset(vc_diag[:, :], 0.0)
            dve.memset(h1v[:, :, :, :], 0.0)
            dve.memset(pc[:, :, :, :], 0.0)
            dve.memset(pcg[:, :, :, :], 0.0)
            dve.memset(cmp_bias[:, :, :, :], NEG)
            dve.memset(pair_bias, 0.0).then_inc(zeroed, 1)
            for k in range(1, NC, 2):
                dve.wait_ge(x_turned, k + 1)
                dve.tensor_copy(xT[:, k, :], acc[1][:, :]).then_inc(evacuated[1], 1)
            for s in range(SLOTS):
                dve.wait_ge(w_loaded[s], 16)
                split_piece(s)
            dve.wait_ge(t5_loaded, 16)
            for t in range(NT):
                n = (t + 1) * P // CMP_STRIDE - 1
                first = (NT - 1 - t) * P + CMP_LEN - 1
                dve.tensor_copy(cmp_bias[:, t, :, 0:n],
                                t5_nsa[:, :, first:first + (n - 1) * CMP_STRIDE + 1:CMP_STRIDE])
            dve.drain()
            dve.tensor_scalar(cmp_mask[:, :, :, :].rearrange("p t h n -> p (t h n)"),
                              cmp_bias[:, :, :, :].rearrange("p t h n -> p (t h n)"), NEG / 10, None, ALU.is_gt)
            finish(dve, dve_end)

            with dve.Fori(0, DEPTH) as layer:
                stage = layer * STAGES1 + 1
                begin(dve, stage + ST_NORM)
                dve.wait_ge(par_loaded, layer * 16 + 16)
                lv = p1("lam").rearrange("p (a b d) -> p a b d", a=2, b=2)
                dve.tensor_tensor(lam_prod.rearrange("p (a d) -> p a d", a=2), lv[:, :, 0, :], lv[:, :, 1, :], ALU.mult)
                dve.drain()
                dve.tensor_reduce(lam_tmp, lam_prod.rearrange("p (a d) -> p a d", a=2), AX.X, ALU.add
                                  ).then_inc(lam_dots, 1)
                dve.wait_ge(lam_exps, layer + 1)
                dve.scalar_tensor_tensor(lam_one, lam2[:, 0:1], p1("lam_init")[:, 0:1], lam2[:, 1:2], ALU.add,
                                         ALU.subtract)
                dve.drain()
                dve.scalar_tensor_tensor(lam_scale, lam_one, -1.0, lam_one, ALU.mult, ALU.max)
                dve.drain()
                dve.tensor_scalar(lam_scale, lam_scale, 1.0, None, ALU.max)
                dve.drain()
                dve.reciprocal(lam_scale, lam_scale)
                dve.drain()
                dve.tensor_tensor(lam_one, lam_one, lam_scale, ALU.mult)
                dve.tensor_scalar(lam_eps, lam_scale, lam_scale, NORM_EPS, ALU.mult, ALU.mult)
                dve.tensor_tensor(subln, p1("subln"), p1("lam_init")[:, 1:2], ALU.mult)
                norm(layer * 2, p1("norm_attn"), mixT, layer * SPLITS1)
                with dve.Fori(0, PAIRS) as pair:
                    begin(dve, stage + pair + ST_SB)
                    stick_breaking(layer, pair)
                with dve.Fori(0, PAIRS) as pair:
                    begin(dve, stage + pair + ST_MB)
                    moba(layer, pair)
                with dve.Fori(0, PAIRS) as pair:
                    begin(dve, stage + pair + ST_DF)
                    differential(layer, pair)
                begin(dve, stage + ST_NSA)
                nsa_select(layer)
                with dve.Fori(0, PAIRS) as pair:
                    begin(dve, stage + pair + ST_NSP)
                    nsa_pair(layer, pair)
                begin(dve, stage + ST_OUT)
                op_low(mixT, layer * SPLITS1 + 1)
                add_out(layer * ROUNDS1 + ROUND_OUT)
                finish(dve, dve_end)
                begin(dve, stage + ST_NORM2)
                norm(layer * 2 + 1, p1("norm_mlp"), mixT, layer * SPLITS1 + 2)
                begin(dve, stage + ST_MLP)
                with dve.Fori(0, PARTS1) as part:
                    rounds = layer * ROUNDS1 + part * R_PART1 + ROUND_MLP
                    tiles = layer * (PARTS1 * PART) + part * PART
                    for j in range(PART):
                        split(rounds + j // SLOTS, j % SLOTS)
                        dve.wait_ge(relu_ready, tiles + j + 1)
                        dve.tensor_tensor(raw[:, j % 2, :], evac[:, j % 2, :], evac[:, j % 2, :], ALU.mult)
                        dve.drain()
                        hidden_low(j, raw[:, j % 2, :])
                    add_out(rounds + R_UP)
                finish(dve, dve_end)
            begin(dve, ST_FINAL)
            norm(2 * DEPTH, p1("final_norm"), xT, DEPTH * SPLITS1)
            with dve.Fori(0, DEPTH) as layer:
                stage = layer * STAGES2 + ST_B2
                ffn(stage + ST_FFN1, layer * ROUNDS2 + ROUND_B2, layer * (2 * sum(PARTS2)))
                begin(dve, stage + ST_LN0)
                dve.wait_ge(par_loaded, layer * 16 + 16 * (DEPTH + 1))
                layer_norm(layer * 3, 0, layer * SPLITS2 + SPLIT_B2)
                begin(dve, stage + ST_PROJ)
                split_round(layer * ROUNDS2 + (ROUND_B2 + ROUND_PROJ))
                finish(dve, dve_end)
                with dve.Fori(0, NA_PAIRS) as pair:
                    begin(dve, stage + pair + ST_NA)
                    neighbourhood(layer, pair)
                begin(dve, stage + ST_POOL)
                border = max(POOL_WINDOWS)
                wide = SEQ + 2 * border
                pads = [big_pad(n, wide) for n in range(3)]
                dve.memset(pads[0], 0.0)
                dve.memset(pads[1], 0.0)
                dve.memset(pads[2], 0.0)
                dve.drain()
                for i in range(2):
                    dve.tensor_copy(pads[0][:, border:border + SEQ], side[:, i, :])
                    dve.drain()
                    at, reach, done = 0, 1, 0
                    for w in POOL_WINDOWS[0:2 * i + 2]:
                        lo, hi = (1, 0) if w == 2 else (w // 4, w // 4)
                        to = 1 if at != 1 else 2
                        span = slice(border // 2, wide - border // 2)
                        dve.tensor_tensor(pads[to][:, span], pads[at][:, span.start - lo:span.stop - lo],
                                          pads[at][:, span.start + hi:span.stop + hi], ALU.add)
                        dve.drain()
                        at = to
                        if w in POOL_WINDOWS[2 * i:2 * i + 2]:
                            g = slice(HEAD * done, HEAD * (done + 1))
                            mean = score[g, i, :]
                            dve.tensor_tensor(mean, pads[at][g, border:border + SEQ],
                                              c("inv_count")[g, i * SEQ:(i + 1) * SEQ], ALU.mult)
                            dve.drain()
                            dve.tensor_tensor(mean, mean, side[g, i, :], ALU.subtract)
                            done += 1
                    dve.drain().then_inc(pooled, 1)
                for i in range(2):
                    w = p2("conv")[:, 3 * i:3 * i + 3]
                    z = pads[1 + i]
                    dve.memset(z[:, 0:SEQ + 2], 0.0)
                    dve.drain()
                    dve.tensor_tensor(z[:, 1:SEQ + 1], side[:, 4 + i, :], side[:, 6 + i, :], ALU.mult)
                    dve.drain()
                    y = mixT[:, 2 + i, :]
                    dve.tensor_scalar(y, z[:, 0:SEQ], w[:, 0:1], None, ALU.mult)
                    dve.drain()
                    for k in (1, 2):
                        dve.scalar_tensor_tensor(y, z[:, k:k + SEQ], w[:, k:k + 1], y, ALU.mult, ALU.add)
                        dve.drain()
                    dve.tensor_tensor(y, y, side[:, 2 + i, :], ALU.mult)
                finish(dve, dve_end)
                begin(dve, stage + ST_OUT2)
                op_low(mixT, layer * SPLITS2 + (SPLIT_B2 + 1))
                add_out(layer * ROUNDS2 + (ROUND_B2 + ROUND_OUT2), ALPHA)
                finish(dve, dve_end)
                begin(dve, stage + ST_LN1)
                layer_norm(layer * 3 + 1, 1, layer * SPLITS2 + (SPLIT_B2 + 2))
                ffn(stage + ST_FFN2, layer * ROUNDS2 + (ROUND_B2 + ROUND_FFN2),
                    layer * (2 * sum(PARTS2)) + sum(PARTS2))
                begin(dve, stage + ST_LN2)
                layer_norm(layer * 3 + 2, 2, layer * SPLITS2 + (SPLIT_B2 + 3))

        @block.gpsimd
        def _(pool):
            def scale_prob(m, width, p):
                return pool.tensor_tensor(p[:, 0:width], p[:, 0:width],
                                          recip[:, m % STATS:m % STATS + 1].to_broadcast([P, width]), ALU.mult)

            def softmax_maps(rb, widths):
                for m, w in enumerate(widths):
                    pool.wait_ge(recip_ready, rb + m + 1)
                    scale_prob(m, w, prob[:, m % 4, :]).then_inc(normed, 1)

            def idle(stage):
                finish(pool, pool_end)

            causal = [(t + 1) * P for hh in range(2) for t in range(NT)]

            def op_low(src, n):
                for k in range(1, NC, 2):
                    settle(pool, (op_hi, n * NC + k + 1))
                    pool.tensor_tensor(opL[:, k, :], src[:, k, :], opH[:, k, :].bitcast(F32), ALU.subtract
                                       ).then_inc(op_lo_pool, 1)

            def low_stage(stage, src, n):
                begin(pool, stage)
                op_low(src, n)
                finish(pool, pool_end)

            finish(pool, pool_end)
            with pool.Fori(0, DEPTH) as layer:
                stage = layer * STAGES1 + 1
                low_stage(stage + ST_NORM, mixT, layer * SPLITS1)
                with pool.Fori(0, PAIRS) as pair:
                    idle(stage + pair + ST_SB)
                with pool.Fori(0, PAIRS) as pair:
                    begin(pool, stage + pair + ST_MB)
                    softmax_maps(layer * RECIPS1 + pair * U + RECIP_MB, causal)
                    finish(pool, pool_end)
                with pool.Fori(0, PAIRS) as pair:
                    begin(pool, stage + pair + ST_DF)
                    for u, w in enumerate(causal):
                        pool.wait_ge(recip_ready, layer * RECIPS1 + pair * U + (RECIP_DF + u + 1))
                        scale_prob(2 * u + 1, w, df_probs[u % 4][1]).then_inc(df_second, 1)
                    finish(pool, pool_end)
                begin(pool, stage + ST_NSA)
                pool.memset(blkL[:, :, :].bitcast(F32), 0.0).then_inc(low_cleared, 1)
                finish(pool, pool_end)
                with pool.Fori(0, PAIRS) as pair:
                    begin(pool, stage + pair + ST_NSP)
                    settle(pool, (t5_loaded, layer * (T5_LOADS * 16) + pair * 16 + (2 * PAIRS * 16 + 32)))
                    rb = layer * RECIPS1 + pair * (2 * U) + RECIP_NS
                    mb = layer * MAPS1 + pair * (2 * U) + MAPS_NS

                    def select(n):
                        hh, t = n // NT, n % NT
                        w = (t + 1) * P
                        if n >= 2:
                            pool.wait_ge(biased, mb + 2 * (n - 2) + 1)
                        pool.tensor_tensor(
                            sel_bias[:, n % 2, 0:w].rearrange("p (j k) -> p j k", k=SLC_LEN),
                            pair_bias[:, hh, SEQ - w:SEQ].rearrange("p (j k) -> p j k", k=SLC_LEN),
                            sel_neg[:, t, 0:w // SLC_LEN].unsqueeze(2).to_broadcast([P, w // SLC_LEN, SLC_LEN]),
                            ALU.add).then_inc(sel_ready, 1)

                    select(0)
                    select(1)
                    for m in range(2 * U):
                        w = causal[m // 2]
                        pool.wait_ge(recip_ready, rb + m + 1)
                        scale_prob(m, w, prob[:, m % 4, :]).then_inc(normed, 1)
                        if m % 2 and m // 2 + 2 < U:
                            select(m // 2 + 2)
                    finish(pool, pool_end)
                low_stage(stage + ST_OUT, mixT, layer * SPLITS1 + 1)
                low_stage(stage + ST_NORM2, mixT, layer * SPLITS1 + 2)
                idle(stage + ST_MLP)
            low_stage(ST_FINAL, xT, DEPTH * SPLITS1)
            with pool.Fori(0, DEPTH) as layer:
                stage = layer * STAGES2 + ST_B2
                idle(stage + ST_FFN1)
                low_stage(stage + ST_LN0, xT, layer * SPLITS2 + SPLIT_B2)
                idle(stage + ST_PROJ)
                with pool.Fori(0, NA_PAIRS) as pair:
                    begin(pool, stage + pair + ST_NA)
                    settle(pool, (rpb_loaded, layer * (64 * NA_PAIRS) + pair * 64 + 64))
                    for hh in range(2):
                        rel = pair_bias[:, hh, :].rearrange("p (j k) -> p j k", k=GRID_W)
                        pool.tensor_tensor(rel, rel, c("col_mask").unsqueeze(1).to_broadcast([P, NA_J, GRID_W]),
                                           ALU.add)
                    pool.drain().then_inc(bias_ready, 1)
                    softmax_maps(layer * (4 * U) + pair * U + DEPTH * RECIPS1, [SEQ] * U)
                    finish(pool, pool_end)
                idle(stage + ST_POOL)
                low_stage(stage + ST_OUT2, mixT, layer * SPLITS2 + (SPLIT_B2 + 1))
                low_stage(stage + ST_LN1, xT, layer * SPLITS2 + (SPLIT_B2 + 2))
                idle(stage + ST_FFN2)
                low_stage(stage + ST_LN2, xT, layer * SPLITS2 + (SPLIT_B2 + 3))


def _bucket(n):
    exact = N_BUCKETS // 2
    nf = np.maximum(n, 1).astype(np.float32)
    large = exact + (np.log(nf / np.float32(exact)) / np.float32(math.log(MAX_DISTANCE / exact))
                     * np.float32(N_BUCKETS - exact)).astype(np.int32)
    return np.where(n < exact, n, np.minimum(large, N_BUCKETS - 1))


def _constants():
    a = np.zeros((P, CONST_W), np.float32)

    def put(name, v):
        lo, hi = CONST[name]
        a[:v.shape[0], lo:hi] = v.reshape(v.shape[0], -1)

    p, m = np.arange(P)[:, None], np.arange(SEQ)[None]
    put("ident", np.eye(P))
    put("ones", np.ones((P, P)))
    put("head_ones", np.kron(np.eye(2), np.ones((HEAD, HEAD))))
    put("strict", np.where(p + SEQ - P - m >= 1, 0.0, NEG))
    start = np.arange(CMP_PAD)[:, None] * CMP_STRIDE
    s0 = np.arange(N_SLC)[None] * SLC_LEN
    cover = np.clip(np.minimum(start + CMP_LEN - 1, s0 + SLC_LEN - 1) - np.maximum(start, s0) + 1, 0, None) / CMP_LEN
    cover[N_CMP:] = 0
    put("cover", np.tile(cover, (HEADS, 1)))
    own = (np.arange(NT)[None, :, None] * P + p[:, :, None]) // SLC_LEN
    j = np.arange(N_SLC)[None, None]
    put("past", (j < own).astype(np.float32))
    put("force", np.where(j == own, -NEG, np.where(j < own, 0.0, NEG)))
    put("earlier", np.broadcast_to(np.arange(N_SLC)[None, None] < np.arange(N_SLC)[None, :, None], (P, N_SLC, N_SLC)))
    t = np.arange(SEQ)
    counts = [np.clip(t - w // 2 + w, 0, SEQ) - np.clip(t - w // 2, 0, SEQ) for w in POOL_WINDOWS]
    inv = 1.0 / np.stack(counts)
    put("inv_count", np.stack([np.repeat(inv[0:2], HEAD, 0), np.repeat(inv[2:4], HEAD, 0)], 1))
    qc, kc = np.arange(P)[:, None] % GRID_W, np.arange(GRID_W)[None]
    left = np.clip(qc - NA_COLS // 2, 0, GRID_W - NA_COLS)
    put("col_mask", np.where((kc >= left) & (kc < left + NA_COLS), 0.0, NEG))
    u = np.arange(SEQ + P)
    dist = SEQ - 1 - u
    hot = np.where(dist[None] >= 0, np.arange(N_BUCKETS)[:, None] == _bucket(np.maximum(dist, 0))[None], False)
    put("neg_rows", np.full((P, 12), NEG))
    return a, np.concatenate([hot, (dist < 0)[None]], 0).astype(np.float32)


def _pieces(inputs):
    out = []

    def put(w):
        k = w.shape[0] // P
        out.append(w.reshape(k, P, P).transpose(1, 0, 2).reshape(-1))

    g = inputs
    sizes = (GROUP,) * 7 + (HEAD,) * 6 + (3 * HEADS,) + (GROUP,) * 3
    at = np.concatenate([[0], np.cumsum(sizes)]).tolist()
    for l in range(DEPTH):
        w = g["w_in"][l]

        def cols(i, pair):
            return w[:, at[i] + pair * P:at[i] + (pair + 1) * P]

        gate_cols = np.zeros((D_MODEL, P), w.dtype)
        gate_cols[:, 0:3 * HEADS] = w[:, at[13]:at[14]]
        sides = [[cols(7, 0), cols(9, 0)], [cols(11, 0), gate_cols], [cols(6, 0), cols(6, 1)]]
        for first, fourth in zip((0, 3, 14), sides):
            for pair in range(PAIRS):
                for i in range(3):
                    put(cols(first + i, pair))
                put(fourth[pair])
        both = np.concatenate([g[n][l].reshape(CMP_LEN, HEAD, CMP_HIDDEN).transpose(1, 0, 2)
                               for n in ("cmp_k_w1", "cmp_v_w1")], 0)
        per = PIECE // CMP_HIDDEN
        for n in range(CMP_LEN // per):
            out.append(both[:, n * per:(n + 1) * per].reshape(-1))
        for d in range(NC):
            put(g["w_out"][l][:, d * P:(d + 1) * P])
        for part in range(PARTS1):
            for f in range(part * PART, (part + 1) * PART):
                put(g["w_up"][l][:, f * P:(f + 1) * P])
            for d in range(NC):
                put(g["w_down"][l][part * PART * P:(part + 1) * PART * P, d * P:(d + 1) * P])
    for l in range(DEPTH):
        def ffn(name):
            f0 = 0
            for n in PARTS2:
                for f in range(f0, f0 + n):
                    for part in ("gate", "up"):
                        put(g[f"{name}_w_{part}_2"][l][:, f * P:(f + 1) * P])
                for d in range(NC):
                    put(g[f"{name}_w_down_2"][l][f0 * P:(f0 + n) * P, d * P:(d + 1) * P])
                f0 += n

        ffn("ffn1")
        w = g["w_in_2"][l]
        for i in (4, 5, 6, 7):
            put(w[:, i * P:(i + 1) * P])
        qkv = NC * P
        for pair in range(NA_PAIRS):
            for i in range(3):
                lo = qkv + i * NA_HEADS * HEAD + pair * P
                put(w[:, lo:lo + P])
            put(w[:, pair * P:(pair + 1) * P])
        for d in range(NC):
            put(g["w_out_2"][l][:, d * P:(d + 1) * P])
        ffn("ffn2")
    out.append(np.zeros(SLOTS * P * PIECE, np.float32))
    return np.concatenate(out)


def _parameters(g):
    a = np.zeros((DEPTH, P, PAR1_W), np.float32)
    b = np.zeros((DEPTH, P, PAR2_W), np.float32)

    def put(to, cols, l, name, v):
        lo, hi = cols[name]
        to[l, :, lo:hi] = v.reshape(P, -1)

    def chunks(v):
        return v.reshape(-1, P).T

    for l in range(DEPTH):
        put(a, PAR1, l, "norm_attn", chunks(g["norm_attn"][l]))
        put(a, PAR1, l, "norm_mlp", chunks(g["norm_mlp"][l]))
        put(a, PAR1, l, "final_norm", chunks(g["final_norm"]))
        put(a, PAR1, l, "pos", np.concatenate([g["cmp_pos_k"][l].T, g["cmp_pos_v"][l].T], 0))
        put(a, PAR1, l, "subln", np.tile(g["diff_subln"][l], 2))
        init = 0.8 - 0.6 * math.exp(-0.3 * l)
        put(a, PAR1, l, "lam_init", np.tile(np.array([init, 1.0 - init], np.float32), (P, 1)))
        put(a, PAR1, l, "lam", np.tile(g["diff_lambda"][l].reshape(1, -1), (P, 1)))
        for n in "kv":
            put(a, PAR1, l, f"w2{n}", g[f"cmp_{n}_w2"][l].reshape(2, P, HEAD).transpose(1, 0, 2))
        put(b, PAR2, l, "ln_g", chunks(g["ln_g_2"][l]))
        put(b, PAR2, l, "ln_b", chunks(g["ln_b_2"][l]))
        put(b, PAR2, l, "pool_scale", chunks(g["pool_scale_2"][l]))
        put(b, PAR2, l, "conv", g["conv_w_2"][l].reshape(3, 2, P).transpose(2, 1, 0))
        put(b, PAR2, l, "pool_w", g["pool_w_2"][l].reshape(2, P, HEAD).transpose(1, 0, 2))
    return a, b


def kernel(**inputs):
    import concourse.bacc as bacc
    from concourse.bass_utils import run_bass_kernel_spmd

    g = {k: np.asarray(v) for k, v in inputs.items()}
    par1, par2 = _parameters(g)
    const, bucket = _constants()
    rpb = np.pad(g["rpb_2"].reshape(DEPTH, 1, -1), ((0, 0), (0, 0), (RPB_PAD, RPB_PAD)))
    rpb = np.ascontiguousarray(np.broadcast_to(rpb, (DEPTH, GRID_W, RPB_SIZE)))
    arrays = {
        "in_x": np.ascontiguousarray(g["x"].reshape(SEQ, D_MODEL)),
        "in_weights": _pieces(g),
        "in_const": const,
        "in_bucket": bucket,
        "in_par1": par1,
        "in_par2": par2,
        "in_table": np.ascontiguousarray(g["rel_bias"]),
        "in_rpb": rpb,
    }
    nc = bacc.Bacc("TRN2", target_bir_lowering=False, num_devices=1)
    args = [nc.dram_tensor(n, a.shape, mybir.dt.from_np(a.dtype), kind="ExternalInput").ap() for n, a in arrays.items()]
    out = nc.dram_tensor("out_x", (SEQ, D_MODEL), F32, kind="ExternalOutput").ap()
    emit(nc, *args, out)
    r = run_bass_kernel_spmd(nc, [arrays], core_ids=[0])
    return r.results[0]["out_x"].reshape(1, SEQ, D_MODEL)
```

```python
import math
from contextlib import ExitStack

import numpy as np

import concourse.bass as bass
from concourse import mybir

ALU = mybir.AluOpType
ACT = mybir.ActivationFunctionType
AX = mybir.AxisListType
F32 = mybir.dt.float32
F32R = mybir.dt.float32r

P = 128
DEPTH = 2
SEQ = 512
D_MODEL = 1024
NT = SEQ // P
NC = D_MODEL // P
HEAD = 64
HEADS = 4
GROUP = HEADS * HEAD
PAIRS = HEADS // 2
D_FF = 4 * D_MODEL
D_FF2 = 2816
NORM_EPS = 1e-6
LN_EPS = 1e-5
TINY = 1e-30
NEG = -1e30
N_BUCKETS, MAX_DISTANCE = 32, 128
CMP_LEN, CMP_STRIDE, CMP_HIDDEN = 32, 16, 256
N_CMP = (SEQ - CMP_LEN) // CMP_STRIDE + 1
CMP_PAD = 32
SLC_LEN, SLC_TOPN = 64, 4
N_SLC = SEQ // SLC_LEN
DIFF_HALF = HEAD // 2
ALPHA = (2.0 * DEPTH) ** 0.25
POOL_WINDOWS = (2, 4, 8, 16)
GRID_W = 64
GRID_H = SEQ // GRID_W
NA_HEADS, NA_PAIRS = 8, 4
NA_COLS = 16
RPB_W = 2 * NA_COLS - 1
RPB_H = 2 * GRID_H - 1
RPB_PAD = 32
RPB_SIZE = NA_HEADS * GRID_H * RPB_W + 2 * RPB_PAD
NA_TILES = ((0, 2), (0, 3), (1, 3), (2, 2))
NA_KEYS = [n * P for _, n in NA_TILES]
NA_REACH = 3 * NA_COLS
NA_EDGE = 2 * NA_COLS
NA_BIAS = GRID_H * (NA_REACH + 2 * NA_EDGE)
assert GRID_W == NT * NA_COLS and NA_COLS * GRID_H == P
PART = 8
PARTS1 = D_FF // P // PART
PARTS2 = (8, 8, 6)
assert sum(PARTS2) * P == D_FF2

SLOTS = 4
BLOCKS_AT = 12 * SEQ
PIECE = NC * P

R_ATT, R_CMP, R_OUT = 2, 2, NC // SLOTS
R_UP, R_DOWN = PART // SLOTS, NC // SLOTS
ROUND_SB, ROUND_MB, ROUND_DF, ROUND_CMP = 0, R_ATT, 2 * R_ATT, 3 * R_ATT
ROUND_OUT = ROUND_CMP + R_CMP
ROUND_MLP = ROUND_OUT + R_OUT
R_PART1 = R_UP + R_DOWN
ROUNDS1 = ROUND_MLP + PARTS1 * R_PART1
R_GU = [2 * n // SLOTS for n in PARTS2]
ROUNDS_FFN = sum(R_GU) + len(PARTS2) * R_DOWN
ROUND_PROJ = ROUNDS_FFN
ROUND_NA = ROUND_PROJ + 1
ROUND_OUT2 = ROUND_NA + NA_PAIRS
ROUND_FFN2 = ROUND_OUT2 + R_OUT
ROUNDS2 = ROUND_FFN2 + ROUNDS_FFN
ROUND_B2 = DEPTH * ROUNDS1

GP_SETUP = NC // 2
GP_OUT = 3 * R_ATT * 2
GP_MLP = GP_OUT + NC // 2
GP_PART1 = (PART + NC) // 2
GPS1 = GP_MLP + PARTS1 * GP_PART1
GP_FFN = sum(PARTS2) + len(PARTS2) * NC // 2
GP_PROJ = GP_FFN
GP_NA = GP_PROJ + 2
GP_OUT2 = GP_NA + 2 * NA_PAIRS
GP_FFN2 = GP_OUT2 + NC // 2
GPS2 = GP_FFN2 + GP_FFN
GP_B2 = GP_SETUP + DEPTH * GPS1

SPLITS1, SPLITS2 = 3, 4
SPLIT_B2 = DEPTH * SPLITS1 + 1

(ST_NORM, ST_SB, ST_MB, ST_DF, ST_NSA, ST_NSP, ST_OUT, ST_NORM2, ST_MLP) = (0, 1, 3, 5, 7, 8, 10, 11, 12)
STAGES1 = 13
ST_FINAL = 1 + DEPTH * STAGES1
ST_B2 = ST_FINAL + 1
(ST_FFN1, ST_LN0, ST_PROJ, ST_NA, ST_POOL, ST_OUT2, ST_LN1, ST_FFN2, ST_LN2) = (0, 1, 2, 3, 7, 8, 9, 10, 11)
STAGES2 = 12
ST_END = ST_B2 + DEPTH * STAGES2
T5_LOADS = 3 * PAIRS

LAG = 3
STATS = 8
U = 2 * NT
MAPS_MB, MAPS_DF, MAPS_NS = 0, 2 * U, 6 * U
MAPS1 = 10 * U
NORM_MB, NORM_NS = 0, 2 * U
NORMS1 = 6 * U
TR_SB, TR_MB, TR_DF, TR_NS = 0, 2 * U, 4 * U, 6 * U
TRS1 = 10 * U



def columns(**widths):
    at, out = 0, {}
    for name, w in widths.items():
        out[name] = (at, at + w)
        at += w
    return out, at


CONST, CONST_W = columns(ident=P, ones=P, neg_rows=12, head_ones=P, strict=SEQ, cover=N_SLC, past=NT * N_SLC,
                         force=NT * N_SLC, earlier=N_SLC * N_SLC, inv_count=2 * SEQ, mask_inner=NA_REACH,
                         mask_first=NA_EDGE, mask_last=NA_EDGE)
PAR1, PAR1_W = columns(norm_attn=NC, norm_mlp=NC, final_norm=NC, pos=CMP_LEN, subln=1, lam_init=2,
                       lam=4 * DIFF_HALF, w2k=2 * HEAD, w2v=2 * HEAD)
PAR2, PAR2_W = columns(ln_g=3 * NC, ln_b=3 * NC, pool_scale=2, conv=6, pool_w=2 * HEAD)


def emit(nc, x_in, weights, const_in, bucket_in, par1_in, par2_in, table_in, rpb_in, out):
    with ExitStack() as ctx:
        def sb(name, shape, dtype=F32):
            return ctx.enter_context(nc.sbuf_tensor(name, shape, dtype))

        def sem(name):
            return ctx.enter_context(nc.semaphore(name))

        bias_scratch = nc.dram_tensor("bias_scratch", (12, P, SEQ + P), F32, kind="Internal").ap()

        xT = sb("xT", [P, NC, SEQ])
        mixT = sb("mixT", [P, NC, SEQ])
        opH = sb("opH", [P, NC, SEQ], F32R)
        opL = sb("opL", [P, NC, SEQ], F32R)
        wraw = sb("wraw", [P, SLOTS, PIECE])
        wH = sb("wH", [P, SLOTS, PIECE], F32R)
        wL = sb("wL", [P, SLOTS, PIECE], F32R)
        const = sb("const", [P, CONST_W])
        par1 = sb("par1", [P, PAR1_W])
        par2 = sb("par2", [P, PAR2_W])
        with ExitStack() as hidden_ctx:
            hidH = hidden_ctx.enter_context(nc.sbuf_tensor("hidH", [P, PART, SEQ], F32R))
            hidL = hidden_ctx.enter_context(nc.sbuf_tensor("hidL", [P, PART, SEQ], F32R))
        with ExitStack() as blocks_ctx:
            blocks_ctx.enter_context(nc.sbuf_tensor("below_blocks", [P, BLOCKS_AT], F32))
            blkH = blocks_ctx.enter_context(nc.sbuf_tensor("blkH", [P, CMP_LEN + 1, HEAD], F32R))
            blkL = blocks_ctx.enter_context(nc.sbuf_tensor("blkL", [P, CMP_LEN + 1, HEAD], F32R))
        big = sb("big", [P, 32 * SEQ])
        rows = sb("rows", [P, 2, SEQ])
        small = sb("small", [P, 1024])

        def c(name):
            return const[:, CONST[name][0]:CONST[name][1]]

        def p1(name):
            return par1[:, PAR1[name][0]:PAR1[name][1]]

        def p2(name):
            return par2[:, PAR2[name][0]:PAR2[name][1]]

        ident, ones = c("ident"), c("ones")
        space = big[:, :].rearrange("p (f s) -> p f s", s=SEQ)
        place = [0]

        def cut(n):
            place[0] += n
            assert place[0] <= 32 * SEQ
            return big[:, place[0] - n:place[0]]

        qT, kT, vT = cut(SEQ), cut(SEQ), cut(SEQ)
        v_nat = cut(SEQ).rearrange("p (t d) -> p t d", t=NT)
        side = cut(8 * SEQ).rearrange("p (i s) -> p i s", i=8)
        score_at = place[0]
        assert score_at == BLOCKS_AT
        score = cut(2 * SEQ).rearrange("p (b s) -> p b s", b=2)
        prob = cut(4 * SEQ).rearrange("p (b s) -> p b s", b=4)
        probT = cut(2 * SEQ).rearrange("p (b s) -> p b s", b=2)
        bias_at = place[0]
        pair_bias = cut(2 * NA_BIAS).rearrange("p (h k) -> p h k", h=2)
        cuts = (0, GRID_H * NA_REACH, GRID_H * (NA_REACH + NA_EDGE), NA_BIAS)
        inner_bias, first_bias, last_bias = (
            pair_bias[:, :, a:b].rearrange("p h (r k) -> p h r k", r=GRID_H) for a, b in zip(cuts, cuts[1:]))
        raw_size = NA_HEADS * GRID_H * NA_REACH
        assert place[0] + raw_size <= 32 * SEQ
        rpb_raw = big[:, place[0]:place[0] + raw_size].rearrange("p (h r k) -> p h r k", h=NA_HEADS, r=GRID_H)
        sel_bias = cut(2 * SEQ).rearrange("p (b s) -> p b s", b=2)
        vs_nat = cut(SEQ).rearrange("p (t d) -> p t d", t=NT)
        vw_nat = cut(SEQ).rearrange("p (t d) -> p t d", t=NT)
        blocks = cut(CMP_LEN * CMP_PAD).rearrange("p (l n) -> p l n", l=CMP_LEN)
        pcT = cut(SEQ)
        assert place[0] <= 32 * SEQ
        def flat2(a):
            return a[:, :, :].rearrange("p t d -> p (t d)")

        sb_width = P * NT * (NT + 1) // 2
        sb_z_buf = [big[:, score_at + h * sb_width:score_at + (h + 1) * sb_width] for h in range(2)]
        sb_t = [big[:, bias_at + h * sb_width:bias_at + (h + 1) * sb_width] for h in range(2)]

        def sb_unit(bufs, hh, t):
            at = P * t * (t + 1) // 2
            return bufs[hh][:, at:at + (t + 1) * P]

        df_probs = [(prob[:, 0, :], prob[:, 1, :]), (prob[:, 2, :], prob[:, 3, :]),
                    (sel_bias[:, 0, :], sel_bias[:, 1, :]), (flat2(vs_nat), flat2(vw_nat))]
        t5_nsa = side[:, 4:8, :]
        bucket = score[:, :, :].rearrange("p b s -> p (b s)")[0:N_BUCKETS + 1, 0:SEQ + P]
        vec = prob[:, :, :].rearrange("p b s -> p (b s)")[0:12, 0:SEQ + P]
        squares = space[:, 16:16 + NC, :]
        evac = space[:, 24:26, :]
        raw = space[:, 26:28, :]
        chunk_squares = space[:, 28:30, :]
        stat = rows[:, 1, :]

        place2 = [0]

        def bit(n):
            place2[0] += n
            assert place2[0] <= 1024
            return small[:, place2[0] - n:place2[0]]

        negmax, denom, recip = bit(STATS), bit(STATS), bit(STATS)
        lam2, lam_pair, lam_eps, lam_tmp, subln = bit(2), bit(2), bit(1), bit(2), bit(1)
        lam_scale, lam_one = lam_pair[:, 0:1], lam_pair[:, 1:2]
        gates = bit(NT * 12).rearrange("p (t g) -> p t g", t=NT)
        kc_diag = bit(2 * CMP_PAD)
        imp = bit(NT * N_SLC).rearrange("p (t j) -> p t j", t=NT)
        rank = bit(NT * N_SLC).rearrange("p (t j) -> p t j", t=NT)
        sel_neg = bit(NT * N_SLC).rearrange("p (t j) -> p t j", t=NT)
        cmax, csum = bit(NT * HEADS), bit(NT * HEADS)
        eps_norm, eps_ln, one_col = bit(1), bit(1), bit(1)
        lam_prod = bit(2 * DIFF_HALF)
        gx = bit(4 * CMP_PAD).rearrange("p (g n) -> p g n", g=4)
        gt = bit(4 * CMP_PAD).rearrange("p (g n) -> p g n", g=4)
        h1v = sb("h1v", [P, 2, HEADS, CMP_PAD])
        vc_diag = sb("vc_diag", [P, GROUP])
        vc_pair = sb("vc_pair", [P, P])
        cmp_bias = sb("cmp_bias", [P, NT, HEADS, CMP_PAD])
        cmp_mask = sb("cmp_mask", [P, NT, HEADS, CMP_PAD])
        pc = sb("pc", [P, NT, HEADS, CMP_PAD])
        pcg = sb("pcg", [P, NT, HEADS, CMP_PAD])
        beats = score[:, 0, :].rearrange("p (b n) -> p b n", b=2)
        tab33 = sb("tab33", [N_BUCKETS + 1, 12])

        def bank(name):
            return ctx.enter_context(nc.psum_tensor(name, [P, SEQ], F32))

        acc = [bank("acc0"), bank("acc1")]
        scp = [bank("score0"), bank("score1")]
        trp = [bank("trans0"), bank("trans1")]
        outp, spare = bank("outp"), bank("spare")

        w_loaded = [sem(f"w_loaded{s}") for s in range(SLOTS)]
        pieces_done = sem("pieces_done")
        evacuated = [sem("evacuated0"), sem("evacuated1")]
        const_rest = sem("const_rest")
        const_loaded, x_loaded, table_loaded = sem("const_loaded"), sem("x_loaded"), sem("table_loaded")
        par_loaded, rpb_loaded = sem("par_loaded"), sem("rpb_loaded")
        split_done = sem("split_done")
        op_raw, op_hi, op_lo, op_lo_pool = sem("op_raw"), sem("op_hi"), sem("op_lo"), sem("op_lo_pool")
        hid_ready, relu_ready = sem("hid_ready"), sem("relu_ready")
        nsa_bias_stored = sem("nsa_bias_stored")
        bias_stored, t5_loaded, stored = sem("bias_stored"), sem("t5_loaded"), sem("stored")
        pe_end, act_end, dve_end, pool_end = sem("pe_end"), sem("act_end"), sem("dve_end"), sem("pool_end")
        x_turned, vec_ready, vec_copied, tab_set, zeroed = (sem("x_turned"), sem("vec_ready"), sem("vec_copied"),
                                                            sem("tab_set"), sem("zeroed"))
        squared, summed, rstd_ready = sem("squared"), sem("summed"), sem("rstd_ready")
        stat_ready, ln_stat_ready = sem("stat_ready"), sem("ln_stat_ready")
        ln_summed, centred, ln_squared, ln_var, ln_rstd, ln_scaled = (
            sem("ln_summed"), sem("centred"), sem("ln_squared"), sem("ln_var"), sem("ln_rstd"), sem("ln_scaled"))
        lam_dots, lam_exps = sem("lam_dots"), sem("lam_exps")
        qk_ready, v_ready = sem("qk_ready"), sem("v_ready")
        v_turned, v_copied = sem("v_turned"), sem("v_copied")
        pair_ready = sem("pair_ready")
        bias_ready = sem("bias_ready")
        scores_ready, biased, exped, normed = sem("scores_ready"), sem("biased"), sem("exped"), sem("normed")
        sel_ready = sem("sel_ready")
        transposed, pt_ready, pv_done = sem("transposed"), sem("pt_ready"), sem("pv_done")
        sb_scores, sb_z, sb_log, sb_arg, sb_prob = (sem("sb_scores"), sem("sb_z"), sem("sb_log"), sem("sb_arg"),
                                                    sem("sb_prob"))
        df_weight, df_sq, df_sum, df_rstd = sem("df_weight"), sem("df_sq"), sem("df_sum"), sem("df_rstd")
        hid_out, hid_turned, low_cleared = sem("hid_out"), sem("hid_turned"), sem("low_cleared")
        ns_turned, blocks_ready, hid_copied, hid_sq, hid_poly, hid_exp, gelu_ready = (
            sem("ns_turned"), sem("blocks_ready"), sem("hid_copied"), sem("hid_sq"),
            sem("hid_poly"), sem("hid_exp"), sem("gelu_ready"))
        cmp_kv, cmp_copied, cmp_scores, cmp_shift, cmp_exp, pc_ready, pc_turned, pc_copied, imp_ready = (
            sem("cmp_kv"), sem("cmp_copied"), sem("cmp_scores"), sem("cmp_shift"), sem("cmp_exp"),
            sem("pc_ready"), sem("pc_turned"), sem("pc_copied"), sem("imp_ready"))
        gate_exp = sem("gate_exp")
        silu_ready = sem("silu_ready")
        pooled, pool_mm = sem("pooled"), sem("pool_mm")
        out_turned, out_copied = sem("out_turned"), sem("out_copied")

        def big_pad(n, wide):
            return prob[:, :, :].rearrange("p b s -> p (b s)")[:, n * wide:(n + 1) * wide]

        block = ctx.enter_context(nc.Block())

        def settle(eng, *waits):
            waits = [(s, eng.compute_val(value)) for s, value in waits]
            eng.wait_ge(const_loaded, 16)
            for s, value in waits:
                eng.wait_ge(s, value)

        def begin(eng, stage):
            settle(eng, *[(end, stage) for end in (pe_end, act_end, dve_end, pool_end)])

        def finish(eng, end):
            eng.drain().then_inc(end, 1)

        @block.sync
        def _(sp):
            first = CONST["neg_rows"][1]
            sp.dma_start(const[:, 0:first], const_in[:, 0:first]).then_inc(const_loaded, 16)
            sp.dma_start(space[:, 0:2 * NT, :].rearrange("p (t h) s -> p t (h s)", t=NT),
                         x_in.rearrange("(t p) d -> p t d", p=P)).then_inc(x_loaded, 16)

            def piece(offset, width, slot, split):
                if split is not None:
                    sp.wait_ge(split_done, split)
                sp.dma_start(wraw[:, slot, 0:width], bass.AP(weights.tensor, offset, [[width, P], [1, width]])
                             ).then_inc(w_loaded[slot], 16)

            size = P * PIECE
            for s in range(SLOTS):
                piece(s * size, PIECE, s, None)
            sp.dma_start(const[:, first:], const_in[:, first:]).then_inc(const_rest, 16)
            with sp.Fori(1, DEPTH * ROUNDS1) as r:
                for s in range(SLOTS):
                    piece(r * (SLOTS * size) + s * size, PIECE, s, r * SLOTS + s - SLOTS + 1)
            ffn = []
            for n, r_gu in zip(PARTS2, R_GU):
                ffn += [(r_gu, PIECE), (R_DOWN, n * P)]
            runs = ffn + [(1 + NA_PAIRS + R_OUT, PIECE)] + ffn
            layer_size = sum(k * SLOTS * P * w for k, w in runs)
            with sp.Fori(0, DEPTH) as layer:
                at, rounds = DEPTH * ROUNDS1 * SLOTS * size, ROUND_B2
                for k, w in runs:
                    with sp.Fori(0, k) as r:
                        for s in range(SLOTS):
                            piece(layer * layer_size + r * (SLOTS * P * w) + (at + s * P * w), w, s,
                                  layer * (ROUNDS2 * SLOTS) + r * SLOTS + ((rounds - 1) * SLOTS + s + 1))
                    at += k * SLOTS * P * w
                    rounds += k
            for s in range(SLOTS):
                last = DEPTH * (ROUNDS1 * SLOTS * size + layer_size)
                piece(last + s * size, PIECE, s, (ROUND_B2 + DEPTH * ROUNDS2 - 1) * SLOTS + s + 1)

        @block.tensor
        def _(pe):
            def product(slot, rnd, accum, n=NC, hi=opH, lo=opL, ready=None):
                pe.wait_ge(split_done, rnd * SLOTS + slot + 1)
                for k in range(n):
                    if ready is not None:
                        pe.wait_ge(*ready(k))
                    w = slice(k * P, (k + 1) * P)
                    pe.matmul(accum[:, :], wH[:, slot, w], hi[:, k, :], start=k == 0, stop=False)
                    pe.matmul(accum[:, :], wH[:, slot, w], lo[:, k, :], start=False, stop=False)
                    mm = pe.matmul(accum[:, :], wL[:, slot, w], hi[:, k, :], start=False, stop=k == n - 1)
                mm.then_inc(pieces_done, 1)

            def group(j, rnd, gp, n=NC, hi=opH, lo=opL, ready=None):
                pe.wait_ge(evacuated[j % 2], gp + j // 2)
                product(j, rnd, acc[j % 2], n, hi, lo, ready)

            def four(rnd, gp, n=NC, hi=opH, lo=opL, ready=None):
                for j in range(SLOTS):
                    group(j, rnd, gp, n, hi, lo, ready if j == 0 else None)

            def down(rounds, gps, hids, n):
                for r in range(R_DOWN):
                    four(r + rounds, r * 2 + gps, n, hidH, hidL,
                         (lambda k: (hid_ready, hids + k + 1)) if r == 0 else None)

            def op_ready(n):
                return lambda k: ((op_lo, op_lo_pool)[k % 2], n * (NC // 2) + (k // 2 + 1))

            def norm(n):
                settle(pe, (stat_ready, n + 1))
                pe.matmul(scp[0][:, :], ones, stat, start=True, stop=True).then_inc(summed, 1)
                finish(pe, pe_end)

            def layer_norm(n):
                settle(pe, (ln_stat_ready, n + 1))
                pe.matmul(scp[0][:, :], ones, stat, start=True, stop=True).then_inc(ln_summed, 1)
                for k in range(NC):
                    pe.wait_ge(ln_squared, n * NC + k + 1)
                    mm = pe.matmul(scp[1][:, :], ones, squares[:, k, :], start=k == 0, stop=k == NC - 1)
                mm.then_inc(ln_var, 1)
                finish(pe, pe_end)

            def project(it, rnd, gp, ready=None):
                group(0, rnd, gp, ready=ready)
                group(1, rnd, gp)
                pe.wait_ge(qk_ready, it + 1)

                def rest():
                    pe.wait_ge(v_ready, it + 1)
                    for t in range(NT):
                        mm = pe.transpose(spare[:, t * P:(t + 1) * P], vT[:, t * P:(t + 1) * P], ident)
                    mm.then_inc(v_turned, 1)
                    group(3, rnd, gp)
                    pe.wait_ge(v_copied, it + 1)

                return {1: lambda: group(2, rnd, gp), 2: rest}

            def turn_probs(m, width, tb):
                if m >= 2:
                    pe.wait_ge(pt_ready, tb + m - 1)
                for j in range(width // P):
                    mm = pe.transpose(trp[m % 2][:, j * P:(j + 1) * P], m_prob[0][:, j * P:(j + 1) * P], ident)
                mm.then_inc(transposed, 1)

            m_prob = [None]

            def apply_values(m, tb, hh, t, width, values, first=True, last=True, extra=None):
                pe.wait_ge(pt_ready, tb + m + 1)
                o = outp[HEAD * hh:HEAD * (hh + 1), t * P:(t + 1) * P]
                if extra is not None:
                    pe.matmul(o, extra[0], extra[1], start=True, stop=False)
                n = width // P
                for j in range(n):
                    mm = pe.matmul(o, values(j), probT[:, m % 2, j * P:(j + 1) * P],
                                   start=first and extra is None and j == 0, stop=last and j == n - 1)
                mm.then_inc(pv_done, 1)

            def softmax_maps(mb, nb, tb, maps, after={}):
                n = len(maps)
                for i in range(n + LAG + 1):
                    if i < n:
                        q, k, width = maps[i][:3]
                        if i >= 2:
                            pe.wait_ge(biased, mb + i - 1)
                        pe.matmul(scp[i % 2][:, 0:width], q, k, start=True, stop=True).then_inc(scores_ready, 1)
                    turned, applied = i - LAG, i - LAG - 1
                    if 0 <= turned < n:
                        pe.wait_ge(normed, nb + turned + 1)
                        m_prob[0] = prob[:, turned % 4, :]
                        turn_probs(turned, maps[turned][2], tb)
                    if applied >= 0:
                        _, _, width, args = maps[applied]
                        apply_values(applied, tb, width=width, **args)
                    if i in after:
                        after[i]()

            def half_of(a, hh):
                return a[HEAD * hh:HEAD * (hh + 1)]

            def q_tile(hh, t):
                return half_of(qT, hh)[:, t * P:(t + 1) * P]

            def v_head(hh):
                return lambda j: v_nat[:, j, HEAD * hh:HEAD * (hh + 1)]

            def stick_breaking(layer, pair):
                it = layer * 6 + pair
                after = project(it, layer * ROUNDS1 + pair + ROUND_SB, layer * GPS1 + pair * 2 + GP_SETUP,
                                op_ready(layer * SPLITS1))
                ub, tb = layer * (2 * U) + pair * U, layer * TRS1 + pair * U + TR_SB
                units = [(hh, t) for hh in range(2) for t in range(NT)]
                for i, (hh, t) in enumerate(units):
                    if i >= 2:
                        pe.wait_ge(sb_z, ub + i - 1)
                    pe.matmul(scp[i % 2][:, 0:(t + 1) * P], q_tile(hh, t), half_of(kT, hh)[:, 0:(t + 1) * P],
                              start=True, stop=True).then_inc(sb_scores, 1)
                for step in (1, 2):
                    after[step]()
                for i in range(U + 1):
                    if i < U:
                        hh, t = units[i]
                        if t == 0:
                            pe.wait_ge(sb_prob, layer * 4 + pair * 2 + hh + 1)
                        m_prob[0] = sb_unit(sb_t, hh, t)
                        turn_probs(i, (t + 1) * P, tb)
                    if i >= 1:
                        hh, t = units[i - 1]
                        apply_values(i - 1, tb, hh, t, (t + 1) * P, v_head(hh))
                finish(pe, pe_end)

            def moba(layer, pair):
                it = layer * 6 + pair + 2
                after = project(it, layer * ROUNDS1 + pair + ROUND_MB,
                                layer * GPS1 + pair * 2 + (GP_SETUP + 2 * R_ATT))
                softmax_maps(layer * MAPS1 + pair * U + MAPS_MB, layer * NORMS1 + pair * U + NORM_MB,
                             layer * TRS1 + pair * U + TR_MB,
                             [(q_tile(hh, t), half_of(kT, hh)[:, 0:(t + 1) * P], (t + 1) * P,
                               dict(hh=hh, t=t, values=v_head(hh))) for hh in range(2) for t in range(NT)], after)
                finish(pe, pe_end)

            def differential(layer, pair):
                it = layer * 6 + pair + 4
                after = project(it, layer * ROUNDS1 + pair + ROUND_DF,
                                layer * GPS1 + pair * 2 + (GP_SETUP + 4 * R_ATT))
                mb = layer * MAPS1 + pair * (2 * U) + MAPS_DF
                tb = layer * TRS1 + pair * U + TR_DF
                ub = layer * (2 * U) + pair * U
                units = [(hh, t) for hh in range(2) for t in range(NT)]
                for i in range(U + LAG + 1):
                    if i < U:
                        hh, t = units[i]
                        for half in range(2):
                            m = 2 * i + half
                            at = HEAD * hh + DIFF_HALF * half
                            if m >= 2:
                                pe.wait_ge(biased, mb + m - 1)
                            pe.matmul(scp[half][:, 0:(t + 1) * P], qT[at:at + DIFF_HALF, t * P:(t + 1) * P],
                                      kT[at:at + DIFF_HALF, 0:(t + 1) * P], start=True, stop=True
                                      ).then_inc(scores_ready, 1)
                    turned, applied = i - LAG, i - LAG - 1
                    if 0 <= turned < U:
                        pe.wait_ge(df_weight, ub + turned + 1)
                        m_prob[0] = df_probs[turned % 4][0]
                        turn_probs(turned, (units[turned][1] + 1) * P, tb)
                    if applied >= 0:
                        hh, t = units[applied]
                        apply_values(applied, tb, hh, t, (t + 1) * P, v_head(hh))
                    if i in after:
                        after[i]()
                pe.wait_ge(df_sq, layer * PAIRS + pair + 1)
                pe.matmul(spare[:, :], c("head_ones"), score[:, 0, :], start=True, stop=True).then_inc(df_sum, 1)
                finish(pe, pe_end)

            def nsa_select(layer):
                rnd = layer * ROUNDS1 + ROUND_CMP
                for i, to in ((1, acc[0]), (2, acc[1]), (3, spare)):
                    for t in range(NT):
                        mm = pe.transpose(to[:, t * P:(t + 1) * P], side[:, i, t * P:(t + 1) * P], ident)
                    mm.then_inc(ns_turned, 1)
                pe.wait_ge(blocks_ready, layer + 1)
                per = PIECE // CMP_HIDDEN
                flatH, flatL = (b[:, :, :].rearrange("p l n -> p (l n)") for b in (blkH, blkL))
                for n in range(R_CMP * SLOTS):
                    s = n % SLOTS
                    pe.wait_ge(split_done, (rnd + n // SLOTS) * SLOTS + s + 1)
                    for k in range(per):
                        l = n * per + k
                        w = slice(k * CMP_HIDDEN, (k + 1) * CMP_HIDDEN)
                        b = slice(l * HEAD, l * HEAD + P)
                        to = scp[0][:, 0:CMP_HIDDEN]
                        pe.matmul(to, flatH[:, b], wH[:, s, w], start=l == 0, stop=False)
                        pe.matmul(to, flatH[:, b], wL[:, s, w], start=False, stop=False)
                        mm = pe.matmul(to, flatL[:, b], wH[:, s, w], start=False, stop=l == CMP_LEN - 1)
                    mm.then_inc(pieces_done, 1)
                settle(pe, (hid_out, layer + 1))
                for h in range(2):
                    mm = pe.transpose(scp[1][:, h * HEAD:(h + 1) * HEAD], rows[0:HEAD, 1, h * P:(h + 1) * P],
                                      ident[0:HEAD, 0:HEAD])
                mm.then_inc(hid_turned, 1)
                pe.wait_ge(gelu_ready, layer * 2 + 2)
                for half in range(2):
                    for h in range(2):
                        pe.matmul(half_of(scp[0], half)[:, 0:N_CMP], p1("w2k")[:, h * HEAD:(h + 1) * HEAD],
                                  gx[:, h, 0:N_CMP], start=h == 0, stop=h == 1)
                for h in range(2):
                    mm = pe.matmul(scp[1][:, 0:HEAD], h1v[:, h, :, :].rearrange("p a b -> p (a b)"),
                                   p1("w2v")[:, h * HEAD:(h + 1) * HEAD], start=h == 0, stop=h == 1)
                mm.then_inc(cmp_kv, 1)
                pe.wait_ge(cmp_copied, layer + 1)
                for t in range(NT):
                    for pair in range(PAIRS):
                        at = (t * PAIRS + pair) * 2 * CMP_PAD
                        mm = pe.matmul(trp[0][:, at:at + 2 * CMP_PAD], side[:, 4 + pair, t * P:(t + 1) * P],
                                       kc_diag[:, :], start=True, stop=True)
                mm.then_inc(cmp_scores, 1)
                for n, src, to in ((0, pc, trp[1]), (1, pcg, trp[0])):
                    pe.wait_ge(pc_ready, layer * 2 + n + 1)
                    for t in range(NT):
                        mm = pe.transpose(to[:, t * P:(t + 1) * P], src[:, t, :, :].rearrange("p a b -> p (a b)"),
                                          ident)
                    mm.then_inc(pc_turned, 1)
                    if n == 0:
                        pe.wait_ge(pc_copied, layer * 2 + 1)
                        for t in range(NT):
                            mm = pe.matmul(scp[0][:, t * N_SLC:(t + 1) * N_SLC], pcT[:, t * P:(t + 1) * P],
                                           c("cover"), start=True, stop=True)
                        mm.then_inc(imp_ready, 1)
                finish(pe, pe_end)

            def nsa_pair(layer, pair):
                pe.wait_ge(pair_ready, layer * PAIRS + pair + 1)
                maps = []
                for hh in range(2):
                    for t in range(NT):
                        cols = slice(0, (t + 1) * P)
                        maps.append((q_tile(hh, t), half_of(side[:, 1, :], hh)[:, cols], (t + 1) * P,
                                     dict(hh=hh, t=t, values=lambda j: vs_nat[:, j, HEAD:2 * HEAD], last=False,
                                          extra=(vc_pair[:, HEAD * hh:HEAD * (hh + 1)],
                                                 pcT[:, t * P:(t + 1) * P]))))
                        maps.append((q_tile(hh, t), half_of(side[:, 2, :], hh)[:, cols], (t + 1) * P,
                                     dict(hh=hh, t=t, values=lambda j: vw_nat[:, j, HEAD:2 * HEAD], first=False)))
                softmax_maps(layer * MAPS1 + pair * (2 * U) + MAPS_NS, layer * NORMS1 + pair * (2 * U) + NORM_NS,
                             layer * TRS1 + pair * (2 * U) + TR_NS, maps)
                finish(pe, pe_end)

            def neighbourhood(layer, pair):
                it = layer * NA_PAIRS + pair + DEPTH * 6
                after = project(it, layer * ROUNDS2 + pair + (ROUND_B2 + ROUND_NA),
                                layer * GPS2 + pair * 2 + (GP_B2 + GP_NA))
                softmax_maps(layer * (4 * U) + pair * U + DEPTH * MAPS1, layer * (4 * U) + pair * U + DEPTH * NORMS1,
                             layer * (4 * U) + pair * U + DEPTH * TRS1,
                             [(q_tile(hh, t), half_of(kT, hh)[:, k0 * P:(k0 + n) * P], n * P,
                               dict(hh=hh, t=t, values=lambda j, hh=hh, k0=k0: v_head(hh)(k0 + j)))
                              for hh in range(2) for t, (k0, n) in enumerate(NA_TILES)], after)
                finish(pe, pe_end)

            def ffn(split, rounds, gps, hids):
                for part, (r_gu, n) in enumerate(zip(R_GU, PARTS2)):
                    with pe.Fori(0, r_gu) as r:
                        four(r + rounds, r * 2 + gps, ready=op_ready(split) if part == 0 else None)
                    down(rounds + r_gu, gps + n, hids, n)
                    rounds, gps, hids = rounds + r_gu + R_DOWN, gps + n + NC // 2, hids + n
                finish(pe, pe_end)

            pe.wait_ge(const_loaded, 16)
            pe.wait_ge(x_loaded, 16)
            for k in range(NC):
                if k >= 2:
                    pe.wait_ge(evacuated[k % 2], k // 2)
                for t in range(NT):
                    at = t * D_MODEL + k * P
                    mm = pe.transpose(acc[k % 2][:, t * P:(t + 1) * P], big[:, at:at + P], ident)
                mm.then_inc(x_turned, 1)
            pe.wait_ge(table_loaded, 32)
            pe.matmul(scp[0][0:12, 0:SEQ], tab33[:, :], bucket[:, 0:SEQ], start=True, stop=True)
            pe.matmul(scp[1][0:12, 0:P], tab33[:, :], bucket[:, SEQ:SEQ + P], start=True, stop=True
                      ).then_inc(vec_ready, 1)
            pe.wait_ge(vec_copied, 1)
            finish(pe, pe_end)

            with pe.Fori(0, DEPTH) as layer:
                stage = layer * STAGES1 + 1
                norm(layer * 2)
                with pe.Fori(0, PAIRS) as pair:
                    stick_breaking(layer, pair)
                with pe.Fori(0, PAIRS) as pair:
                    moba(layer, pair)
                with pe.Fori(0, PAIRS) as pair:
                    differential(layer, pair)
                begin(pe, stage + ST_NSA)
                nsa_select(layer)
                with pe.Fori(0, PAIRS) as pair:
                    begin(pe, stage + pair + ST_NSP)
                    nsa_pair(layer, pair)
                with pe.Fori(0, R_OUT) as r:
                    four(layer * ROUNDS1 + r + ROUND_OUT, layer * GPS1 + r * 2 + (GP_SETUP + GP_OUT),
                         ready=op_ready(layer * SPLITS1 + 1))
                finish(pe, pe_end)
                norm(layer * 2 + 1)
                with pe.Fori(0, PARTS1) as part:
                    rounds = layer * ROUNDS1 + part * R_PART1 + ROUND_MLP
                    gps = layer * GPS1 + part * GP_PART1 + (GP_SETUP + GP_MLP)
                    with pe.Fori(0, R_UP) as r:
                        four(r + rounds, r * 2 + gps, ready=op_ready(layer * SPLITS1 + 2))
                    down(rounds + R_UP, gps + PART // 2, layer * (PARTS1 * PART) + part * PART, PART)
                finish(pe, pe_end)
            norm(2 * DEPTH)
            with pe.Fori(0, DEPTH) as layer:
                stage = layer * STAGES2 + ST_B2
                rounds, gps = layer * ROUNDS2 + ROUND_B2, layer * GPS2 + GP_B2
                hids = layer * (2 * sum(PARTS2)) + DEPTH * PARTS1 * PART
                ffn(layer * SPLITS2 + (SPLIT_B2 - 1), rounds, gps, hids)
                layer_norm(layer * 3)
                four(rounds + ROUND_PROJ, gps + GP_PROJ, ready=op_ready(layer * SPLITS2 + SPLIT_B2))
                finish(pe, pe_end)
                with pe.Fori(0, NA_PAIRS) as pair:
                    neighbourhood(layer, pair)
                begin(pe, stage + ST_POOL)
                for i in range(2):
                    settle(pe, (pooled, layer * 2 + i + 1))
                    for g in range(2):
                        mm = pe.matmul(half_of(scp[i], g)[:, :], half_of(p2("pool_w"), g)[:, i * HEAD:(i + 1) * HEAD],
                                       half_of(side[:, i, :], g), start=True, stop=True)
                    mm.then_inc(pool_mm, 1)
                finish(pe, pe_end)
                with pe.Fori(0, R_OUT) as r:
                    four(rounds + r + ROUND_OUT2, gps + r * 2 + GP_OUT2,
                         ready=op_ready(layer * SPLITS2 + (SPLIT_B2 + 1)))
                finish(pe, pe_end)
                layer_norm(layer * 3 + 1)
                ffn(layer * SPLITS2 + (SPLIT_B2 + 2), rounds + ROUND_FFN2, gps + GP_FFN2, hids + sum(PARTS2))
                layer_norm(layer * 3 + 2)
            begin(pe, ST_END)
            for n in range(2 * NT):
                t, half = n // 2, n % 2
                if n >= 2:
                    pe.wait_ge(out_copied, n - 1)
                for k in range(NC // 2):
                    mm = pe.transpose(acc[n % 2][:, k * P:(k + 1) * P],
                                      xT[:, half * NC // 2 + k, t * P:(t + 1) * P], ident)
                mm.then_inc(out_turned, 1)

        @block.scalar
        def _(act):
            def copy(to, src, scale=1.0):
                return act.activation(to, src, ACT.Copy, scale=scale)

            def power(rs, src, scale, eps, n_ready):
                act.activation(rs, src, ACT.Ln, scale=scale, bias=eps)
                act.drain()
                act.activation(rs, rs, ACT.Exp, scale=-0.5).then_inc(n_ready, 1)

            def op_high(src, k, n=None):
                if n is not None:
                    act.wait_ge(op_raw, n * NC + k + 1)
                copy(opH[:, k, :], src[:, k, :]).then_inc(op_hi, 1)

            def norm(n):
                act.wait_ge(summed, n + 1)
                power(rows[:, 0, :], scp[0][:, :], 1.0 / D_MODEL, eps_norm, rstd_ready)

            def norm_high(n, to):
                for k in range(NC):
                    op_high(to, k, n)

            def layer_norm(n):
                for k in range(NC):
                    act.wait_ge(centred, n * NC + k + 1)
                    act.activation(squares[:, k, :], xT[:, k, :], ACT.Square).then_inc(ln_squared, 1)
                act.wait_ge(ln_var, n + 1)
                power(rows[:, 0, :], scp[1][:, :], 1.0 / D_MODEL, eps_ln, ln_rstd)

            def shift(n, which):
                for k in range(NC):
                    act.wait_ge(ln_scaled, n * NC + k + 1)
                    bias = p2("ln_b")[:, which * NC + k:which * NC + k + 1]
                    act.activation(opH[:, k, :], xT[:, k, :], ACT.Identity, bias=bias)
                    act.activation(xT[:, k, :], xT[:, k, :], ACT.Identity, bias=bias).then_inc(op_hi, 1)
                finish(act, act_end)

            def project(done, scale, to_side, side_scale, it, by_column=False):
                def out_of(j, to, s, order=None):
                    settle(act, (pieces_done, done + j + 1))
                    src = acc[j % 2][:, :]
                    if by_column and order == "tiles":
                        src = src.rearrange("p (r t c) -> p r t c", r=GRID_H, t=NT)
                        to = to.rearrange("p (t r c) -> p r t c", r=GRID_H, t=NT)
                    elif by_column and order == "columns":
                        src = src.rearrange("p (r c) -> p r c", r=GRID_H)
                        to = to.rearrange("p (c r) -> p r c", r=GRID_H)
                    return copy(to, src, s).then_inc(evacuated[j % 2], 1)

                out_of(0, qT, scale, "tiles")
                out_of(1, kT, 1.0, "columns")
                act.drain().then_inc(qk_ready, 1)

                def value():
                    out_of(2, vT, 1.0, "columns")
                    act.drain().then_inc(v_ready, 1)

                def by_token():
                    act.wait_ge(v_turned, it + 1)
                    copy(flat2(v_nat), spare[:, :]).then_inc(v_copied, 1)

                def fourth():
                    out_of(3, side[:, to_side, :].rearrange("p a s -> p (a s)"), side_scale)

                return {1: value, 2: by_token, 3: fourth}

            def probs_out(m, width, tb):
                if m >= 2:
                    act.wait_ge(pv_done, tb + m - 1)
                act.wait_ge(transposed, tb + m + 1)
                copy(probT[:, m % 2, 0:width], trp[m % 2][:, 0:width]).then_inc(pt_ready, 1)

            def softmax_exp(m, width, mb, to):
                act.wait_ge(biased, mb + m + 1)
                act.activation(to[:, 0:width], score[:, m % 2, 0:width], ACT.Exp,
                               bias=negmax[:, m % STATS:m % STATS + 1], scale=-1.0,
                               accum_out=denom[:, m % STATS:m % STATS + 1]).then_inc(exped, 1)

            def softmax_maps(mb, tb, widths, after={}):
                n = len(widths)
                for i in range(n + LAG):
                    if i < n:
                        if i >= 4:
                            act.wait_ge(transposed, tb + i - 3)
                        softmax_exp(i, widths[i], mb, prob[:, i % 4, :])
                    if i >= LAG:
                        probs_out(i - LAG, widths[i - LAG], tb)
                    if i in after:
                        after[i]()

            causal = [(t + 1) * P for hh in range(2) for t in range(NT)]

            def stick_breaking(layer, pair):
                after = project(layer * (ROUNDS1 * SLOTS) + pair * SLOTS + ROUND_SB * SLOTS, HEAD ** -0.5,
                                bass.ds(pair, 1), 1.0, layer * 6 + pair)
                ub, tb = layer * (2 * U) + pair * U, layer * TRS1 + pair * U + TR_SB
                heads = layer * 4 + pair * 2
                for hh in range(2):
                    act.wait_ge(sb_z, ub + (hh + 1) * NT)
                    act.activation(sb_t[hh], sb_z_buf[hh], ACT.Abs)
                    act.drain()
                    act.activation(sb_t[hh], sb_t[hh], ACT.Exp, scale=-1.0)
                act.drain()
                for hh in range(2):
                    act.activation(sb_t[hh], sb_t[hh], ACT.Ln, bias=one_col).then_inc(sb_log, 1)
                after[1]()
                after[2]()

                def weights_of(hh):
                    act.wait_ge(sb_arg, heads + hh + 1)
                    act.activation(sb_t[hh], sb_t[hh], ACT.Exp).then_inc(sb_prob, 1)

                weights_of(0)
                after[3]()
                for i in range(U):
                    probs_out(i, causal[i], tb)
                    if i == 1:
                        weights_of(1)
                finish(act, act_end)

            def moba(layer, pair):
                after = project(layer * (ROUNDS1 * SLOTS) + pair * SLOTS + ROUND_MB * SLOTS, HEAD ** -0.5,
                                bass.ds(pair + 2, 1), 1.0, layer * 6 + pair + 2)
                softmax_maps(layer * MAPS1 + pair * U + MAPS_MB, layer * TRS1 + pair * U + TR_MB, causal, after)
                finish(act, act_end)

            def differential(layer, pair):
                after = project(layer * (ROUNDS1 * SLOTS) + pair * SLOTS + ROUND_DF * SLOTS, DIFF_HALF ** -0.5,
                                bass.ds(pair + 4, 1), HEAD ** -0.5, layer * 6 + pair + 4)
                mb = layer * MAPS1 + pair * (2 * U) + MAPS_DF
                tb = layer * TRS1 + pair * U + TR_DF
                for i in range(U + LAG):
                    if i < U:
                        for half in range(2):
                            if i >= 4:
                                act.wait_ge(transposed, tb + i - 3)
                            softmax_exp(2 * i + half, causal[i], mb, df_probs[i % 4][half])
                    if i >= LAG:
                        probs_out(i - LAG, causal[i - LAG], tb)
                    if i in after:
                        after[i]()
                n = layer * PAIRS + pair
                act.wait_ge(pv_done, tb + U)
                act.activation(score[:, 0, :], outp[:, :], ACT.Square).then_inc(df_sq, 1)
                act.wait_ge(df_sum, n + 1)
                power(rows[:, 1, :], spare[:, :], 1.0 / HEAD, lam_eps, df_rstd)
                finish(act, act_end)

            def nsa_select(layer):
                act.wait_ge(ns_turned, layer * 3 + 1)
                copy(flat2(vs_nat), acc[0][:, :])
                copy(side[HEAD:P, 1, :], side[0:HEAD, 1, :])
                act.wait_ge(ns_turned, layer * 3 + 2)
                copy(flat2(vw_nat), acc[1][:, :])
                copy(side[HEAD:P, 2, :], side[0:HEAD, 2, :])
                act.wait_ge(ns_turned, layer * 3 + 3)
                act.activation(gates, spare[:, :].rearrange("p (t g) -> p t g", t=NT)[:, :, 0:12], ACT.Exp,
                               scale=-1.0).then_inc(gate_exp, 1)
                act.wait_ge(pieces_done, layer * (ROUNDS1 * SLOTS) + (ROUND_CMP + R_CMP) * SLOTS)
                copy(rows[0:HEAD, 1, 0:CMP_HIDDEN], scp[0][0:HEAD, 0:CMP_HIDDEN]).then_inc(hid_out, 1)
                act.wait_ge(hid_turned, layer + 1)
                for kv in range(2):
                    copy(gx[:, 2 * kv:2 * kv + 2, :],
                         scp[1][:, 0:2 * HEAD].rearrange("p (h k n) -> p h k n", h=2, k=2)[:, :, kv, :])
                act.drain().then_inc(hid_copied, 1)
                act.activation(gt[:, :, 0:N_CMP], gx[:, :, 0:N_CMP], ACT.Square).then_inc(hid_sq, 1)
                act.wait_ge(hid_poly, layer + 1)
                act.activation(gt[:, :, 0:N_CMP], gt[:, :, 0:N_CMP], ACT.Exp,
                               scale=-2.0 * math.sqrt(2.0 / math.pi)).then_inc(hid_exp, 1)
                act.wait_ge(cmp_kv, layer + 1)
                for half in range(2):
                    rows_of = slice(HEAD * half, HEAD * (half + 1))
                    copy(kc_diag[rows_of, CMP_PAD * half:CMP_PAD * half + N_CMP], scp[0][rows_of, 0:N_CMP])
                for h in range(HEADS):
                    at = slice(h * CMP_PAD, (h + 1) * CMP_PAD)
                    copy(vc_diag[at, h * HEAD:(h + 1) * HEAD], scp[1][at, 0:HEAD])
                act.drain().then_inc(cmp_copied, 1)
                act.wait_ge(cmp_shift, layer + 1)
                act.activation(pc[:, :, :, 0:N_CMP].rearrange("p t h n -> p (t h) n"),
                               pcg[:, :, :, 0:N_CMP].rearrange("p t h n -> p (t h) n"), ACT.Exp
                               ).then_inc(cmp_exp, 1)
                for n, src in enumerate((trp[1], trp[0])):
                    act.wait_ge(pc_turned, layer * 2 + n + 1)
                    if n == 1:
                        act.wait_ge(imp_ready, layer + 1)
                    copy(pcT, src[:, :]).then_inc(pc_copied, 1)
                finish(act, act_end)

            def nsa_pair(layer, pair):
                softmax_maps(layer * MAPS1 + pair * (2 * U) + MAPS_NS, layer * TRS1 + pair * (2 * U) + TR_NS,
                             [w for w in causal for _ in range(2)])
                finish(act, act_end)

            def neighbourhood(layer, pair):
                after = project(layer * (ROUNDS2 * SLOTS) + pair * SLOTS + (ROUND_B2 + ROUND_NA) * SLOTS, HEAD ** -0.5,
                                bass.ds(pair, 1), 1.0, layer * NA_PAIRS + pair + DEPTH * 6, by_column=True)
                softmax_maps(layer * (4 * U) + pair * U + DEPTH * MAPS1, layer * (4 * U) + pair * U + DEPTH * TRS1,
                             NA_KEYS * 2, after)
                finish(act, act_end)

            def ffn(stage, rounds, count):
                begin(act, stage)
                for r_gu, n in zip(R_GU, PARTS2):
                    with act.Fori(0, r_gu) as r:
                        for j in range(2):
                            settle(act, (pieces_done, r * SLOTS + rounds * SLOTS + 2 * j + 1),
                                   *[(evacuated[1], r * 2 + count)][j:])
                            act.activation(evac[:, j, :], acc[0][:, :], ACT.Silu).then_inc(evacuated[0], 1)
                            act.drain().then_inc(silu_ready, 1)
                    rounds, count = rounds + r_gu + R_DOWN, count + n + NC // 2
                finish(act, act_end)

            act.dma_start(bucket, bucket_in).then_inc(table_loaded, 16)
            act.dma_start(tab33[0:N_BUCKETS, :], table_in).then_inc(table_loaded, 16)
            act.wait_ge(const_loaded, 16)
            act.wait_ge(zeroed, 1)
            copy(tab33[N_BUCKETS:N_BUCKETS + 1, :], c("neg_rows")[N_BUCKETS:N_BUCKETS + 1, :]).then_inc(tab_set, 1)
            for k in range(0, NC, 2):
                act.wait_ge(x_turned, k + 1)
                copy(xT[:, k, :], acc[0][:, :]).then_inc(evacuated[0], 1)
            act.wait_ge(vec_ready, 1)
            copy(vec[:, 0:SEQ], scp[0][0:12, 0:SEQ])
            copy(vec[:, SEQ:SEQ + P], scp[1][0:12, 0:P])
            act.drain().then_inc(vec_copied, 1)
            act.wait_ge(vec_copied, 1)

            def store_bias(head, done):
                act.dma_start(bias_scratch[head:head + HEADS],
                              vec[head:head + HEADS].unsqueeze(1).to_broadcast([HEADS, P, SEQ + P])).then_inc(done, 16)

            def load_t5(to, head, heads):
                act.dma_start(to, bass.AP(bias_scratch.tensor, head * (P * (SEQ + P)) + (P - 1),
                                          [[SEQ + P - 1, P], [P * (SEQ + P), heads], [1, SEQ]])
                              ).then_inc(t5_loaded, 16)

            store_bias(HEADS, nsa_bias_stored)
            for k in range(NC):
                act.wait_ge(evacuated[k % 2], k // 2 + 1)
                act.activation(squares[:, k, :], xT[:, k, :], ACT.Square).then_inc(squared, 1)
            act.wait_ge(nsa_bias_stored, 16)
            load_t5(t5_nsa, HEADS, HEADS)
            store_bias(0, bias_stored)
            store_bias(2 * HEADS, bias_stored)
            act.wait_ge(const_rest, 16)
            finish(act, act_end)

            with act.Fori(0, DEPTH) as layer:
                stage = layer * STAGES1 + 1
                begin(act, stage + ST_NORM)
                act.dma_start(par1[:, :], par1_in[bass.ds(layer, 1)].rearrange("o p n -> p (o n)")
                              ).then_inc(par_loaded, 16)
                norm(layer * 2)
                norm_high(layer * 2, mixT)
                act.wait_ge(lam_dots, layer + 1)
                act.activation(lam2, lam_tmp, ACT.Exp).then_inc(lam_exps, 1)
                finish(act, act_end)
                with act.Fori(0, PAIRS) as pair:
                    begin(act, stage + pair + ST_SB)
                    stick_breaking(layer, pair)
                with act.Fori(0, PAIRS) as pair:
                    begin(act, stage + pair + ST_MB)
                    act.wait_ge(bias_stored, 32)
                    load_t5(pair_bias[:, :, 0:SEQ], pair * 2, 2)
                    moba(layer, pair)
                with act.Fori(0, PAIRS) as pair:
                    begin(act, stage + pair + ST_DF)
                    act.wait_ge(bias_stored, 32)
                    load_t5(pair_bias[:, :, 0:SEQ], pair * 2 + 2 * HEADS, 2)
                    differential(layer, pair)
                begin(act, stage + ST_NSA)
                nsa_select(layer)
                with act.Fori(0, PAIRS) as pair:
                    begin(act, stage + pair + ST_NSP)
                    act.wait_ge(bias_stored, 32)
                    load_t5(pair_bias[:, :, 0:SEQ], pair * 2 + HEADS, 2)
                    nsa_pair(layer, pair)
                begin(act, stage + ST_OUT)
                for k in range(NC):
                    op_high(mixT, k)
                finish(act, act_end)
                begin(act, stage + ST_NORM2)
                norm(layer * 2 + 1)
                norm_high(layer * 2 + 1, mixT)
                finish(act, act_end)
                begin(act, stage + ST_MLP)
                with act.Fori(0, PARTS1) as part:
                    done = layer * (ROUNDS1 * SLOTS) + part * (R_PART1 * SLOTS) + ROUND_MLP * SLOTS
                    tiles = layer * (PARTS1 * PART) + part * PART
                    for j in range(PART):
                        waits = [(pieces_done, done + j + 1)]
                        if j >= 2:
                            waits.append((hid_ready, tiles + j - 1))
                        settle(act, *waits)
                        act.activation(evac[:, j % 2, :], acc[j % 2][:, :], ACT.Relu).then_inc(evacuated[j % 2], 1)
                        act.drain()
                        act.activation(hidH[:, j, :], evac[:, j % 2, :], ACT.Square).then_inc(relu_ready, 1)
                finish(act, act_end)
            begin(act, ST_FINAL)
            norm(2 * DEPTH)
            norm_high(2 * DEPTH, xT)
            finish(act, act_end)
            with act.Fori(0, DEPTH) as layer:
                stage = layer * STAGES2 + ST_B2
                begin(act, stage + ST_FFN1)
                act.dma_start(par2[:, :], par2_in[bass.ds(layer, 1)].rearrange("o p n -> p (o n)")
                              ).then_inc(par_loaded, 16)
                ffn(stage + ST_FFN1, layer * ROUNDS2 + ROUND_B2, layer * GPS2 + GP_B2)
                begin(act, stage + ST_LN0)
                layer_norm(layer * 3)
                shift(layer * 3, 0)
                begin(act, stage + ST_PROJ)
                for row in range(GRID_H):
                    act.dma_start(
                        rpb_raw[row * NA_COLS:(row + 1) * NA_COLS].rearrange("p h r k -> p (h r) k"),
                        bass.AP(rpb_in.tensor,
                                layer * (GRID_H * NA_COLS * RPB_SIZE) + (row * NA_COLS * RPB_SIZE + RPB_PAD - 1),
                                [[RPB_SIZE - 1, NA_COLS], [RPB_W, NA_HEADS * GRID_H], [1, NA_REACH]])
                    ).then_inc(rpb_loaded, 16)
                for j in range(SLOTS):
                    act.wait_ge(pieces_done, layer * (ROUNDS2 * SLOTS) + (ROUND_B2 + ROUND_PROJ) * SLOTS + j + 1)
                    copy(side[:, 4 + j, :], acc[j % 2][:, :]).then_inc(evacuated[j % 2], 1)
                finish(act, act_end)
                with act.Fori(0, NA_PAIRS) as pair:
                    begin(act, stage + pair + ST_NA)
                    neighbourhood(layer, pair)
                begin(act, stage + ST_POOL)
                for i in range(2):
                    settle(act, (pool_mm, layer * 2 + i + 1))
                    act.activation(mixT[:, i, :], scp[i][:, :], ACT.Copy, scale=p2("pool_scale")[:, i:i + 1])
                finish(act, act_end)
                begin(act, stage + ST_OUT2)
                for k in range(NC):
                    op_high(mixT, k)
                finish(act, act_end)
                begin(act, stage + ST_LN1)
                layer_norm(layer * 3 + 1)
                shift(layer * 3 + 1, 1)
                ffn(stage + ST_FFN2, layer * ROUNDS2 + (ROUND_B2 + ROUND_FFN2), layer * GPS2 + (GP_B2 + GP_FFN2))
                begin(act, stage + ST_LN2)
                layer_norm(layer * 3 + 2)
                shift(layer * 3 + 2, 2)
            begin(act, ST_END)
            for n in range(2 * NT):
                act.wait_ge(out_turned, n + 1)
                copy(big[:, n * SEQ:(n + 1) * SEQ], acc[n % 2][:, :]).then_inc(out_copied, 1)
                if n % 2:
                    t = n // 2
                    act.wait_ge(out_copied, n + 1)
                    act.dma_start(out[t * P:(t + 1) * P, :], big[:, t * D_MODEL:(t + 1) * D_MODEL]
                                  ).then_inc(stored, 16)
            act.wait_ge(stored, 16 * NT)

        @block.vector
        def _(dve):
            def split(rnd, slot):
                dve.wait_ge(w_loaded[slot], rnd * 16 + 32)
                dve.wait_ge(pieces_done, rnd * SLOTS + slot + 1)
                split_piece(slot)

            def split_piece(slot):
                dve.tensor_copy(wH[:, slot, :], wraw[:, slot, :])
                dve.drain()
                dve.tensor_tensor(wL[:, slot, :], wraw[:, slot, :], wH[:, slot, :].bitcast(F32), ALU.subtract
                                  ).then_inc(split_done, 1)

            def split_round(rnd):
                for s in range(SLOTS):
                    split(rnd, s)

            def chunk_low(src, n, k):
                settle(dve, (op_hi, n * NC + k + 1))
                dve.tensor_tensor(opL[:, k, :], src[:, k, :], opH[:, k, :].bitcast(F32), ALU.subtract
                                  ).then_inc(op_lo, 1)

            def op_low(src, n):
                for k in range(0, NC, 2):
                    chunk_low(src, n, k)

            def norm(n, gain, to, at):
                dve.wait_ge(rstd_ready, n + 1)
                for k in range(NC):
                    dve.scalar_tensor_tensor(to[:, k, :], xT[:, k, :], gain[:, k:k + 1], rows[:, 0, :],
                                             ALU.mult, ALU.mult).then_inc(op_raw, 1)
                    if k % 2 == 0 and k > 0:
                        chunk_low(to, at, k - 2)
                chunk_low(to, at, NC - 2)

            def layer_norm(n, which, at):
                dve.wait_ge(ln_summed, n + 1)
                for k in range(NC):
                    dve.scalar_tensor_tensor(xT[:, k, :], scp[0][:, :], -1.0 / D_MODEL, xT[:, k, :],
                                             ALU.mult, ALU.add).then_inc(centred, 1)
                dve.drain()
                dve.wait_ge(ln_rstd, n + 1)
                for k in range(NC):
                    dve.scalar_tensor_tensor(xT[:, k, :], xT[:, k, :],
                                             p2("ln_g")[:, which * NC + k:which * NC + k + 1], rows[:, 0, :],
                                             ALU.mult, ALU.mult).then_inc(ln_scaled, 1)
                    if k % 2 and k > 1:
                        chunk_low(xT, at, k - 3)
                chunk_low(xT, at, NC - 2)
                finish(dve, dve_end)

            def out_chunk(chunk):
                return mixT[:, chunk, :].rearrange("p a s -> p (a s)")

            def bias_map(m, width, mb, bias, selected=None):
                waits = [(scores_ready, mb + m + 1)]
                if m >= 2:
                    waits.append((exped, mb + m - 1))
                if selected is not None:
                    waits.append((sel_ready, selected))
                settle(dve, *waits)
                to, src = score[:, m % 2, 0:width], scp[m % 2][:, 0:width]
                if len(bias.shape) == 3:
                    to, src = (a.rearrange("p (k r) -> p k r", r=GRID_H) for a in (to, src))
                dve.tensor_tensor_reduce(to, src, bias, -1.0, 3e38,
                                         ALU.add, ALU.min, negmax[:, m % STATS:m % STATS + 1]).then_inc(biased, 1)

            def reciprocal_of(m, mb, gate=None):
                col = slice(m % STATS, m % STATS + 1)
                dve.wait_ge(exped, mb + m + 1)
                dve.tensor_scalar(denom[:, col], denom[:, col], TINY, None, ALU.max)
                dve.drain()
                if gate is None:
                    return dve.reciprocal(recip[:, col], denom[:, col])
                dve.reciprocal(recip[:, col], denom[:, col])
                dve.drain()
                return dve.tensor_tensor(recip[:, col], recip[:, col], gate, ALU.mult)

            def splits(rnd):
                split(rnd, 0)
                return {step: lambda step=step: split(rnd, step) for step in (1, 2, 3)}

            def second_third(after):
                return {1: lambda: (after[1](), after[2]()), 3: after[3]}

            def softmax_maps(mb, maps, after={}):
                for i in range(len(maps) + 1):
                    if i < len(maps):
                        width, bias, _, ready = maps[i]
                        bias_map(i, width, mb, bias, ready)
                    if i >= 1:
                        m, w = i - 1, maps[i - 1][0]
                        reciprocal_of(m, mb, maps[m][2])
                        dve.drain()
                        p = prob[:, m % 4, 0:w]
                        dve.tensor_scalar(p, p, recip[:, m % STATS:m % STATS + 1], None, ALU.mult).then_inc(normed, 1)
                    if i in after:
                        after[i]()

            def heads_out(tb, count, chunk):
                dve.wait_ge(pv_done, tb + count)
                dve.tensor_scalar(out_chunk(chunk), outp[:, :], 1.0, None, ALU.mult)
                finish(dve, dve_end)

            def t5_cols(a, hh, t):
                return a[:, hh, SEQ - (t + 1) * P:SEQ]

            units = [(hh, t) for hh in range(2) for t in range(NT)]

            def t5_wait(eng, layer, n):
                settle(eng, (t5_loaded, layer * (T5_LOADS * 16) + n * 16 + 32))

            def stick_breaking(layer, pair):
                after = splits(layer * ROUNDS1 + pair + ROUND_SB)
                ub, tb = layer * (2 * U) + pair * U, layer * TRS1 + pair * U + TR_SB
                dve.memset(blocks[:, 0:SEQ // CMP_PAD, :], 1.0)
                one_row = blocks[:, 0:SEQ // CMP_PAD, :].rearrange("p a b -> p (a b)")
                for i, (hh, t) in enumerate(units):
                    w = (t + 1) * P
                    dve.wait_ge(sb_scores, ub + i + 1)
                    dve.tensor_tensor(sb_unit(sb_z_buf, hh, t), scp[i % 2][:, 0:w], c("strict")[:, SEQ - w:SEQ], ALU.add
                                      ).then_inc(sb_z, 1)
                dve.drain()
                after[1]()
                for hh in range(2):
                    dve.wait_ge(sb_log, layer * 4 + pair * 2 + hh + 1)
                    dve.scalar_tensor_tensor(sb_t[hh], sb_z_buf[hh], 0.0, sb_t[hh], ALU.max, ALU.add)
                    dve.drain()
                    for t in range(NT):
                        a = sb_unit(sb_t, hh, t)
                        dve.tensor_tensor_scan(a[:, ::-1], one_row[:, 0:(t + 1) * P], a[:, ::-1], 0.0,
                                               ALU.mult, ALU.subtract)
                    dve.drain()
                    dve.tensor_tensor(sb_t[hh], sb_t[hh], sb_z_buf[hh], ALU.add).then_inc(sb_arg, 1)
                    after[2 + hh]()
                heads_out(tb, U, bass.ds(pair, 1))

            def moba(layer, pair):
                after = second_third(splits(layer * ROUNDS1 + pair + ROUND_MB))
                t5_wait(dve, layer, pair)
                softmax_maps(layer * MAPS1 + pair * U + MAPS_MB,
                             [((t + 1) * P, t5_cols(pair_bias, hh, t), None, None) for hh, t in units], after)
                heads_out(layer * TRS1 + pair * U + TR_MB, U, bass.ds(pair + 2, 1))

            def differential(layer, pair):
                mb = layer * MAPS1 + pair * (2 * U) + MAPS_DF
                ub = layer * (2 * U) + pair * U
                after = second_third(splits(layer * ROUNDS1 + pair + ROUND_DF))
                t5_wait(dve, layer, pair + PAIRS)
                for i in range(U + 1):
                    if i < U:
                        hh, t = units[i]
                        for half in range(2):
                            bias_map(2 * i + half, (t + 1) * P, mb, t5_cols(pair_bias, hh, t))
                    if i >= 1:
                        u = i - 1
                        w = (units[u][1] + 1) * P
                        m = 2 * u
                        col = slice(m % STATS, m % STATS + 2)
                        dve.wait_ge(exped, mb + m + 2)
                        dve.tensor_scalar(denom[:, col], denom[:, col], TINY, None, ALU.max)
                        dve.drain()
                        dve.reciprocal(recip[:, col], denom[:, col])
                        dve.drain()
                        dve.tensor_tensor(recip[:, col], recip[:, col], lam_pair, ALU.mult)
                        dve.drain()
                        first, second = df_probs[u % 4]
                        dve.tensor_scalar(second[:, 0:w], second[:, 0:w],
                                          recip[:, (m + 1) % STATS:(m + 1) % STATS + 1], None, ALU.mult)
                        dve.drain()
                        dve.scalar_tensor_tensor(first[:, 0:w], first[:, 0:w], recip[:, m % STATS:m % STATS + 1],
                                                 second[:, 0:w], ALU.mult, ALU.subtract).then_inc(df_weight, 1)
                    if i in after:
                        after[i]()
                dve.wait_ge(df_rstd, layer * PAIRS + pair + 1)
                dve.scalar_tensor_tensor(out_chunk(bass.ds(pair + 6, 1)), outp[:, :], subln, rows[:, 1, :],
                                         ALU.mult, ALU.mult)
                finish(dve, dve_end)

            def nsa_select(layer):
                src = side[:, 0, :]
                dve.tensor_tensor(blocks[:, :, 0:N_CMP],
                                  bass.AP(src.tensor, src.offset, [list(src.ap[0]), [1, CMP_LEN], [CMP_STRIDE, N_CMP]]),
                                  p1("pos").unsqueeze(2).to_broadcast([P, CMP_LEN, N_CMP]), ALU.add)
                dve.memset(blkH[:, :, :].bitcast(F32), 0.0)
                dve.drain()
                diagonal = [(slice(HEAD * kv, HEAD * (kv + 1)), slice(CMP_PAD * kv, CMP_PAD * kv + N_CMP))
                            for kv in range(2)]
                for p, n in diagonal:
                    dve.tensor_copy(blkH[p, 0:CMP_LEN, n], blocks[p, :, 0:N_CMP])
                dve.drain()
                dve.wait_ge(low_cleared, layer + 1)
                for p, n in diagonal:
                    dve.tensor_tensor(blkL[p, 0:CMP_LEN, n], blocks[p, :, 0:N_CMP],
                                      blkH[p, 0:CMP_LEN, n].bitcast(F32), ALU.subtract)
                dve.drain().then_inc(blocks_ready, 1)
                dve.wait_ge(gate_exp, layer + 1)
                dve.tensor_scalar(gates, gates, 1.0, None, ALU.add)
                dve.drain()
                dve.reciprocal(gates, gates)
                split_round(layer * ROUNDS1 + ROUND_CMP)
                last = layer * ROUNDS1 + (ROUND_CMP + 1)
                split(last, 0)
                split(last, 1)
                x, g = gx[:, :, 0:N_CMP], gt[:, :, 0:N_CMP]
                dve.wait_ge(hid_sq, layer + 1)
                dve.tensor_scalar(g, g, 0.044715, 1.0, ALU.mult, ALU.add)
                dve.drain()
                dve.tensor_tensor(g, g, x, ALU.mult).then_inc(hid_poly, 1)
                dve.wait_ge(hid_exp, layer + 1)
                dve.tensor_scalar(g, g, 1.0, None, ALU.add)
                dve.drain()
                dve.reciprocal(g, g)
                dve.drain()
                for h in range(2):
                    dve.tensor_tensor(h1v[:, h, :, 0:N_CMP],
                                      gx[:, 2 + h, 0:N_CMP].unsqueeze(1).to_broadcast([P, HEADS, N_CMP]),
                                      gt[:, 2 + h, 0:N_CMP].unsqueeze(1).to_broadcast([P, HEADS, N_CMP]), ALU.mult)
                dve.drain().then_inc(gelu_ready, 1)
                dve.tensor_tensor(gx[:, 0:2, 0:N_CMP], gx[:, 0:2, 0:N_CMP], gt[:, 0:2, 0:N_CMP], ALU.mult
                                  ).then_inc(gelu_ready, 1)
                split(last, 2)
                split(last, 3)

                def flat(a):
                    return a[:, :, :, 0:N_CMP].rearrange("p t h n -> p (t h) n")

                def spread(a):
                    return a.unsqueeze(2).to_broadcast([P, NT * HEADS, N_CMP])

                dve.wait_ge(cmp_scores, layer + 1)
                dve.tensor_tensor(flat(pcg), trp[0][:, :].rearrange("p (a n) -> p a n", n=CMP_PAD)[:, :, 0:N_CMP],
                                  flat(cmp_bias), ALU.add)
                dve.drain()
                dve.tensor_reduce(cmax, flat(pcg), AX.X, ALU.max)
                dve.drain()
                dve.tensor_tensor(flat(pcg), flat(pcg), spread(cmax), ALU.subtract).then_inc(cmp_shift, 1)
                dve.wait_ge(cmp_exp, layer + 1)
                dve.tensor_tensor(flat(pc), flat(pc), flat(cmp_mask), ALU.mult)
                dve.drain()
                dve.tensor_reduce(csum, flat(pc), AX.X, ALU.add)
                dve.drain()
                dve.tensor_scalar(csum, csum, TINY, None, ALU.max)
                dve.drain()
                dve.reciprocal(csum, csum)
                dve.drain()
                dve.tensor_tensor(flat(pc), flat(pc), spread(csum), ALU.mult).then_inc(pc_ready, 1)
                dve.drain()
                dve.tensor_tensor(pcg[:, :, :, 0:N_CMP].rearrange("p t h n -> p (t h) n"), flat(pc),
                                  gates_of(0), ALU.mult).then_inc(pc_ready, 1)
                dve.wait_ge(imp_ready, layer + 1)
                dve.tensor_tensor(imp, scp[0][:, 0:NT * N_SLC].rearrange("p (t j) -> p t j", t=NT),
                                  c("past").rearrange("p (t j) -> p t j", t=NT), ALU.mult)
                dve.drain()
                dve.tensor_tensor(imp, imp, c("force").rearrange("p (t j) -> p t j", t=NT), ALU.add)
                dve.drain()
                shape = [P, NT, N_SLC, N_SLC]
                mine, other = imp.unsqueeze(3).to_broadcast(shape), imp.unsqueeze(2).to_broadcast(shape)
                more = beats[:, 0, :].rearrange("p (t j i) -> p t j i", t=NT, j=N_SLC)
                same = beats[:, 1, :].rearrange("p (t j i) -> p t j i", t=NT, j=N_SLC)
                dve.tensor_tensor(more, other, mine, ALU.is_gt)
                dve.tensor_tensor(same, other, mine, ALU.is_equal)
                dve.drain()
                dve.tensor_tensor(beats[:, 1, :].rearrange("p (t j) -> p t j", t=NT),
                                  beats[:, 1, :].rearrange("p (t j) -> p t j", t=NT),
                                  c("earlier").unsqueeze(1).to_broadcast([P, NT, N_SLC * N_SLC]), ALU.mult)
                dve.drain()
                dve.tensor_tensor(beats[:, 0, :], beats[:, 0, :], beats[:, 1, :], ALU.add)
                dve.drain()
                dve.tensor_reduce(rank, more, AX.X, ALU.add)
                dve.drain()
                dve.tensor_scalar(sel_neg, rank, float(SLC_TOPN), NEG, ALU.is_ge, ALU.mult)
                finish(dve, dve_end)

            def gates_of(branch):
                g = gates[:, :, branch * HEADS:(branch + 1) * HEADS]
                return g.unsqueeze(3).to_broadcast([P, NT, HEADS, N_CMP])

            def nsa_pair(layer, pair):
                dve.tensor_copy(qT, side[:, bass.ds(pair + 4, 1), :].rearrange("p a s -> p (a s)"))
                dve.tensor_copy(vc_pair[:, :], vc_diag[:, bass.ds(pair * P, P)])
                dve.drain().then_inc(pair_ready, 1)
                t5_wait(dve, layer, pair + 2 * PAIRS)
                sel = layer * (2 * U) + pair * U
                maps = []
                for n, (hh, t) in enumerate(units):
                    w = (t + 1) * P
                    for branch in (1, 2):
                        g = gates[:, t, bass.ds(pair * 2 + (branch * HEADS + hh), 1)]
                        if branch == 1:
                            maps.append((w, sel_bias[:, n % 2, 0:w], g, sel + n + 1))
                        else:
                            maps.append((w, t5_cols(pair_bias, hh, t), g, None))
                softmax_maps(layer * MAPS1 + pair * (2 * U) + MAPS_NS, maps)
                heads_out(layer * TRS1 + pair * (2 * U) + TR_NS, 2 * U, bass.ds(pair + 4, 1))

            def neighbourhood(layer, pair):
                after = second_third(splits(layer * ROUNDS2 + pair + (ROUND_B2 + ROUND_NA)))
                dve.wait_ge(bias_ready, layer * NA_PAIRS + pair + 1)
                maps = []
                for hh, t in units:
                    n = NA_TILES[t][1] * NA_COLS
                    bias = first_bias if t == 0 else last_bias if t == NT - 1 else inner_bias
                    maps.append((NA_KEYS[t], bias[:, hh, :, 0:n].rearrange("p r k -> p k r"), None, None))
                softmax_maps(layer * (4 * U) + pair * U + DEPTH * MAPS1, maps, after)
                dve.wait_ge(pv_done, layer * (4 * U) + pair * U + (DEPTH * TRS1 + U))
                dve.tensor_scalar(out_chunk(bass.ds(pair + 4, 1)).rearrange("p (r t c) -> p t r c", r=GRID_H, t=NT),
                                  outp[:, :].rearrange("p (t r c) -> p t r c", r=GRID_H, t=NT), 1.0, None, ALU.mult)
                finish(dve, dve_end)

            def add_tile(rounds, r, j, scale):
                dve.wait_ge(pieces_done, r * SLOTS + rounds * SLOTS + j + 1)
                x = xT[:, bass.ds(r * SLOTS + j, 1), :].rearrange("p a s -> p (a s)")
                if scale is None:
                    ins = dve.tensor_tensor(x, acc[j % 2][:, :], x, ALU.add)
                else:
                    ins = dve.scalar_tensor_tensor(x, x, scale, acc[j % 2][:, :], ALU.mult, ALU.add)
                ins.then_inc(evacuated[j % 2], 1)

            def add_out(rounds, scale=None):
                with dve.Fori(0, R_OUT) as r:
                    for j in range(SLOTS):
                        add_tile(rounds, r, j, scale)
                        split(r + rounds, j)

            def hidden_tile(a, tile):
                return a[:, bass.ds(tile, 1), :].rearrange("p a s -> p (a s)")

            def hidden_low(tile, value):
                dve.tensor_tensor(hidden_tile(hidL, tile), value, hidden_tile(hidH, tile).bitcast(F32), ALU.subtract
                                  ).then_inc(hid_ready, 1)

            def ffn(stage, rounds, silu):
                begin(dve, stage)
                for part, (r_gu, n) in enumerate(zip(R_GU, PARTS2)):
                    with dve.Fori(0, r_gu) as r:
                        for j in range(2):
                            split(r + rounds, 2 * j)
                            dve.wait_ge(silu_ready, silu + r * 2 + j + 1)
                            dve.wait_ge(pieces_done, r * SLOTS + rounds * SLOTS + 2 * j + 2)
                            dve.scalar_tensor_tensor(raw[:, j, :], acc[1][:, :], 0.5, evac[:, j, :], ALU.mult,
                                                     ALU.mult).then_inc(evacuated[1], 1)
                            dve.drain()
                            tile = r * 2 + j
                            dve.tensor_copy(hidden_tile(hidH, tile), raw[:, j, :])
                            dve.drain()
                            hidden_low(tile, raw[:, j, :])
                            split(r + rounds, 2 * j + 1)
                    add_out(rounds + r_gu, ALPHA if part == 0 else None)
                    rounds, silu = rounds + r_gu + R_DOWN, silu + n
                finish(dve, dve_end)

            dve.memset(eps_norm, NORM_EPS)
            dve.memset(eps_ln, LN_EPS)
            dve.memset(one_col, 1.0)
            dve.memset(vc_diag[:, :], 0.0)
            dve.memset(kc_diag, 0.0)
            dve.memset(h1v[:, :, :, :], 0.0)
            dve.memset(pc[:, :, :, :], 0.0)
            dve.memset(pcg[:, :, :, :], 0.0)
            dve.memset(cmp_bias[:, :, :, :], NEG)
            dve.memset(pair_bias, 0.0).then_inc(zeroed, 1)
            for k in range(1, NC, 2):
                dve.wait_ge(x_turned, k + 1)
                dve.tensor_copy(xT[:, k, :], acc[1][:, :]).then_inc(evacuated[1], 1)
            for s in range(SLOTS):
                dve.wait_ge(w_loaded[s], 16)
                split_piece(s)
            dve.wait_ge(t5_loaded, 16)
            for t in range(NT):
                n = (t + 1) * P // CMP_STRIDE - 1
                first = (NT - 1 - t) * P + CMP_LEN - 1
                dve.tensor_copy(cmp_bias[:, t, :, 0:n],
                                t5_nsa[:, :, first:first + (n - 1) * CMP_STRIDE + 1:CMP_STRIDE])
            dve.drain()
            dve.tensor_scalar(cmp_mask[:, :, :, :].rearrange("p t h n -> p (t h n)"),
                              cmp_bias[:, :, :, :].rearrange("p t h n -> p (t h n)"), NEG / 10, None, ALU.is_gt)
            finish(dve, dve_end)

            with dve.Fori(0, DEPTH) as layer:
                stage = layer * STAGES1 + 1
                begin(dve, stage + ST_NORM)
                dve.wait_ge(par_loaded, layer * 16 + 16)
                norm(layer * 2, p1("norm_attn"), mixT, layer * SPLITS1)
                lv = p1("lam").rearrange("p (a b d) -> p a b d", a=2, b=2)
                dve.tensor_tensor(lam_prod.rearrange("p (a d) -> p a d", a=2), lv[:, :, 0, :], lv[:, :, 1, :], ALU.mult)
                dve.drain()
                dve.tensor_reduce(lam_tmp, lam_prod.rearrange("p (a d) -> p a d", a=2), AX.X, ALU.add
                                  ).then_inc(lam_dots, 1)
                dve.wait_ge(lam_exps, layer + 1)
                dve.scalar_tensor_tensor(lam_one, lam2[:, 0:1], p1("lam_init")[:, 0:1], lam2[:, 1:2], ALU.add,
                                         ALU.subtract)
                dve.drain()
                dve.scalar_tensor_tensor(lam_scale, lam_one, -1.0, lam_one, ALU.mult, ALU.max)
                dve.drain()
                dve.tensor_scalar(lam_scale, lam_scale, 1.0, None, ALU.max)
                dve.drain()
                dve.reciprocal(lam_scale, lam_scale)
                dve.drain()
                dve.tensor_tensor(lam_one, lam_one, lam_scale, ALU.mult)
                dve.tensor_scalar(lam_eps, lam_scale, lam_scale, NORM_EPS, ALU.mult, ALU.mult)
                dve.tensor_tensor(subln, p1("subln"), p1("lam_init")[:, 1:2], ALU.mult)
                finish(dve, dve_end)
                with dve.Fori(0, PAIRS) as pair:
                    begin(dve, stage + pair + ST_SB)
                    stick_breaking(layer, pair)
                with dve.Fori(0, PAIRS) as pair:
                    begin(dve, stage + pair + ST_MB)
                    moba(layer, pair)
                with dve.Fori(0, PAIRS) as pair:
                    begin(dve, stage + pair + ST_DF)
                    differential(layer, pair)
                begin(dve, stage + ST_NSA)
                nsa_select(layer)
                with dve.Fori(0, PAIRS) as pair:
                    begin(dve, stage + pair + ST_NSP)
                    nsa_pair(layer, pair)
                begin(dve, stage + ST_OUT)
                op_low(mixT, layer * SPLITS1 + 1)
                add_out(layer * ROUNDS1 + ROUND_OUT)
                finish(dve, dve_end)
                begin(dve, stage + ST_NORM2)
                norm(layer * 2 + 1, p1("norm_mlp"), mixT, layer * SPLITS1 + 2)
                finish(dve, dve_end)
                begin(dve, stage + ST_MLP)
                with dve.Fori(0, PARTS1) as part:
                    rounds = layer * ROUNDS1 + part * R_PART1 + ROUND_MLP
                    tiles = layer * (PARTS1 * PART) + part * PART
                    for j in range(PART):
                        split(rounds + j // SLOTS, j % SLOTS)
                        dve.wait_ge(relu_ready, tiles + j + 1)
                        dve.tensor_tensor(raw[:, j % 2, :], evac[:, j % 2, :], evac[:, j % 2, :], ALU.mult)
                        dve.drain()
                        hidden_low(j, raw[:, j % 2, :])
                    add_out(rounds + R_UP)
                finish(dve, dve_end)
            begin(dve, ST_FINAL)
            norm(2 * DEPTH, p1("final_norm"), xT, DEPTH * SPLITS1)
            finish(dve, dve_end)
            with dve.Fori(0, DEPTH) as layer:
                stage = layer * STAGES2 + ST_B2
                ffn(stage + ST_FFN1, layer * ROUNDS2 + ROUND_B2, layer * (2 * sum(PARTS2)))
                begin(dve, stage + ST_LN0)
                dve.wait_ge(par_loaded, layer * 16 + 16 * (DEPTH + 1))
                layer_norm(layer * 3, 0, layer * SPLITS2 + SPLIT_B2)
                begin(dve, stage + ST_PROJ)
                split_round(layer * ROUNDS2 + (ROUND_B2 + ROUND_PROJ))
                groups = layer * GPS2 + (GP_B2 + GP_PROJ + 2)
                settle(dve, (evacuated[0], groups), (evacuated[1], groups))
                for i in range(2):
                    w = p2("conv")[:, 3 * i:3 * i + 3]
                    z = big_pad(i, SEQ + 2)
                    dve.memset(z, 0.0)
                    dve.drain()
                    dve.tensor_tensor(z[:, 1:SEQ + 1], side[:, 4 + i, :], side[:, 6 + i, :], ALU.mult)
                    dve.drain()
                    y = mixT[:, 2 + i, :]
                    dve.tensor_scalar(y, z[:, 0:SEQ], w[:, 0:1], None, ALU.mult)
                    dve.drain()
                    for k in (1, 2):
                        dve.scalar_tensor_tensor(y, z[:, k:k + SEQ], w[:, k:k + 1], y, ALU.mult, ALU.add)
                        dve.drain()
                finish(dve, dve_end)
                with dve.Fori(0, NA_PAIRS) as pair:
                    begin(dve, stage + pair + ST_NA)
                    neighbourhood(layer, pair)
                begin(dve, stage + ST_POOL)
                for i in range(2):
                    y = mixT[:, 2 + i, :]
                    dve.tensor_tensor(y, y, side[:, 2 + i, :], ALU.mult)
                finish(dve, dve_end)
                begin(dve, stage + ST_OUT2)
                op_low(mixT, layer * SPLITS2 + (SPLIT_B2 + 1))
                add_out(layer * ROUNDS2 + (ROUND_B2 + ROUND_OUT2), ALPHA)
                finish(dve, dve_end)
                begin(dve, stage + ST_LN1)
                layer_norm(layer * 3 + 1, 1, layer * SPLITS2 + (SPLIT_B2 + 2))
                ffn(stage + ST_FFN2, layer * ROUNDS2 + (ROUND_B2 + ROUND_FFN2),
                    layer * (2 * sum(PARTS2)) + sum(PARTS2))
                begin(dve, stage + ST_LN2)
                layer_norm(layer * 3 + 2, 2, layer * SPLITS2 + (SPLIT_B2 + 3))

        @block.gpsimd
        def _(pool):
            def add_chunks(gp, ready, squared):
                for k in range(NC):
                    settle(pool, (evacuated[k % 2], gp + (k // 2 + 1)))
                    pool.drain()
                    if squared:
                        to = stat if k == 0 else chunk_squares[:, k % 2, :]
                        pool.tensor_tensor(to, xT[:, k, :], xT[:, k, :], ALU.mult)
                        pool.drain()
                        if k > 0:
                            pool.tensor_tensor(stat, stat, to, ALU.add)
                    elif k > 0:
                        pool.tensor_tensor(stat, xT[:, 0, :] if k == 1 else stat, xT[:, k, :], ALU.add)
                pool.drain().then_inc(ready, 1)

            def stat_stage(stage, gp, ready, squared):
                begin(pool, stage)
                add_chunks(gp, ready, squared)
                finish(pool, pool_end)

            def out_stage(stage, n, gp, ready, squared):
                begin(pool, stage)
                op_low(mixT, n)
                add_chunks(gp, ready, squared)
                finish(pool, pool_end)

            def idle(stage):
                finish(pool, pool_end)

            causal = [(t + 1) * P for hh in range(2) for t in range(NT)]

            def op_low(src, n):
                for k in range(1, NC, 2):
                    settle(pool, (op_hi, n * NC + k + 1))
                    pool.tensor_tensor(opL[:, k, :], src[:, k, :], opH[:, k, :].bitcast(F32), ALU.subtract
                                       ).then_inc(op_lo_pool, 1)

            def low_stage(stage, src, n):
                begin(pool, stage)
                op_low(src, n)
                finish(pool, pool_end)

            def window_means(i):
                border = max(POOL_WINDOWS)
                wide = SEQ + 2 * border
                space4 = side[:, 4:8, :].rearrange("p i s -> p (i s)")
                pads = [space4[:, n * wide:(n + 1) * wide] for n in range(3)]
                for pad in pads:
                    pool.memset(pad, 0.0)
                pool.drain()
                pool.tensor_copy(pads[0][:, border:border + SEQ], side[:, i, :])
                pool.drain()
                at, done = 0, 0
                for w in POOL_WINDOWS[0:2 * i + 2]:
                    lo, hi = (1, 0) if w == 2 else (w // 4, w // 4)
                    to = 1 if at != 1 else 2
                    span = slice(border // 2, wide - border // 2)
                    pool.tensor_tensor(pads[to][:, span], pads[at][:, span.start - lo:span.stop - lo],
                                       pads[at][:, span.start + hi:span.stop + hi], ALU.add)
                    pool.drain()
                    at = to
                    if w in POOL_WINDOWS[2 * i:2 * i + 2]:
                        g = slice(HEAD * done, HEAD * (done + 1))
                        pool.tensor_tensor(pcT[g], pads[at][g, border:border + SEQ],
                                           c("inv_count")[g, i * SEQ:(i + 1) * SEQ], ALU.mult)
                        pool.drain()
                        pool.tensor_tensor(side[g, i, :], pcT[g], side[g, i, :], ALU.subtract)
                        done += 1
                pool.drain().then_inc(pooled, 1)

            for k in range(1, NC):
                pool.wait_ge(squared, k + 1)
                pool.tensor_tensor(stat, squares[:, 0, :] if k == 1 else stat, squares[:, k, :], ALU.add)
                pool.drain()
            pool.drain().then_inc(stat_ready, 1)
            finish(pool, pool_end)
            with pool.Fori(0, DEPTH) as layer:
                stage = layer * STAGES1 + 1
                low_stage(stage + ST_NORM, mixT, layer * SPLITS1)
                with pool.Fori(0, PAIRS) as pair:
                    idle(stage + pair + ST_SB)
                with pool.Fori(0, 2 * PAIRS) as pair:
                    idle(stage + pair + ST_MB)
                begin(pool, stage + ST_NSA)
                pool.memset(blkL[:, :, :].bitcast(F32), 0.0).then_inc(low_cleared, 1)
                finish(pool, pool_end)
                with pool.Fori(0, PAIRS) as pair:
                    begin(pool, stage + pair + ST_NSP)
                    settle(pool, (t5_loaded, layer * (T5_LOADS * 16) + pair * 16 + (2 * PAIRS * 16 + 32)))
                    mb = layer * MAPS1 + pair * (2 * U) + MAPS_NS

                    def select(n):
                        hh, t = n // NT, n % NT
                        w = (t + 1) * P
                        if n >= 2:
                            pool.wait_ge(biased, mb + 2 * (n - 2) + 1)
                        pool.tensor_tensor(
                            sel_bias[:, n % 2, 0:w].rearrange("p (j k) -> p j k", k=SLC_LEN),
                            pair_bias[:, hh, SEQ - w:SEQ].rearrange("p (j k) -> p j k", k=SLC_LEN),
                            sel_neg[:, t, 0:w // SLC_LEN].unsqueeze(2).to_broadcast([P, w // SLC_LEN, SLC_LEN]),
                            ALU.add).then_inc(sel_ready, 1)

                    for n in range(U):
                        select(n)
                    finish(pool, pool_end)
                gps = layer * GPS1 + GP_SETUP
                out_stage(stage + ST_OUT, layer * SPLITS1 + 1, gps + GP_OUT, stat_ready, True)
                low_stage(stage + ST_NORM2, mixT, layer * SPLITS1 + 2)
                stat_stage(stage + ST_MLP, gps + (GPS1 - NC // 2), stat_ready, True)
            low_stage(ST_FINAL, xT, DEPTH * SPLITS1)
            with pool.Fori(0, DEPTH) as layer:
                stage = layer * STAGES2 + ST_B2
                gps = layer * GPS2 + GP_B2
                stat_stage(stage + ST_FFN1, gps + (GP_FFN - NC // 2), ln_stat_ready, False)
                low_stage(stage + ST_LN0, xT, layer * SPLITS2 + SPLIT_B2)
                idle(stage + ST_PROJ)
                def na_bias(pair):
                    begin(pool, stage + pair + ST_NA)
                    settle(pool, (rpb_loaded, layer * (GRID_H * 16) + GRID_H * 16))
                    for hh in range(2):
                        rel = rpb_raw[:, bass.ds(pair * 2 + hh, 1)].rearrange("p o r k -> p (o r) k")
                        for to, cols, mask in ((first_bias[:, hh], slice(NA_COLS, NA_REACH), "mask_first"),
                                               (inner_bias[:, hh], slice(0, NA_REACH), "mask_inner"),
                                               (last_bias[:, hh], slice(0, NA_EDGE), "mask_last")):
                            pool.tensor_tensor(to, rel[:, :, cols],
                                               c(mask).unsqueeze(1).to_broadcast(list(to.shape)), ALU.add)
                    pool.drain().then_inc(bias_ready, 1)

                with pool.Fori(0, 2) as pair:
                    na_bias(pair)
                    finish(pool, pool_end)
                for i in range(2):
                    na_bias(2 + i)
                    window_means(i)
                    finish(pool, pool_end)
                idle(stage + ST_POOL)
                out_stage(stage + ST_OUT2, layer * SPLITS2 + (SPLIT_B2 + 1), gps + GP_OUT2, ln_stat_ready, False)
                low_stage(stage + ST_LN1, xT, layer * SPLITS2 + (SPLIT_B2 + 2))
                stat_stage(stage + ST_FFN2, gps + (GPS2 - NC // 2), ln_stat_ready, False)
                low_stage(stage + ST_LN2, xT, layer * SPLITS2 + (SPLIT_B2 + 3))


def _bucket(n):
    exact = N_BUCKETS // 2
    nf = np.maximum(n, 1).astype(np.float32)
    large = exact + (np.log(nf / np.float32(exact)) / np.float32(math.log(MAX_DISTANCE / exact))
                     * np.float32(N_BUCKETS - exact)).astype(np.int32)
    return np.where(n < exact, n, np.minimum(large, N_BUCKETS - 1))


def _constants():
    a = np.zeros((P, CONST_W), np.float32)

    def put(name, v):
        lo, hi = CONST[name]
        a[:v.shape[0], lo:hi] = v.reshape(v.shape[0], -1)

    p, m = np.arange(P)[:, None], np.arange(SEQ)[None]
    put("ident", np.eye(P))
    put("ones", np.ones((P, P)))
    put("head_ones", np.kron(np.eye(2), np.ones((HEAD, HEAD))))
    put("strict", np.where(p + SEQ - P - m >= 1, 0.0, NEG))
    start = np.arange(CMP_PAD)[:, None] * CMP_STRIDE
    s0 = np.arange(N_SLC)[None] * SLC_LEN
    cover = np.clip(np.minimum(start + CMP_LEN - 1, s0 + SLC_LEN - 1) - np.maximum(start, s0) + 1, 0, None) / CMP_LEN
    cover[N_CMP:] = 0
    put("cover", np.tile(cover, (HEADS, 1)))
    own = (np.arange(NT)[None, :, None] * P + p[:, :, None]) // SLC_LEN
    j = np.arange(N_SLC)[None, None]
    put("past", (j < own).astype(np.float32))
    put("force", np.where(j == own, -NEG, np.where(j < own, 0.0, NEG)))
    put("earlier", np.broadcast_to(np.arange(N_SLC)[None, None] < np.arange(N_SLC)[None, :, None], (P, N_SLC, N_SLC)))
    t = np.arange(SEQ)
    counts = [np.clip(t - w // 2 + w, 0, SEQ) - np.clip(t - w // 2, 0, SEQ) for w in POOL_WINDOWS]
    inv = 1.0 / np.stack(counts)
    put("inv_count", np.stack([np.repeat(inv[0:2], HEAD, 0), np.repeat(inv[2:4], HEAD, 0)], 1))
    qc, kc = np.arange(P)[:, None] % NA_COLS, np.arange(GRID_W)[None]
    for name, tile in (("first", 0), ("inner", 1), ("last", NT - 1)):
        left = np.clip(tile * NA_COLS + qc - NA_COLS // 2, 0, GRID_W - NA_COLS)
        first, n = NA_TILES[tile]
        mask = np.where((kc >= left) & (kc < left + NA_COLS), 0.0, NEG)
        put(f"mask_{name}", mask[:, first * NA_COLS:(first + n) * NA_COLS])
    u = np.arange(SEQ + P)
    dist = SEQ - 1 - u
    hot = np.where(dist[None] >= 0, np.arange(N_BUCKETS)[:, None] == _bucket(np.maximum(dist, 0))[None], False)
    put("neg_rows", np.full((P, 12), NEG))
    return a, np.concatenate([hot, (dist < 0)[None]], 0).astype(np.float32)


def _pieces(inputs):
    out = []

    def put(w):
        k = w.shape[0] // P
        out.append(w.reshape(k, P, P).transpose(1, 0, 2).reshape(-1))

    g = inputs
    sizes = (GROUP,) * 7 + (HEAD,) * 6 + (3 * HEADS,) + (GROUP,) * 3
    at = np.concatenate([[0], np.cumsum(sizes)]).tolist()
    for l in range(DEPTH):
        w = g["w_in"][l]

        def cols(i, pair):
            return w[:, at[i] + pair * P:at[i] + (pair + 1) * P]

        gate_cols = np.zeros((D_MODEL, P), w.dtype)
        gate_cols[:, 0:3 * HEADS] = w[:, at[13]:at[14]]
        sides = [[cols(7, 0), cols(9, 0)], [cols(11, 0), gate_cols], [cols(6, 0), cols(6, 1)]]
        for first, fourth in zip((0, 3, 14), sides):
            for pair in range(PAIRS):
                for i in range(3):
                    put(cols(first + i, pair))
                put(fourth[pair])
        both = np.concatenate([g[n][l].reshape(CMP_LEN, HEAD, CMP_HIDDEN).transpose(1, 0, 2)
                               for n in ("cmp_k_w1", "cmp_v_w1")], 0)
        per = PIECE // CMP_HIDDEN
        for n in range(CMP_LEN // per):
            out.append(both[:, n * per:(n + 1) * per].reshape(-1))
        for d in range(NC):
            put(g["w_out"][l][:, d * P:(d + 1) * P])
        for part in range(PARTS1):
            for f in range(part * PART, (part + 1) * PART):
                put(g["w_up"][l][:, f * P:(f + 1) * P])
            for d in range(NC):
                put(g["w_down"][l][part * PART * P:(part + 1) * PART * P, d * P:(d + 1) * P])
    for l in range(DEPTH):
        def ffn(name):
            f0 = 0
            for n in PARTS2:
                for f in range(f0, f0 + n):
                    for part in ("gate", "up"):
                        put(g[f"{name}_w_{part}_2"][l][:, f * P:(f + 1) * P])
                for d in range(NC):
                    put(g[f"{name}_w_down_2"][l][f0 * P:(f0 + n) * P, d * P:(d + 1) * P])
                f0 += n

        ffn("ffn1")
        w = g["w_in_2"][l]
        for i in (4, 5, 6, 7):
            put(w[:, i * P:(i + 1) * P])
        qkv = NC * P
        for pair in range(NA_PAIRS):
            for i in range(3):
                lo = qkv + i * NA_HEADS * HEAD + pair * P
                put(w[:, lo:lo + P])
            put(w[:, pair * P:(pair + 1) * P])
        for d in range(NC):
            put(g["w_out_2"][l][:, d * P:(d + 1) * P])
        ffn("ffn2")
    out.append(np.zeros(SLOTS * P * PIECE, np.float32))
    return np.concatenate(out)


def _parameters(g):
    a = np.zeros((DEPTH, P, PAR1_W), np.float32)
    b = np.zeros((DEPTH, P, PAR2_W), np.float32)

    def put(to, cols, l, name, v):
        lo, hi = cols[name]
        to[l, :, lo:hi] = v.reshape(P, -1)

    def chunks(v):
        return v.reshape(-1, P).T

    for l in range(DEPTH):
        put(a, PAR1, l, "norm_attn", chunks(g["norm_attn"][l]))
        put(a, PAR1, l, "norm_mlp", chunks(g["norm_mlp"][l]))
        put(a, PAR1, l, "final_norm", chunks(g["final_norm"]))
        put(a, PAR1, l, "pos", np.concatenate([g["cmp_pos_k"][l].T, g["cmp_pos_v"][l].T], 0))
        put(a, PAR1, l, "subln", np.tile(g["diff_subln"][l], 2))
        init = 0.8 - 0.6 * math.exp(-0.3 * l)
        put(a, PAR1, l, "lam_init", np.tile(np.array([init, 1.0 - init], np.float32), (P, 1)))
        put(a, PAR1, l, "lam", np.tile(g["diff_lambda"][l].reshape(1, -1), (P, 1)))
        for n in "kv":
            put(a, PAR1, l, f"w2{n}", g[f"cmp_{n}_w2"][l].reshape(2, P, HEAD).transpose(1, 0, 2))
        put(b, PAR2, l, "ln_g", chunks(g["ln_g_2"][l]))
        put(b, PAR2, l, "ln_b", chunks(g["ln_b_2"][l]))
        put(b, PAR2, l, "pool_scale", chunks(g["pool_scale_2"][l]))
        put(b, PAR2, l, "conv", g["conv_w_2"][l].reshape(3, 2, P).transpose(2, 1, 0))
        put(b, PAR2, l, "pool_w", g["pool_w_2"][l].reshape(2, P, HEAD).transpose(1, 0, 2))
    return a, b


def kernel(**inputs):
    import concourse.bacc as bacc
    from concourse.bass_utils import run_bass_kernel_spmd

    g = {k: np.asarray(v) for k, v in inputs.items()}
    par1, par2 = _parameters(g)
    const, bucket = _constants()
    rpb = np.stack([g["rpb_2"][:, :, GRID_H - 1 - r:RPB_H - r] for r in range(GRID_H)], 1)
    rpb = np.pad(rpb.reshape(DEPTH, GRID_H, 1, -1), ((0, 0), (0, 0), (0, 0), (RPB_PAD, RPB_PAD)))
    rpb = np.ascontiguousarray(np.broadcast_to(rpb, (DEPTH, GRID_H, NA_COLS, RPB_SIZE)))
    arrays = {
        "in_x": np.ascontiguousarray(g["x"].reshape(SEQ, D_MODEL)),
        "in_weights": _pieces(g),
        "in_const": const,
        "in_bucket": bucket,
        "in_par1": par1,
        "in_par2": par2,
        "in_table": np.ascontiguousarray(g["rel_bias"]),
        "in_rpb": rpb,
    }
    nc = bacc.Bacc("TRN2", target_bir_lowering=False, num_devices=1)
    args = [nc.dram_tensor(n, a.shape, mybir.dt.from_np(a.dtype), kind="ExternalInput").ap() for n, a in arrays.items()]
    out = nc.dram_tensor("out_x", (SEQ, D_MODEL), F32, kind="ExternalOutput").ap()
    emit(nc, *args, out)
    r = run_bass_kernel_spmd(nc, [arrays], core_ids=[0])
    return r.results[0]["out_x"].reshape(1, SEQ, D_MODEL)
```
